# Optimizing a Trainium2 kernel written in Bass

```python
import math
import jax, jax.numpy as jnp
from jax import lax
import numpy as np

D_MODEL = 1024
BATCH = 1
SEQ = 512
DEPTH = 1

CHUNK = 64
Q_BLOCK = 128
HEAD_DIM = 64
N_DIFF_HEADS = 4
N_SB_HEADS = 8
DIFF_WIDTH = N_DIFF_HEADS * 2 * HEAD_DIM
SB_WIDTH = N_SB_HEADS * HEAD_DIM
MIX_WIDTH = DIFF_WIDTH + SB_WIDTH
IN_WIDTH = 3 * MIX_WIDTH
D_FF = 4 * D_MODEL
ROPE_THETA = 10000.0
NORM_EPS = 1e-6
N_MOD = 6


def rms_norm(x, g):
    xf = x.astype(jnp.float32)
    y = xf * lax.rsqrt(jnp.mean(xf * xf, axis=-1, keepdims=True) + NORM_EPS)
    return (y * g.astype(jnp.float32)).astype(x.dtype)

def rope_tables(seq_len, dim):
    inv = 1.0 / (ROPE_THETA ** (jnp.arange(0, dim, 2, dtype=jnp.float32) / dim))
    ang = jnp.arange(seq_len, dtype=jnp.float32)[:, None] * inv[None, :]
    ang = jnp.concatenate([ang, ang], axis=-1)
    return jnp.cos(ang), jnp.sin(ang)

def apply_rope(x, cos, sin):
    x1, x2 = jnp.split(x, 2, axis=-1)
    rot = jnp.concatenate([-x2, x1], axis=-1)
    return (x * cos + rot * sin).astype(x.dtype)

def diff_attention(q, k, v, lam, subln_g, lambda_init):
    seq_len = q.shape[3]
    scale = HEAD_DIM ** -0.5
    outs = []
    for blk in range(seq_len // Q_BLOCK):
        q0 = blk * Q_BLOCK
        kv_len = q0 + Q_BLOCK
        qb = q[:, :, :, q0:kv_len]
        kb = k[:, :, :, :kv_len]
        vb = v[:, :, :kv_len]
        s = jnp.einsum("bhmqd,bhmkd->bhmqk", qb, kb).astype(jnp.float32) * scale
        q_chunk = (q0 + jnp.arange(Q_BLOCK)) // CHUNK
        k_chunk = jnp.arange(kv_len) // CHUNK
        mask = k_chunk[None, :] <= q_chunk[:, None]
        p = jax.nn.softmax(jnp.where(mask, s, -jnp.inf), axis=-1)
        w = p[:, :, 0] - lam * p[:, :, 1]
        outs.append(jnp.einsum("bhqk,bhkd->bhqd", w.astype(vb.dtype), vb))
    o = jnp.concatenate(outs, axis=2)
    return rms_norm(o, subln_g) * (1.0 - lambda_init)

def stick_breaking_attention(q, k, v):
    seq_len = q.shape[2]
    scale = HEAD_DIM ** -0.5
    outs = []
    for blk in range(seq_len // Q_BLOCK):
        q0 = blk * Q_BLOCK
        kv_len = q0 + Q_BLOCK
        qb = q[:, :, q0:kv_len]
        kb = k[:, :, :kv_len]
        vb = v[:, :, :kv_len]
        z = jnp.einsum("bhqd,bhkd->bhqk", qb, kb).astype(jnp.float32) * scale
        t_idx = q0 + jnp.arange(Q_BLOCK)
        s_idx = jnp.arange(kv_len)
        causal = s_idx[None, :] < t_idx[:, None]
        log_beta = jax.nn.log_sigmoid(z)
        log_1m = jnp.where(causal, jax.nn.log_sigmoid(-z), 0.0)
        suffix = lax.cumsum(log_1m, axis=3, reverse=True) - log_1m
        a = jnp.where(causal, jnp.exp(log_beta + suffix), 0.0)
        outs.append(jnp.einsum("bhqk,bhkd->bhqd", a.astype(vb.dtype), vb))
    return jnp.concatenate(outs, axis=2)

def first_inputs(seed: int = 0) -> dict:
    key = jax.random.key(seed)
    ks = jax.random.split(key, 16)
    f32 = jnp.float32
    x = jax.random.normal(ks[0], (BATCH, SEQ, D_MODEL), f32)
    c = jax.random.normal(ks[1], (BATCH, D_MODEL), f32)
    ada_w = jax.random.normal(ks[2], (DEPTH, D_MODEL, N_MOD * D_MODEL), f32) * (0.5 * D_MODEL ** -0.5)
    ada_b = jax.random.normal(ks[3], (DEPTH, N_MOD * D_MODEL), f32) * 0.01
    mix_norm_g = 1.0 + 0.02 * jax.random.normal(ks[4], (DEPTH, D_MODEL), f32)
    w_in = jax.random.normal(ks[5], (DEPTH, D_MODEL, IN_WIDTH), f32) * D_MODEL ** -0.5
    lambda_q1 = 0.1 * jax.random.normal(ks[6], (DEPTH, HEAD_DIM), f32)
    lambda_k1 = 0.1 * jax.random.normal(ks[7], (DEPTH, HEAD_DIM), f32)
    lambda_q2 = 0.1 * jax.random.normal(ks[8], (DEPTH, HEAD_DIM), f32)
    lambda_k2 = 0.1 * jax.random.normal(ks[9], (DEPTH, HEAD_DIM), f32)
    diff_subln_g = 1.0 + 0.02 * jax.random.normal(ks[10], (DEPTH, 2 * HEAD_DIM), f32)
    w_out = jax.random.normal(ks[11], (DEPTH, MIX_WIDTH, D_MODEL), f32) * MIX_WIDTH ** -0.5
    ffn_norm_g = 1.0 + 0.02 * jax.random.normal(ks[12], (DEPTH, D_MODEL), f32)
    w_ff1 = jax.random.normal(ks[13], (DEPTH, D_MODEL, D_FF), f32) * D_MODEL ** -0.5
    w_ff2 = jax.random.normal(ks[14], (DEPTH, D_FF, D_MODEL), f32) * D_FF ** -0.5
    final_norm_g = 1.0 + 0.02 * jax.random.normal(ks[15], (D_MODEL,), f32)
    return {"x": x, "c": c, "ada_w": ada_w, "ada_b": ada_b, "mix_norm_g": mix_norm_g,
            "w_in": w_in, "lambda_q1": lambda_q1, "lambda_k1": lambda_k1,
            "lambda_q2": lambda_q2, "lambda_k2": lambda_k2, "diff_subln_g": diff_subln_g,
            "w_out": w_out, "ffn_norm_g": ffn_norm_g, "w_ff1": w_ff1, "w_ff2": w_ff2,
            "final_norm_g": final_norm_g}

def first_block(x, c, ada_w, ada_b, mix_norm_g, w_in, lambda_q1, lambda_k1, lambda_q2,
              lambda_k2, diff_subln_g, w_out, ffn_norm_g, w_ff1, w_ff2, final_norm_g):
    bsz, seq_len, _ = x.shape
    cos, sin = rope_tables(seq_len, HEAD_DIM)
    cos = cos.astype(x.dtype)
    sin = sin.astype(x.dtype)
    c_act = jax.nn.silu(c)
    for layer in range(DEPTH):
        lambda_init = 0.8 - 0.6 * math.exp(-0.3 * layer)
        mod = c_act @ ada_w[layer] + ada_b[layer]
        sh_m, sc_m, g_m, sh_f, sc_f, g_f = [m[:, None, :] for m in jnp.split(mod, N_MOD, axis=-1)]

        h = rms_norm(x, mix_norm_g[layer]) * (1.0 + sc_m) + sh_m
        proj = h @ w_in[layer]
        dq, dk, dv, sq, sk, sv = jnp.split(proj, 6, axis=-1)
        dq = dq.reshape(bsz, seq_len, N_DIFF_HEADS, 2, HEAD_DIM).transpose(0, 2, 3, 1, 4)
        dk = dk.reshape(bsz, seq_len, N_DIFF_HEADS, 2, HEAD_DIM).transpose(0, 2, 3, 1, 4)
        dv = dv.reshape(bsz, seq_len, N_DIFF_HEADS, 2 * HEAD_DIM).transpose(0, 2, 1, 3)
        dq = apply_rope(dq, cos, sin)
        dk = apply_rope(dk, cos, sin)
        lam = (jnp.exp(jnp.sum(lambda_q1[layer].astype(jnp.float32) * lambda_k1[layer].astype(jnp.float32)))
               - jnp.exp(jnp.sum(lambda_q2[layer].astype(jnp.float32) * lambda_k2[layer].astype(jnp.float32)))
               + lambda_init)
        o_diff = diff_attention(dq, dk, dv, lam, diff_subln_g[layer], lambda_init)
        o_diff = o_diff.transpose(0, 2, 1, 3).reshape(bsz, seq_len, DIFF_WIDTH)

        sq = sq.reshape(bsz, seq_len, N_SB_HEADS, HEAD_DIM).transpose(0, 2, 1, 3)
        sk = sk.reshape(bsz, seq_len, N_SB_HEADS, HEAD_DIM).transpose(0, 2, 1, 3)
        sv = sv.reshape(bsz, seq_len, N_SB_HEADS, HEAD_DIM).transpose(0, 2, 1, 3)
        o_sb = stick_breaking_attention(sq, sk, sv)
        o_sb = o_sb.transpose(0, 2, 1, 3).reshape(bsz, seq_len, SB_WIDTH)

        mixed = jnp.concatenate([o_diff, o_sb], axis=-1) @ w_out[layer]
        x = x + g_m * mixed

        h = rms_norm(x, ffn_norm_g[layer]) * (1.0 + sc_f) + sh_f
        f = jnp.square(jax.nn.relu(h @ w_ff1[layer])) @ w_ff2[layer]
        x = x + g_f * f
    return rms_norm(x, final_norm_g)


DEPTH_2 = 2

N_MIXERS = 2
EXPAND = 2
D_INNER = EXPAND * D_MODEL
CONV_WIDTH = 31
CONV_IN_PROJ = 3 * D_INNER
RET_HEADS = 4
RET_QK_DIM = D_MODEL // RET_HEADS
RET_V_DIM = D_INNER // RET_HEADS
RET_IN_PROJ = 2 * RET_HEADS * RET_QK_DIM + 2 * D_INNER
CHUNK_2 = 128
ROPE_BASE = 10000.0
EPS = 1e-6
N_CONV_LAYERS = (DEPTH_2 + 1) // 2
N_RET_LAYERS = DEPTH_2 // 2


def rms_norm_2(x, g):
    xf = x.astype(jnp.float32)
    y = xf * lax.rsqrt(jnp.mean(xf * xf, axis=-1, keepdims=True) + EPS)
    return (y * g.astype(jnp.float32)).astype(x.dtype)

def conv_module(h, w_in, dw_w, dw_b, ln_g, ln_b, w_out):
    proj = h @ w_in
    a, b, z = jnp.split(proj, 3, axis=-1)
    u = a * jax.nn.sigmoid(b)
    c = lax.conv_general_dilated(
        u, dw_w[:, None, :].astype(u.dtype), window_strides=(1,),
        padding=((CONV_WIDTH - 1, 0),),
        dimension_numbers=("NWC", "WIO", "NWC"),
        feature_group_count=D_INNER) + dw_b
    cf = c.astype(jnp.float32)
    mu = jnp.mean(cf, axis=-1, keepdims=True)
    var = jnp.mean(jnp.square(cf - mu), axis=-1, keepdims=True)
    cn = ((cf - mu) * lax.rsqrt(var + EPS) * ln_g.astype(jnp.float32) + ln_b.astype(jnp.float32))
    y = jax.nn.silu(cn).astype(h.dtype) * jax.nn.silu(z)
    return y @ w_out

def apply_rotary(t, cos, sin):
    t1, t2 = jnp.split(t.astype(jnp.float32), 2, axis=-1)
    return jnp.concatenate([t1 * cos - t2 * sin, t1 * sin + t2 * cos], axis=-1).astype(t.dtype)

def retention_module(h, positions, w_in, w_out):
    bsz, seq, _ = h.shape
    nc = seq // CHUNK_2
    qk_w = RET_HEADS * RET_QK_DIM
    proj = h @ w_in
    q, k, v, g = jnp.split(proj, [qk_w, 2 * qk_w, 2 * qk_w + D_INNER], axis=-1)
    q = q.reshape(bsz, seq, RET_HEADS, RET_QK_DIM)
    k = k.reshape(bsz, seq, RET_HEADS, RET_QK_DIM)
    v = v.reshape(bsz, seq, RET_HEADS, RET_V_DIM)

    inv_freq = ROPE_BASE ** (-jnp.arange(RET_QK_DIM // 2, dtype=jnp.float32) / (RET_QK_DIM // 2))
    ang = positions.astype(jnp.float32)[..., None] * inv_freq
    cos, sin = jnp.cos(ang)[:, :, None, :], jnp.sin(ang)[:, :, None, :]
    q = apply_rotary(q, cos, sin)
    k = apply_rotary(k, cos, sin) * (RET_QK_DIM ** -0.5)

    qc = q.reshape(bsz, nc, CHUNK_2, RET_HEADS, RET_QK_DIM)
    kc = k.reshape(bsz, nc, CHUNK_2, RET_HEADS, RET_QK_DIM)
    vc = v.reshape(bsz, nc, CHUNK_2, RET_HEADS, RET_V_DIM)

    log_gamma = jnp.log(1.0 - 2.0 ** (-5.0 - jnp.arange(RET_HEADS, dtype=jnp.float32)))
    idx = jnp.arange(CHUNK_2, dtype=jnp.float32)
    diff = idx[:, None] - idx[None, :]
    causal = diff >= 0
    inner_decay = jnp.where(causal[None], jnp.exp(jnp.where(causal, diff, 0.0)[None] * log_gamma[:, None, None]), 0.0)
    q_decay = jnp.exp((idx + 1.0)[:, None] * log_gamma)[..., None]
    k_decay = jnp.exp((CHUNK_2 - 1.0 - idx)[:, None] * log_gamma)[..., None]
    chunk_decay = jnp.exp(CHUNK_2 * log_gamma)[:, None, None]

    scores = jnp.einsum("bnihd,bnjhd->bnhij", qc, kc) * inner_decay
    inner = jnp.einsum("bnhij,bnjhe->bnihe", scores, vc)

    def step(state, xs):
        qn, kn, vn = xs
        cross = jnp.einsum("bihd,bhde->bihe", qn * q_decay, state)
        state = state * chunk_decay + jnp.einsum("bjhd,bjhe->bhde", kn * k_decay, vn)
        return state, cross

    state0 = jnp.zeros((bsz, RET_HEADS, RET_QK_DIM, RET_V_DIM), jnp.float32)
    _, cross = lax.scan(step, state0, (jnp.moveaxis(qc, 1, 0), jnp.moveaxis(kc, 1, 0), jnp.moveaxis(vc, 1, 0)))
    o = (inner + jnp.moveaxis(cross, 0, 1)).astype(jnp.float32).reshape(bsz, seq, RET_HEADS, RET_V_DIM)

    o = o * lax.rsqrt(jnp.mean(o * o, axis=-1, keepdims=True) + EPS)
    o = o.reshape(bsz, seq, D_INNER).astype(h.dtype)
    return (jax.nn.silu(g) * o) @ w_out

def second_inputs(seed: int = 0) -> dict:
    key = jax.random.key(seed)
    ks = jax.random.split(key, 14)
    f32 = jnp.float32
    x = jax.random.normal(ks[0], (BATCH, SEQ, D_MODEL), f32)
    positions = jnp.broadcast_to(jnp.arange(SEQ, dtype=jnp.int32), (BATCH, SEQ))
    conv_norm = 1.0 + 0.01 * jax.random.normal(ks[1], (N_CONV_LAYERS, D_MODEL), f32)
    conv_w_in = jax.random.normal(ks[2], (N_CONV_LAYERS, D_MODEL, CONV_IN_PROJ), f32) * D_MODEL ** -0.5
    conv_dw_w = jax.random.normal(ks[3], (N_CONV_LAYERS, CONV_WIDTH, D_INNER), f32) * CONV_WIDTH ** -0.5
    conv_dw_b = 0.01 * jax.random.normal(ks[4], (N_CONV_LAYERS, D_INNER), f32)
    conv_ln_g = 1.0 + 0.01 * jax.random.normal(ks[5], (N_CONV_LAYERS, D_INNER), f32)
    conv_ln_b = 0.01 * jax.random.normal(ks[6], (N_CONV_LAYERS, D_INNER), f32)
    conv_w_out = jax.random.normal(ks[7], (N_CONV_LAYERS, D_INNER, D_MODEL), f32) * (0.5 * D_INNER ** -0.5)
    ret_norm = 1.0 + 0.01 * jax.random.normal(ks[8], (N_RET_LAYERS, D_MODEL), f32)
    ret_w_in = jax.random.normal(ks[9], (N_RET_LAYERS, D_MODEL, RET_IN_PROJ), f32) * D_MODEL ** -0.5
    ret_w_out = jax.random.normal(ks[10], (N_RET_LAYERS, D_INNER, D_MODEL), f32) * (0.5 * D_INNER ** -0.5)
    final_norm = 1.0 + 0.01 * jax.random.normal(ks[11], (D_MODEL,), f32)
    return {"x": x, "positions": positions,
            "conv_norm": conv_norm, "conv_w_in": conv_w_in, "conv_dw_w": conv_dw_w, "conv_dw_b": conv_dw_b,
            "conv_ln_g": conv_ln_g, "conv_ln_b": conv_ln_b, "conv_w_out": conv_w_out,
            "ret_norm": ret_norm, "ret_w_in": ret_w_in, "ret_w_out": ret_w_out,
            "final_norm": final_norm}

def second_block(x, positions, conv_norm, conv_w_in, conv_dw_w, conv_dw_b, conv_ln_g, conv_ln_b, conv_w_out,
              ret_norm, ret_w_in, ret_w_out, final_norm):
    for i in range(DEPTH_2):
        j = i // N_MIXERS
        if i % N_MIXERS == 0:
            h = rms_norm_2(x, conv_norm[j])
            y = conv_module(h, conv_w_in[j], conv_dw_w[j], conv_dw_b[j], conv_ln_g[j], conv_ln_b[j], conv_w_out[j])
        else:
            h = rms_norm_2(x, ret_norm[j])
            y = retention_module(h, positions, ret_w_in[j], ret_w_out[j])
        x = x + y.astype(x.dtype)
    return rms_norm_2(x, final_norm)


_first_inputs = second_inputs


def second_inputs(seed=0):
    import zlib

    import numpy as np

    out = dict(_first_inputs(seed))
    spreads = {}
    factors = {'conv_norm': 22.618,
     'conv_dw_b': 79.809,
     'conv_ln_g': 200.0,
     'conv_ln_b': 200.0,
     'ret_norm': 200.0,
     'final_norm': 181.536}
    for name, (base, spread) in spreads.items():
        noise = np.random.default_rng([zlib.crc32(name.encode()), seed]).standard_normal(out[name].shape)
        drawn = base * np.exp(spread * noise) if base else spread * noise
        out[name] = __import__('jax').numpy.asarray(drawn.astype(out[name].dtype))
    for name, factor in factors.items():
        out[name] = (out[name] * factor).astype(out[name].dtype)
    return out


_narrow_inputs = second_inputs


def second_inputs(seed=0):

    out = dict(_narrow_inputs(seed))
    wider = {'conv_ln_g': 6.16, 'conv_ln_b': 6.22, 'ret_norm': 12.0, 'final_norm': 6.38}
    for name, times in wider.items():
        mean = out[name].mean()
        out[name] = (mean + times * (out[name] - mean)).astype(out[name].dtype)
    return out


M_HEADS = 8
M_DQK = 64
M_DV = 128
M_QK = M_HEADS * M_DQK
M_V = M_HEADS * M_DV
M_CONV = 4
S_HEADDIM = 64
S_INNER = D_MODEL
S_HEADS = S_INNER // S_HEADDIM
S_GROUPS = 4
S_STATE = 128
S_CONV = 4
S_XBC = S_INNER + 2 * S_GROUPS * S_STATE
D_FF_3 = 2752
FFN_CONV = 3
IN_SIZES = (M_QK, M_QK, M_V, M_V, M_HEADS, M_HEADS, S_INNER, S_XBC, S_HEADS, D_MODEL, D_MODEL)
D_IN = sum(IN_SIZES)
ALPHA = (2 * DEPTH) ** 0.25
BETA = (8 * DEPTH) ** -0.25
LN_EPS = 1e-5
RMS_EPS = 1e-6
NEG_BIG = -1e30


def layer_norm(x, g, b):
    xf = x.astype(jnp.float32)
    mu = jnp.mean(xf, -1, keepdims=True)
    var = jnp.mean(jnp.square(xf - mu), -1, keepdims=True)
    return ((xf - mu) * lax.rsqrt(var + LN_EPS) * g.astype(jnp.float32) + b.astype(jnp.float32)).astype(x.dtype)

def group_rms_norm(x, g, n_groups):
    shp = x.shape
    xf = x.astype(jnp.float32).reshape(shp[:-1] + (n_groups, shp[-1] // n_groups))
    xf = xf * lax.rsqrt(jnp.mean(xf * xf, -1, keepdims=True) + RMS_EPS)
    return (xf.reshape(shp) * g.astype(jnp.float32)).astype(x.dtype)

def causal_dwconv(x, w, b):
    K, C = w.shape
    y = lax.conv_general_dilated(x, w[:, None, :], window_strides=(1,), padding=[(K - 1, 0)],
                                 dimension_numbers=('NWC', 'WIO', 'NWC'), feature_group_count=C)
    return y + b

def mlstm_chunkwise(q, k, v, i_pre, f_pre):
    f32 = jnp.float32
    Bsz, T = q.shape[0], q.shape[1]
    nc = T // CHUNK

    def chunks(a):
        a = a.reshape((Bsz, nc, CHUNK) + a.shape[2:])
        return jnp.moveaxis(a, 3, 1)

    qc = chunks(q.astype(f32))
    kc = chunks(k.astype(f32)) * (M_DQK ** -0.5)
    vc = chunks(v.astype(f32))
    log_i = chunks(i_pre.astype(f32))
    log_f = jax.nn.log_sigmoid(chunks(f_pre.astype(f32)))
    b = jnp.cumsum(log_f, -1)
    g = b[..., -1]

    a = g[..., None] - b + log_i
    m_loc = jnp.max(a, -1)
    w_s = jnp.exp(a - m_loc[..., None])
    kw = kc * w_s[..., None]
    c_loc = jnp.einsum('bhcsk,bhcsv->bhckv', kw, vc)
    n_loc = jnp.sum(kw, 3)

    def step(carry, inp):
        C, n, m = carry
        g_c, m_l, C_l, n_l = inp
        m_new = jnp.maximum(g_c + m, m_l)
        s_prev = jnp.exp(g_c + m - m_new)
        s_loc = jnp.exp(m_l - m_new)
        C_new = s_prev[..., None, None] * C + s_loc[..., None, None] * C_l
        n_new = s_prev[..., None] * n + s_loc[..., None] * n_l
        return (C_new, n_new, m_new), (C, n, m)

    init = (jnp.zeros((Bsz, M_HEADS, M_DQK, M_DV), f32),
            jnp.zeros((Bsz, M_HEADS, M_DQK), f32),
            jnp.full((Bsz, M_HEADS), NEG_BIG, f32))
    xs = (jnp.moveaxis(g, 2, 0), jnp.moveaxis(m_loc, 2, 0),
          jnp.moveaxis(c_loc, 2, 0), jnp.moveaxis(n_loc, 2, 0))
    _, (C_prev, n_prev, m_prev) = lax.scan(step, init, xs)
    C_prev = jnp.moveaxis(C_prev, 0, 2)
    n_prev = jnp.moveaxis(n_prev, 0, 2)
    m_prev = jnp.moveaxis(m_prev, 0, 2)

    causal = jnp.tril(jnp.ones((CHUNK, CHUNK), bool))
    log_d = jnp.where(causal, b[..., :, None] - b[..., None, :] + log_i[..., None, :], -jnp.inf)
    m_inter = b + m_prev[..., None]
    m_comb = jnp.maximum(m_inter, jnp.max(log_d, -1))
    s_inter = jnp.exp(m_inter - m_comb)
    scores = jnp.einsum('bhctk,bhcsk->bhcts', qc, kc) * jnp.exp(log_d - m_comb[..., None])
    num = (jnp.einsum('bhcts,bhcsv->bhctv', scores, vc)
           + s_inter[..., None] * jnp.einsum('bhctk,bhckv->bhctv', qc, C_prev))
    den = jnp.sum(scores, -1) + s_inter * jnp.einsum('bhctk,bhck->bhct', qc, n_prev)
    h = num / jnp.maximum(jnp.abs(den), jnp.exp(-m_comb))[..., None]
    h = jnp.moveaxis(h, 1, 3).reshape(Bsz, T, M_HEADS, M_DV)
    return h.astype(q.dtype)

def segsum_exp(a):
    cs = jnp.cumsum(a, -1)
    L = a.shape[-1]
    causal = jnp.tril(jnp.ones((L, L), bool))
    return jnp.exp(jnp.where(causal, cs[..., :, None] - cs[..., None, :], -jnp.inf))

def ssd_chunked(x, dt, A, Bm, Cm):
    f32 = jnp.float32
    Bsz, T = x.shape[0], x.shape[1]
    nc = T // CHUNK
    R = S_HEADS // S_GROUPS
    dt = dt.astype(f32)
    xc = (x.astype(f32) * dt[..., None]).reshape(Bsz, nc, CHUNK, S_GROUPS, R, S_HEADDIM)
    a = (dt * A.astype(f32)).reshape(Bsz, nc, CHUNK, S_GROUPS, R)
    a = jnp.transpose(a, (0, 3, 4, 1, 2))
    Bc = Bm.astype(f32).reshape(Bsz, nc, CHUNK, S_GROUPS, S_STATE)
    Cc = Cm.astype(f32).reshape(Bsz, nc, CHUNK, S_GROUPS, S_STATE)
    a_cs = jnp.cumsum(a, -1)

    cb = jnp.einsum('bclgn,bcsgn->bgcls', Cc, Bc)
    mix = cb[:, :, None] * segsum_exp(a)
    y_diag = jnp.einsum('bgrcls,bcsgrp->bclgrp', mix, xc)

    decay_to_end = jnp.transpose(jnp.exp(a_cs[..., -1:] - a_cs), (0, 3, 4, 1, 2))
    states = jnp.einsum('bcsgn,bcsgrp->bcgrpn', Bc, xc * decay_to_end[..., None])

    chunk_decay = jnp.exp(a_cs[..., -1])

    def step(h, inp):
        dec, st = inp
        return dec[..., None, None] * h + st, h

    h0 = jnp.zeros((Bsz, S_GROUPS, R, S_HEADDIM, S_STATE), f32)
    _, h_prev = lax.scan(step, h0, (jnp.moveaxis(chunk_decay, 3, 0), jnp.moveaxis(states, 1, 0)))
    h_prev = jnp.moveaxis(h_prev, 0, 1)

    decay_in = jnp.transpose(jnp.exp(a_cs), (0, 3, 4, 1, 2))
    y_off = jnp.einsum('bclgn,bcgrpn->bclgrp', Cc, h_prev) * decay_in[..., None]
    return (y_diag + y_off).reshape(Bsz, T, S_HEADS, S_HEADDIM)

def mlstm_branch(q, k, v, o_pre, i_pre, f_pre, conv_w, conv_b, i_bias, f_bias, norm_g):
    Bsz, T = q.shape[0], q.shape[1]
    qk = jax.nn.silu(causal_dwconv(jnp.concatenate([q, k], -1), conv_w, conv_b))
    q, k = jnp.split(qk, 2, -1)
    h = mlstm_chunkwise(q.reshape(Bsz, T, M_HEADS, M_DQK), k.reshape(Bsz, T, M_HEADS, M_DQK),
                        v.reshape(Bsz, T, M_HEADS, M_DV), i_pre + i_bias, f_pre + f_bias)
    h = group_rms_norm(h.reshape(Bsz, T, M_V), norm_g, M_HEADS)
    return jax.nn.sigmoid(o_pre) * h

def mamba2_branch(z, xbc, dt_raw, conv_w, conv_b, dt_bias, a_log, d_skip, norm_g):
    Bsz, T = z.shape[0], z.shape[1]
    xbc = jax.nn.silu(causal_dwconv(xbc, conv_w, conv_b))
    xs, Bm, Cm = jnp.split(xbc, [S_INNER, S_INNER + S_GROUPS * S_STATE], -1)
    xs = xs.reshape(Bsz, T, S_HEADS, S_HEADDIM)
    Bm = Bm.reshape(Bsz, T, S_GROUPS, S_STATE)
    Cm = Cm.reshape(Bsz, T, S_GROUPS, S_STATE)
    dt = jax.nn.softplus(dt_raw.astype(jnp.float32) + dt_bias.astype(jnp.float32))
    A = -jnp.exp(a_log.astype(jnp.float32))
    y = ssd_chunked(xs, dt, A, Bm, Cm) + d_skip.astype(jnp.float32)[:, None] * xs.astype(jnp.float32)
    y = y.reshape(Bsz, T, S_INNER).astype(z.dtype)
    return group_rms_norm(y * jax.nn.silu(z), norm_g, S_GROUPS)

def third_inputs(seed: int = 0) -> dict:
    key = jax.random.key(seed)
    ks = jax.random.split(key, 32)
    L = DEPTH
    f32 = jnp.float32

    def nrm(k, shape, scale):
        return scale * jax.random.normal(k, shape, f32)

    dt0 = jnp.exp(jax.random.uniform(ks[12], (L, S_HEADS), f32, math.log(1e-3), math.log(1e-1)))
    return {
        "x": nrm(ks[0], (BATCH, SEQ, D_MODEL), 1.0),
        "in_ln_g": 1.0 + nrm(ks[1], (D_MODEL,), 0.02),
        "in_ln_b": nrm(ks[2], (D_MODEL,), 0.02),
        "w_in": nrm(ks[3], (L, D_MODEL, D_IN), D_MODEL ** -0.5),
        "m_conv_w": nrm(ks[4], (L, M_CONV, 2 * M_QK), M_CONV ** -0.5),
        "m_conv_b": nrm(ks[5], (L, 2 * M_QK), 0.01),
        "m_i_bias": nrm(ks[6], (L, M_HEADS), 0.1),
        "m_f_bias": jnp.linspace(3.0, 6.0, M_HEADS, dtype=f32)[None] + nrm(ks[7], (L, M_HEADS), 0.1),
        "m_norm_g": 1.0 + nrm(ks[8], (L, M_V), 0.02),
        "s_conv_w": nrm(ks[9], (L, S_CONV, S_XBC), S_CONV ** -0.5),
        "s_conv_b": nrm(ks[10], (L, S_XBC), 0.01),
        "s_dt_bias": dt0 + jnp.log(-jnp.expm1(-dt0)),
        "s_a_log": jnp.log(jax.random.uniform(ks[13], (L, S_HEADS), f32, 1.0, 16.0)),
        "s_d": 1.0 + nrm(ks[14], (L, S_HEADS), 0.1),
        "s_norm_g": 1.0 + nrm(ks[15], (L, S_INNER), 0.02),
        "p_a": nrm(ks[16], (L, M_V, D_MODEL), M_V ** -0.5),
        "p_b": nrm(ks[17], (L, S_INNER, D_MODEL), S_INNER ** -0.5),
        "w_out": nrm(ks[18], (L, D_MODEL, D_MODEL), BETA * D_MODEL ** -0.5),
        "ln1_g": 1.0 + nrm(ks[19], (L, D_MODEL), 0.02),
        "ln1_b": nrm(ks[20], (L, D_MODEL), 0.02),
        "w_up": nrm(ks[21], (L, D_MODEL, 2 * D_FF_3), D_MODEL ** -0.5),
        "f_conv_w": nrm(ks[22], (L, FFN_CONV, 2 * D_FF_3), FFN_CONV ** -0.5),
        "f_conv_b": nrm(ks[23], (L, 2 * D_FF_3), 0.01),
        "w_down": nrm(ks[24], (L, D_FF_3, D_MODEL), BETA * D_FF_3 ** -0.5),
        "ln2_g": 1.0 + nrm(ks[25], (L, D_MODEL), 0.02),
        "ln2_b": nrm(ks[26], (L, D_MODEL), 0.02),
    }

def third_block(x, in_ln_g, in_ln_b, w_in, m_conv_w, m_conv_b, m_i_bias, m_f_bias, m_norm_g,
              s_conv_w, s_conv_b, s_dt_bias, s_a_log, s_d, s_norm_g, p_a, p_b, w_out,
              ln1_g, ln1_b, w_up, f_conv_w, f_conv_b, w_down, ln2_g, ln2_b):
    splits = np.cumsum(IN_SIZES)[:-1].tolist()
    x = layer_norm(x, in_ln_g, in_ln_b)
    for l in range(DEPTH):
        proj = x @ w_in[l]
        q, k, v, o_pre, i_pre, f_pre, z, xbc, dt_raw, g_a, g_b = jnp.split(proj, splits, -1)
        h_a = mlstm_branch(q, k, v, o_pre, i_pre, f_pre, m_conv_w[l], m_conv_b[l],
                           m_i_bias[l], m_f_bias[l], m_norm_g[l])
        h_b = mamba2_branch(z, xbc, dt_raw, s_conv_w[l], s_conv_b[l], s_dt_bias[l],
                            s_a_log[l], s_d[l], s_norm_g[l])
        merged = jax.nn.sigmoid(g_a) * (h_a @ p_a[l]) + jax.nn.sigmoid(g_b) * (h_b @ p_b[l])
        x = layer_norm(ALPHA * x + merged @ w_out[l], ln1_g[l], ln1_b[l])
        u = causal_dwconv(x @ w_up[l], f_conv_w[l], f_conv_b[l])
        u_gate, u_val = jnp.split(u, 2, -1)
        x = layer_norm(ALPHA * x + (jax.nn.silu(u_gate) * u_val) @ w_down[l], ln2_g[l], ln2_b[l])
    return x


_first_inputs_3 = third_inputs


def third_inputs(seed=0):
    import zlib

    import numpy as np

    out = dict(_first_inputs_3(seed))
    spreads = {}
    factors = {'m_conv_b': 8.0,
     'm_i_bias': 64.0,
     'm_norm_g': 44.35,
     's_conv_b': 8.0,
     's_norm_g': 23.402,
     'ln1_g': 2.714,
     'ln1_b': 2.806,
     'f_conv_b': 8.0,
     'ln2_g': 7.836,
     'ln2_b': 7.847}
    for name, (base, spread) in spreads.items():
        noise = np.random.default_rng([zlib.crc32(name.encode()), seed]).standard_normal(out[name].shape)
        drawn = base * np.exp(spread * noise) if base else spread * noise
        out[name] = __import__('jax').numpy.asarray(drawn.astype(out[name].dtype))
    for name, factor in factors.items():
        out[name] = (out[name] * factor).astype(out[name].dtype)
    return out


_narrow_inputs_3 = third_inputs


def third_inputs(seed=0):

    out = dict(_narrow_inputs_3(seed))
    wider = {'m_norm_g': 3.86, 's_norm_g': 3.83, 'ln2_g': 3.15, 'ln2_b': 3.15}
    for name, times in wider.items():
        mean = out[name].mean()
        out[name] = (mean + times * (out[name] - mean)).astype(out[name].dtype)
    return out


def setup_inputs(seed=0):
    out = dict(first_inputs(seed))
    for name, value in second_inputs(seed + 1).items():
        if name != "x":
            out[name + "_2"] = value
    for name, value in third_inputs(seed + 2).items():
        if name != "x":
            out[name + "_3"] = value
    return out


def reference(
    x, c, ada_w, ada_b, mix_norm_g, w_in, lambda_q1, lambda_k1, lambda_q2, lambda_k2,
    diff_subln_g, w_out, ffn_norm_g, w_ff1, w_ff2, final_norm_g, positions_2, conv_norm_2,
    conv_w_in_2, conv_dw_w_2, conv_dw_b_2, conv_ln_g_2, conv_ln_b_2, conv_w_out_2, ret_norm_2,
    ret_w_in_2, ret_w_out_2, final_norm_2, in_ln_g_3, in_ln_b_3, w_in_3, m_conv_w_3, m_conv_b_3,
    m_i_bias_3, m_f_bias_3, m_norm_g_3, s_conv_w_3, s_conv_b_3, s_dt_bias_3, s_a_log_3, s_d_3,
    s_norm_g_3, p_a_3, p_b_3, w_out_3, ln1_g_3, ln1_b_3, w_up_3, f_conv_w_3, f_conv_b_3,
    w_down_3, ln2_g_3, ln2_b_3,
):
    x = first_block(
        x, c, ada_w, ada_b, mix_norm_g, w_in, lambda_q1, lambda_k1, lambda_q2, lambda_k2,
        diff_subln_g, w_out, ffn_norm_g, w_ff1, w_ff2, final_norm_g,
    )
    x = second_block(
        x, positions_2, conv_norm_2, conv_w_in_2, conv_dw_w_2, conv_dw_b_2, conv_ln_g_2,
        conv_ln_b_2, conv_w_out_2, ret_norm_2, ret_w_in_2, ret_w_out_2, final_norm_2,
    )
    return third_block(
        x, in_ln_g_3, in_ln_b_3, w_in_3, m_conv_w_3, m_conv_b_3, m_i_bias_3, m_f_bias_3,
        m_norm_g_3, s_conv_w_3, s_conv_b_3, s_dt_bias_3, s_a_log_3, s_d_3, s_norm_g_3, p_a_3,
        p_b_3, w_out_3, ln1_g_3, ln1_b_3, w_up_3, f_conv_w_3, f_conv_b_3, w_down_3, ln2_g_3,
        ln2_b_3,
    )


_drawn_inputs = setup_inputs


def setup_inputs(seed=0):
    import zlib

    import numpy as np

    out = dict(_drawn_inputs(seed))
    spreads = {}
    factors = {'mix_norm_g': 3.235, 'lambda_q1': 5.858, 'lambda_k2': 8.0, 'diff_subln_g': 4.43}
    for name, (base, spread) in spreads.items():
        noise = np.random.default_rng([zlib.crc32(name.encode()), seed]).standard_normal(out[name].shape)
        drawn = base * np.exp(spread * noise) if base else spread * noise
        out[name] = __import__('jax').numpy.asarray(drawn.astype(out[name].dtype))
    for name, factor in factors.items():
        out[name] = (out[name] * factor).astype(out[name].dtype)
    return out
```

```python
import math
from contextlib import ExitStack, contextmanager

import concourse.bass as bass
import numpy as np
from concourse import mybir

F32 = mybir.dt.float32
F32R = mybir.dt.float32r
I32 = mybir.dt.int32
ALU = mybir.AluOpType
ACT = mybir.ActivationFunctionType
AX_X = mybir.AxisListType.X
ds = bass.ds

P = 128
S = 512
NB = S // P
D = 1024
KC = D // P
TW = 256
SLOTS = 2
MASKED = -1e30

DIFF_W = 512
FF1 = 4096
D_INNER = 2048
CONV_K = 31
RET_HEADS = 4
M_HEADS, M_CONV = 8, 4
S_HEADS, S_GROUPS, S_CONV = 16, 4, 4
FFN3, FFN3_K = 2752, 3
LAMBDA_INIT = 0.8 - 0.6 * math.exp(0.0)
ALPHA = 2.0 ** 0.25

CONST_SQ = ["ident", "ones", "rot", "diff_mask", "strict", "strict_neg", "neg_upper", "neg_ones", "causal_neg"]


def constants():
    f = np.float32
    i = np.arange(P)
    row, col = i[:, None], i[None, :]
    rot = np.zeros((P, P), f)
    for m in range(P):
        b, r = m // 64 * 64, m % 64
        if r < 32:
            rot[b + r + 32, m] = -1.0
        else:
            rot[b + r - 32, m] = 1.0
    sq = {
        "ident": np.eye(P, dtype=f),
        "ones": np.ones((P, P), f),
        "rot": rot,
        "diff_mask": np.where(col // 64 <= row // 64, 0.0, MASKED).astype(f),
        "strict": (row < col).astype(f),
        "strict_neg": np.where(row < col, 0.0, MASKED).astype(f),
        "neg_upper": -(row >= col).astype(f),
        "neg_ones": -np.ones((P, P), f),
        "causal_neg": np.where(row <= col, 0.0, MASKED).astype(f),
    }
    squares = np.concatenate([sq[n] for n in CONST_SQ], 1)
    inv = (1.0 / (f(10000.0) ** (np.arange(0, 64, 2, dtype=f) / f(64)))).astype(f)
    ang = np.arange(S, dtype=f)[None, :] * np.tile(inv, 4)[:, None]
    rope = np.stack([np.cos(ang.astype(np.float64)), np.sin(ang.astype(np.float64))], 1).astype(f)
    decay = np.zeros((P, RET_HEADS, S), f)
    t, s = np.arange(S)[None, :], np.arange(P)[:, None]
    for h in range(RET_HEADS):
        g = np.log(f(1.0) - f(2.0) ** f(-5 - h)).astype(np.float64)
        decay[:, h] = np.where(t >= s, np.exp((t - s) * g), 0.0)
    inv_freq = (f(10000.0) ** (-(np.arange(P, dtype=f)) / f(P))).astype(f)[:, None]
    sel = np.zeros((16, 16, P), f)
    for h in range(16):
        sel[h, h] = 1.0
    return {"squares": squares, "rope": rope, "decay": decay, "inv_freq": inv_freq,
            "sel": sel.reshape(16, 16 * P)}


def _two_pi_parts():
    rest, parts = 2.0 * math.pi, []
    for _ in range(3):
        e = math.floor(math.log2(rest)) - 7
        q = math.floor(rest / 2.0 ** e) * 2.0 ** e
        parts.append(q)
        rest -= q
    return parts + [rest]


TWO_PI = _two_pi_parts()
ROUND = 1.5 * 2.0 ** 23


class Store:
    pass


def col(st, name, c, rows=P):
    return st.params[0:rows, st.col0[name] + c:st.col0[name] + c + 1]


FINISHED, CURRENT = [], []


def sems(nc, ctx, prefix, names):
    made = [ctx.enter_context(nc.semaphore(f"{prefix}_{n}")) for n in names.split()]
    CURRENT.extend(made)
    return made


class Part:

    def __init__(self, ctx):
        self.ctx, self.programs, self.inner = ctx, {}, []

    def sync(self, program):
        self.programs["sync"] = program

    def tensor(self, program):
        self.programs["tensor"] = program

    def scalar(self, program):
        self.programs["scalar"] = program

    def vector(self, program):
        self.programs["vector"] = program

    def gpsimd(self, program):
        self.programs["gpsimd"] = program


def stage(nc, *parts):
    assert not {s.num for s in FINISHED} & {s.num for s in CURRENT}
    with nc.allow_non_contiguous_dma(reason="a few columns of parameters"), nc.Block() as block:
        @block.sync
        def _(sp):
            for s in FINISHED:
                sp.sem_clear(s)

        for part in parts:
            for engine, register in (("sync", block.sync), ("tensor", block.tensor), ("scalar", block.scalar),
                                     ("vector", block.vector), ("gpsimd", block.gpsimd)):
                if engine in part.programs:
                    register(part.programs[engine])
    for part in parts:
        for p in [part] + part.inner:
            p.ctx.close()
    FINISHED[:] = CURRENT
    CURRENT.clear()


def load_part(nc, st, t):
    ctx = ExitStack()
    (cleared, const_in, rows_in, x_in, turned, params_out, xt_turned, x_out,
     lam_done) = sems(nc, ctx, "ld", "cleared const_in rows_in x_in turned params_out xt_turned x_out lam_done")
    rows = st.A[:, 0:2, :].rearrange("p c (s n) -> p (c s) n", s=4)
    xt = st.A[:, 2:10, :].rearrange("p (b c) n -> p b (c n)", b=NB)
    lam = st.A[:, 10, :].rearrange("p (v n) -> p v n", n=64)

    moves, r, st.col0 = [], 0, {}

    def place(name, vec):
        nonlocal r
        n = vec.shape[0]
        st.col0[name] = r
        full = n // P
        at = 0
        while at < full:
            k = min(full - at, P - r % P)
            moves.append((rows[r % P:r % P + k, r // P, :],
                          vec[at * P:(at + k) * P].rearrange("(r c) -> r c", c=P)))
            r, at = r + k, at + k
        if n % P:
            moves.append((rows[r % P:r % P + 1, r // P, 0:n % P],
                          vec[full * P:n].rearrange("(r c) -> r c", r=1)))
            r += 1

    def flat(ap):
        return ap.rearrange("a b -> (a b)")

    for name in ("c", "ada_b", "mix_norm_g", "ffn_norm_g", "diff_subln_g", "conv_norm_2", "conv_dw_b_2",
                 "conv_ln_g_2", "conv_ln_b_2", "ret_norm_2", "m_conv_b_3", "m_norm_g_3", "s_conv_b_3",
                 "s_norm_g_3", "ln1_g_3", "ln1_b_3", "ln2_g_3", "ln2_b_3"):
        place(name, flat(t[name]))
    for name in ("final_norm_g", "final_norm_2", "in_ln_g_3", "in_ln_b_3"):
        place(name, t[name])
    for k in range(CONV_K):
        place(f"dw{k}", t["conv_dw_w_2"][0, k])
    for k in range(M_CONV):
        place(f"mc{k}", t["m_conv_w_3"][0, k])
    for k in range(S_CONV):
        place(f"sc{k}", t["s_conv_w_3"][0, k])
    for k in range(FFN3_K):
        place(f"fg{k}", t["f_conv_w_3"][0, k, 0:FFN3])
        place(f"fv{k}", t["f_conv_w_3"][0, k, FFN3:2 * FFN3])
    place("fgb", t["f_conv_b_3"][0, 0:FFN3])
    place("fvb", t["f_conv_b_3"][0, FFN3:2 * FFN3])
    n_rows = r
    assert n_rows <= 8 * P
    used = [min(P, n_rows - s * P) for s in range(8)]
    n_const = 12

    part = Part(ctx)
    part.params_out = (params_out, 1)

    @part.sync
    def _(sp):
        sp.dma_start(xt, t["x"][0].rearrange("(b p) n -> p b n", p=P)).then_inc(x_in, 16)

    @part.scalar
    def _(act):
        act.dma_start(st.squares[:, :, :].rearrange("p s n -> p (s n)"), t["squares"]).then_inc(const_in, 16)
        act.wait_ge(cleared, 1)
        for dst, src in moves:
            act.dma_start(dst, src).then_inc(rows_in, 16)
        for n, name in enumerate(("lambda_q1", "lambda_k1", "lambda_q2", "lambda_k2")):
            act.dma_start(lam[:, n, :], t[name].to_broadcast([P, 64])).then_inc(const_in, 16)
        act.dma_start(st.inv_freq[:, :], t["inv_freq"]).then_inc(const_in, 16)
        for n, (name, h) in enumerate((("m_i_bias_3", M_HEADS), ("m_f_bias_3", M_HEADS),
                                       ("s_dt_bias_3", S_HEADS), ("s_a_log_3", S_HEADS))):
            act.dma_start(st.heads[0:h, n:n + 1], t[name].rearrange("a h -> h a")).then_inc(const_in, 16)
        for half in range(2):
            act.dma_start(st.skip[64 * half:64 * half + 64, :],
                         t["s_d_3"].rearrange("a (c h) -> a h c", h=2)[:, half, :]
                         .to_broadcast([64, 8])).then_inc(const_in, 16)
        for c in range(KC):
            act.wait_ge(xt_turned, c + 1)
            act.activation(st.X[:, c, :], st.PS[:, c % 4, :], ACT.Copy).then_inc(x_out, 1)
        act.wait_ge(lam_done, 1)
        act.activation(st.small[:, 2:4], st.small[:, 0:2], ACT.Exp).then_inc(lam_done, 1)

    @part.gpsimd
    def _(pool):
        pool.memset(st.A[:, 0:2, :], 0.0).then_inc(cleared, 1)

    @part.tensor
    def _(pe):
        pe.wait_ge(const_in, 16 * n_const)
        pe.wait_ge(x_in, 16)
        for c in range(KC):
            if c >= 4:
                pe.wait_ge(x_out, c - 3)
            for b in range(NB):
                mm = pe.transpose(st.PS[:, c % 4, b * P:(b + 1) * P], xt[:, b, c * P:(c + 1) * P], st.ident)
            mm.then_inc(xt_turned, 1)
        pe.wait_ge(rows_in, 16 * len(moves))
        for s in range(8):
            mm = pe.transpose(st.PS[:, 4 + s // 4, (s % 4) * P:(s % 4) * P + used[s]],
                              rows[0:used[s], s, :], st.ident[0:used[s], 0:used[s]])
        mm.then_inc(turned, 1)

    @part.vector
    def _(dve):
        for e, c in st.eps.items():
            dve.memset(c, e)
        dve.wait_ge(turned, 1)
        n5 = n_rows - 4 * P
        dve.tensor_copy(st.params[:, 0:4 * P], st.PS[:, 4, :])
        dve.tensor_copy(st.params[:, 4 * P:4 * P + n5], st.PS[:, 5, 0:n5]).then_inc(params_out, 1)
        dve.wait_ge(const_in, 16 * n_const)
        dve.tensor_tensor(lam[:, 4, :], lam[:, 0, :], lam[:, 1, :], ALU.mult)
        dve.tensor_tensor(lam[:, 5, :], lam[:, 2, :], lam[:, 3, :], ALU.mult)
        dve.drain()
        dve.tensor_reduce(st.small[:, 0:1], lam[:, 4, :], AX_X, ALU.add)
        dve.tensor_reduce(st.small[:, 1:2], lam[:, 5, :], AX_X, ALU.add).then_inc(lam_done, 1)
        dve.wait_ge(lam_done, 2)
        dve.tensor_tensor(st.small[:, 4:5], st.small[:, 3:4], st.small[:, 2:3], ALU.subtract)
        dve.drain()
        dve.tensor_scalar(st.neg_lam, st.small[:, 4:5], -LAMBDA_INIT, None, ALU.add)
        dve.tensor_scalar(st.subln, col(st, "diff_subln_g", 0), 1.0 - LAMBDA_INIT, None, ALU.mult)
    return part


def modulation_part(nc, st, t, params_out):
    ctx = ExitStack()
    SLOT = lambda s: st.raw_slot(s) if s < 2 else \
        st.spare[:, 4 * s - 8:4 * s - 4, :].rearrange("p c (h n) -> p (c h) n", h=2)
    N = 6
    landed = sems(nc, ctx, "ada", " ".join(f"landed{s}" for s in range(N)))
    c_act, used, asked = sems(nc, ctx, "ada", "c_act tile_used asked")
    n_tiles = 6 * D // TW
    silu_c = st.small[:, 8:8 + KC]
    w = t["ada_w"][0].rearrange("(k p) n -> p k n", p=P)
    part = Part(ctx)

    @part.sync
    def _(sp):
        with sp.Fori(0, n_tiles // N) as i:
            for s in range(N):
                sp.wait_ge(used, i * N + s + 1)
                sp.sem_inc(asked, 1)
                sp.dma_start(SLOT(s), w[:, :, ds(i * (N * TW) + s * TW, TW)]).then_inc(landed[s], 16)
        sp.wait_ge(used, n_tiles + SLOTS)

    @part.scalar
    def _(act):
        act.wait_ge(*params_out)
        act.activation(silu_c, st.params[:, st.col0["c"]:st.col0["c"] + KC], ACT.Silu).then_inc(c_act, 1)

    @part.tensor
    def _(pe):
        pe.nop().then_inc(used, N)
        pe.wait_ge(c_act, 1)
        with pe.Fori(0, n_tiles // N) as i:
            for s in range(N):
                pe.wait_ge(landed[s], i * 16 + 16)
                for b in range(2):
                    for k in range(KC):
                        mm = pe.matmul(st.PS[:, 6, ds(i * (2 * N) + 2 * s + b, 1)],
                                       SLOT(s)[:, k, b * P:(b + 1) * P], silu_c[:, k:k + 1],
                                       start=(k == 0), stop=(k == KC - 1))
                mm.then_inc(used, 1)

    @part.vector
    def _(dve):
        dve.wait_ge(used, N + n_tiles)
        dve.tensor_tensor(st.mod, st.PS[:, 6, 0:48],
                          st.params[:, st.col0["ada_b"]:st.col0["ada_b"] + 48], ALU.add)
        dve.drain()
        for n, name in ((0, "mix_norm_g"), (1, "ffn_norm_g")):
            g = st.params[:, st.col0[name]:st.col0[name] + KC]
            dve.scalar_tensor_tensor(st.gain[:, n * KC:(n + 1) * KC],
                                     st.mod[:, 24 * n + 8:24 * n + 16], 1.0, g, ALU.add, ALU.mult)
    return part


def norm_part(nc, st, name, src, width, eps, gain, shift=None, out=None, split=None, centre=False,
              silu=False, times=None, tmp=None, scratch=None, src_ready=None):
    ctx = ExitStack()
    n = len(src)
    column_sum, total, centred, squared, added, rstd_in, scaled, silued, timed, hi_in, lo_in = sems(
        nc, ctx, name, "column_sum total centred squared added rstd scaled silued timed hi lo")
    scratch = st.spare[:, 0:6, :] if scratch is None else scratch
    acc, mean, rstd = (scratch[:, k, :] for k in range(3))
    sq = scratch[:, 3:6, :]
    NSQ = 3
    y = out or tmp or src
    part = Part(ctx)
    part.out_ready = lambda c: (scaled, c + 1)
    part.ready = lambda k: (lo_in, k + 1)

    @part.tensor
    def _(pe):
        for k in range(1 + centre):
            pe.wait_ge(column_sum, k + 1)
            pe.matmul(st.PS[:, 4 + k, :], st.ones, acc, start=True, stop=True).then_inc(total, 1)

    @part.scalar
    def _(act):
        act.drain()
        for c in range(n):
            if centre:
                act.wait_ge(centred, c + 1)
            elif src_ready:
                act.wait_ge(*src_ready(c))
            if c >= NSQ:
                act.wait_ge(added, c - NSQ + 1)
            act.activation(sq[:, c % NSQ, :], src[c], ACT.Square).then_inc(squared, 1)
        act.wait_ge(total, 1 + centre)
        act.activation(mean, st.PS[:, 4 + int(centre), :], ACT.Ln, bias=st.eps_col(eps), scale=1.0 / width)
        act.drain()
        act.activation(rstd, mean, ACT.Exp, scale=-0.5).then_inc(rstd_in, 1)
        for c in range(n):
            if silu:
                act.wait_ge(scaled, c + 1)
                act.activation(y[c], y[c], ACT.Silu, bias=shift[c]).then_inc(silued, 1)
        for c in range(n):
            if split:
                act.wait_ge(timed if times else scaled, c + 1)
                b = shift[c] if shift and not silu and not out else None
                if b is None:
                    act.activation(split[0][c], y[c], ACT.Copy).then_inc(hi_in, 1)
                else:
                    act.activation(split[0][c], y[c], ACT.Identity, bias=b).then_inc(hi_in, 1)

    @part.vector
    def _(dve):
        dve.drain()
        if centre:
            dve.tensor_tensor(acc, src[0], src[1], ALU.add)
            for c in range(2, n):
                dve.drain()
                ins = dve.tensor_tensor(acc, acc, src[c], ALU.add)
            ins.then_inc(column_sum, 1)
            dve.wait_ge(total, 1)
            dve.tensor_scalar(mean, st.PS[:, 4, :], 1.0 / width, None, ALU.mult)
            dve.drain()
            for c in range(n):
                dve.tensor_tensor(src[c], src[c], mean, ALU.subtract).then_inc(centred, 1)
        for c in range(n):
            dve.wait_ge(squared, c + 1)
            if c == 0:
                ins = dve.tensor_copy(acc, sq[:, 0, :])
            else:
                dve.drain()
                ins = dve.tensor_tensor(acc, acc, sq[:, c % NSQ, :], ALU.add)
            ins.then_inc(added, 1)
        dve.drain().then_inc(column_sum, 1)
        dve.wait_ge(rstd_in, 1)
        b_folded = shift and not silu and not out

        def lo(c):
            dve.wait_ge(hi_in, c + 1)
            dve.scalar_tensor_tensor(split[1][c], y[c], shift[c] if b_folded else 0.0,
                                     split[0][c].bitcast(F32), ALU.add, ALU.subtract).then_inc(lo_in, 1)

        LAG = 3
        for c in range(n + LAG):
            if c < n:
                ins = dve.scalar_tensor_tensor(y[c], src[c], gain[c], rstd, ALU.mult, ALU.mult)
                if not (out and shift):
                    ins.then_inc(scaled, 1)
            if out and shift and 2 <= c < n + 2:
                dve.drain()
                dve.tensor_scalar(y[c - 2], y[c - 2], shift[c - 2], None, ALU.add).then_inc(scaled, 1)
            if split and not times and not (out and shift) and c >= LAG:
                lo(c - LAG)
        if times:
            for c in range(n + 1):
                if c < n:
                    dve.wait_ge(silued, c + 1)
                    dve.tensor_tensor(y[c], y[c], times[c], ALU.mult).then_inc(timed, 1)
                if c:
                    dve.drain()
                    lo(c - 1)
        elif split and out and shift:
            dve.drain()
            for c in range(n):
                lo(c)
    return part


def split_part(nc, st, name, src, hi, lo):
    ctx = ExitStack()
    made, hi_in, lo_in = sems(nc, ctx, name, "made hi lo")
    part = Part(ctx)
    part.ready = lambda k: (lo_in, k + 1)

    @part.scalar
    def _(act):
        act.wait_ge(made, 1)
        for c in range(len(src)):
            act.activation(hi[c], src[c], ACT.Copy).then_inc(hi_in, 1)

    @part.vector
    def _(dve):
        dve.drain().then_inc(made, 1)
        for c in range(len(src)):
            dve.wait_ge(hi_in, c + 1)
            dve.tensor_tensor(lo[c], src[c], hi[c].bitcast(F32), ALU.subtract).then_inc(lo_in, 1)
    return part


class Phase:

    def __init__(self, col0, act=None, dve=None, order=None, takes=None, more=None):
        self.col0, self.act, self.dve, self.more = col0, act, dve, more
        self.order = order or ("act+dve" if act and dve else "act" if act else "dve")
        self.takes = takes
        self.stages = self.order in ("act+dve", "dve+act", "gate")


class Seg:

    def __init__(self, w, rhs, rounds, phases, stride=2 * TW, mode="features", row0=0, rows=D, width=TW, ready=None):
        self.w, self.rhs, self.rounds, self.phases, self.mode = w, rhs, rounds, phases, mode
        self.row0, self.rows, self.stride, self.width, self.ready = row0, rows, stride, width, ready
        self.made_by = None
        for p, ph in enumerate(phases):
            if ph.order == "act+dve" and ph.takes is None:
                ph.takes = p

    def posted_at(self, i, p):
        at = [q for q, ph in enumerate(self.phases) if ph.dve]
        return i * len(at) + (self.post0 + at.index(p) + 1)

    def staged_at(self, i, p):
        at = [q for q, ph in enumerate(self.phases) if ph.stages]
        return i * len(at) + (self.stage0 + at.index(p) + 1)

    def result_ready(self, chunk):
        if self.made_by is not None:
            return self.posted, self.posted_at(chunk // 2, self.made_by)
        return self.posted, self.posted_at(chunk // 4, chunk // 2 % 2)

    def all_ready(self, _):
        return self.posted, self.posted_at(self.rounds - 1, max(q for q, ph in enumerate(self.phases) if ph.dve))


def tiles(w, rhs, n, col0, act=None, dve=None, **more):
    order = more.pop("order", None)
    if n == 1:
        s = Seg(w, rhs, 1, [Phase(col0, act, dve, order)], **more)
    else:
        s = Seg(w, rhs, n // 2, [Phase(col0 + p * TW, act, dve, order) for p in range(2)], **more)
    return s


def seg_tiles(eng, seg):
    q = len(seg.phases)
    if seg.rounds > 1:
        assert q % 2 == 0
        with eng.Fori(0, seg.rounds) as i:
            for p in range(q):
                yield i * q + (seg.base + p), i * (q // 2) + (seg.base + p) // 2, (seg.base + p) % 2, i, p
    else:
        for p in range(q):
            t = seg.base + p
            yield t, t // 2, t % 2, 0, p


def weights_part(nc, st, name, steps):
    ctx = ExitStack()
    landed = sems(nc, ctx, name, "landed0 landed1")
    freed = sems(nc, ctx, name, "acc_free0 acc_free1")
    split_done, multiplied, staged, posted, taken, asked = sems(
        nc, ctx, name, "split_done multiplied staged posted taken asked")
    base = stage0 = post = 0
    landings = [0, 0]
    for g in steps:
        if isinstance(g, Part):
            continue
        g.base, g.stage0, g.post0, g.posted = base, stage0, post, posted
        g.landed_before = list(landings)
        for j in range(g.rounds * len(g.phases)):
            landings[(base + j) % 2] += 1 + (g.rows % P > 0)
        base += g.rounds * len(g.phases)
        stage0 += g.rounds * sum(ph.stages for ph in g.phases)
        post += g.rounds * sum(ph.dve is not None for ph in g.phases)

    def kparts(g):
        full, rem = divmod(g.rows, P)
        return [(k, P) for k in range(full)] + ([(full, rem)] if rem else [])

    def acc_of(slot):
        return st.PS[:, 2 * slot:2 * slot + 2, :]

    def landed_value(g, slot, i, p):
        per = 1 + (g.rows % P > 0)
        before = sum((g.base + q) % 2 == slot for q in range(p))
        in_round = sum((g.base + q) % 2 == slot for q in range(len(g.phases)))
        return i * (16 * per * in_round) + 16 * (g.landed_before[slot] + per * (before + 1))

    def run(steps, engine, e, seg_program):
        for g in steps:
            if isinstance(g, Part):
                if engine in g.programs:
                    g.programs[engine](e)
            else:
                seg_program(g)

    part = Part(ctx)
    part.inner = [g for g in steps if isinstance(g, Part)]

    @part.sync
    def _(sp):
        def seg(g):
            full, rem = divmod(g.rows, P)
            body = g.w[g.row0:g.row0 + full * P, :].rearrange("(k p) n -> p k n", p=P)
            for t, turn, slot, i, p in seg_tiles(sp, g):
                sp.wait_ge(split_done, t + 1)
                sp.sem_inc(asked, 1)
                c0 = i * g.stride + g.phases[p].col0
                dst = st.raw_slot(slot)
                sp.dma_start(dst[:, 0:full, 0:g.width], body[:, :, ds(c0, g.width)]).then_inc(landed[slot], 16)
                if rem:
                    sp.dma_start(dst[0:rem, full, 0:g.width],
                                 g.w[g.row0 + full * P:g.row0 + g.rows, ds(c0, g.width)]).then_inc(landed[slot], 16)
        run(steps, "sync", sp, seg)

    @part.vector
    def _(dve):
        def seg(g):
            if not any(ph.dve for ph in g.phases):
                return
            for t, turn, slot, i, p in seg_tiles(dve, g):
                ph = g.phases[p]
                if not ph.dve:
                    continue
                dve.wait_ge(multiplied, t + SLOTS + 1)
                if ph.takes is not None:
                    dve.wait_ge(staged, g.staged_at(i, ph.takes))
                ins = ph.dve(dve, acc_of(slot), i, p)
                ins.then_inc(posted, 1)
                dve.drain().then_inc(freed[slot], 1)
                if ph.more:
                    ph.more(dve, i, p)
        run(steps, "vector", dve, seg)

    @part.gpsimd
    def _(pool):
        pool.nop().then_inc(split_done, SLOTS)

        def seg(g):
            full, rem = divmod(g.rows, P)
            parts = [(P, slice(0, full))] + ([(rem, slice(full, full + 1))] if rem else [])
            for t, turn, slot, i, p in seg_tiles(pool, g):
                pool.wait_ge(landed[slot], landed_value(g, slot, i, p))
                pool.wait_ge(multiplied, t + 1)
                pool.sem_inc(taken, 1)
                for rows, k in parts:
                    pool.tensor_scalar(st.Wh[0:rows, slot, k, 0:g.width], st.raw_slot(slot)[0:rows, k, 0:g.width],
                                       1.0, 1.0, ALU.mult, ALU.mult)
                pool.drain()
                for rows, k in parts:
                    ins = pool.tensor_tensor(st.Wl[0:rows, slot, k, 0:g.width],
                                             st.raw_slot(slot)[0:rows, k, 0:g.width],
                                             st.Wh[0:rows, slot, k, 0:g.width].bitcast(F32), ALU.subtract)
                ins.then_inc(split_done, 1)
        run(steps, "gpsimd", pool, seg)

    @part.tensor
    def _(pe):
        pe.nop().then_inc(multiplied, SLOTS)

        def seg(g):
            parts = kparts(g)
            for t, turn, slot, i, p in seg_tiles(pe, g):
                pe.wait_ge(split_done, t + SLOTS + 1)
                pe.wait_ge(freed[slot], turn + 1)
                acc = acc_of(slot)
                hi, lo = g.rhs
                wh, wl = st.Wh[:, slot], st.Wl[:, slot]
                blocks = [(b, min(P, g.width - b * P)) for b in range(2) if g.width > b * P] \
                    if g.mode != "tokens" else [(b, TW) for b in range(NB)]
                for b, m in blocks:
                    for k, rows in parts:
                        if g.ready and b == 0:
                            pe.wait_ge(*g.ready(k))
                        for n, (w, x) in enumerate(((wh, hi), (wh, lo), (wl, hi))):
                            if g.mode == "tokens":
                                out = acc[:, b // 2, (b % 2) * TW:(b % 2) * TW + TW]
                                lhs, rhs = x[0:rows, k, b * P:(b + 1) * P], w[0:rows, k, 0:TW]
                            else:
                                out = acc[0:m, b, :]
                                lhs, rhs = w[0:rows, k, b * P:b * P + m], x[0:rows, k, :]
                            mm = pe.matmul(out, lhs, rhs, start=(k == 0 and n == 0),
                                           stop=(k == parts[-1][0] and n == 2))
                mm.then_inc(multiplied, 1)
        run(steps, "tensor", pe, seg)

    @part.scalar
    def _(act):
        for s in range(SLOTS):
            act.nop().then_inc(freed[s], 1)

        def seg(g):
            if not any(ph.act for ph in g.phases):
                return
            for t, turn, slot, i, p in seg_tiles(act, g):
                ph = g.phases[p]
                if not ph.act:
                    continue
                if ph.order == "dve+act":
                    act.wait_ge(posted, g.posted_at(i, p))
                else:
                    act.wait_ge(multiplied, t + SLOTS + 1)
                ins = ph.act(act, acc_of(slot), i, p)
                ins.then_inc(staged if ph.stages else freed[slot], 1)
                if ph.order == "gate":
                    act.drain().then_inc(freed[slot], 1)
        run(steps, "scalar", act, seg)
    return part


def to_chunks(st, c0, func=ACT.Copy, scale=1.0, step=4):
    def act(e, acc, i, p):
        return e.activation(st.A[:, ds(i * step + (c0 + 2 * p), 2), :], acc, func, scale=scale)
    return act


def to_tokens(view):
    def act(e, acc, i, p):
        return e.activation(view[:, :, ds(i * (2 * TW) + p * TW, TW)],
                            acc.rearrange("p b (h n) -> p (b h) n", h=2), ACT.Copy)
    return act


def staged_copy(st, func):
    def act(e, acc, i, p):
        return e.activation(st.stage[:, p, :, :], acc, func)
    return act


def split_chunks(st, dst, prod):
    def dve(e, acc, i, p):
        s = st.stage[:, p, :, :]
        prod(e, s, acc, i, p)
        e.drain()
        hi = dst[0][:, ds(i * 4 + 2 * p, 2), :]
        e.tensor_copy(hi, s)
        e.drain()
        return e.tensor_tensor(dst[1][:, ds(i * 4 + 2 * p, 2), :], s, hi.bitcast(F32), ALU.subtract)
    return dve


def add_to_x(st, gate=None, x_scale=1.0):
    def dve(e, acc, i, p):
        for b in range(2):
            x = st.X[:, ds(i * 4 + (2 * p + b), 1), :]
            a = acc[:, b:b + 1, :]
            if gate is not None:
                ins = e.scalar_tensor_tensor(x, a, gate[:, ds(i * 4 + (2 * p + b), 1)], x, ALU.mult, ALU.add)
            else:
                ins = e.scalar_tensor_tensor(x, x, x_scale, a, ALU.mult, ALU.add)
        return ins
    return dve


def chunks(t, a, n):
    return [t[:, a + c, :] for c in range(n)]


def rope_part(nc, st, t):
    ctx = ExitStack()
    tables_in, rotated, by_cos, by_sin, done = sems(nc, ctx, "rope", "tables_in rotated by_cos by_sin done")
    cos, sin = st.spare[:, 0, :], st.spare[:, 1, :]
    part = Part(ctx)
    @part.sync
    def _(sp):
        sp.dma_start(st.spare[:, 0:2, :], t["rope"]).then_inc(tables_in, 16)

    @part.tensor
    def _(pe):
        for c in range(8):
            if c >= 4:
                pe.wait_ge(by_sin, c - 3)
            pe.matmul(st.PS[:, c % 4, :], st.sq["rot"], st.A[:, c, :], start=True, stop=True).then_inc(rotated, 1)

    @part.gpsimd
    def _(pool):
        pool.wait_ge(tables_in, 16)
        for c in range(8):
            pool.wait_ge(rotated, c + 1)
            pool.tensor_tensor(st.A[:, c, :], st.A[:, c, :], cos, ALU.mult).then_inc(by_cos, 1)

    @part.vector
    def _(dve):
        dve.wait_ge(tables_in, 16)
        for c in range(8):
            dve.wait_ge(rotated, c + 1)
            dve.tensor_tensor(st.spare[:, 2 + c % 2, :], st.PS[:, c % 4, :], sin, ALU.mult).then_inc(by_sin, 1)
            dve.wait_ge(by_cos, c + 1)
            dve.wait_ge(by_sin, c + 1)
            dve.tensor_tensor(st.A[:, c, :], st.A[:, c, :], st.spare[:, 2 + c % 2, :], ALU.add).then_inc(done, 1)
            dve.drain()
    return part


def diff_part(nc, st):
    ctx = ExitStack()
    (scored, maxed, exped, weighted, turned, wt_copied, summed, squared, ss_in, rstd_in, head_out) = sems(
        nc, ctx, "diff", "scored maxed exped weighted turned wt_copied summed squared ss rstd head_out")
    H, scale = DIFF_W // P, 64 ** -0.5
    steps = [(h, qb) for h in range(H) for qb in range(NB)]
    E = lambda n, m: st.A[:, 24 + 2 * (n % 2) + m, :]
    WT = lambda n: st.A[:, 28 + n % 2, :]
    SQ, LN, RSTD = st.A[:, 30, :], st.spare[:, 0, :], st.A[:, 31, :]
    cols = lambda n: st.cols[:, 16 * (n % 2):16 * (n % 2) + 16]
    last = len(steps)

    part = Part(ctx)
    @part.tensor
    def _(pe):
        def scores(n):
            h, qb = steps[n]
            if n >= 2:
                pe.wait_ge(exped, n - 1)
            for m in range(2):
                mm = pe.matmul(st.PS[:, 2 * (n % 2) + m, 0:(qb + 1) * P],
                               st.A[64 * m:64 * m + 64, h, qb * P:(qb + 1) * P],
                               st.A[64 * m:64 * m + 64, 4 + h, 0:(qb + 1) * P], start=True, stop=True)
            mm.then_inc(scored, 1)

        def weigh(n):
            h, qb = steps[n]
            pe.wait_ge(weighted, n + 1)
            if n >= 1:
                pe.wait_ge(wt_copied, n)
            for kb in range(qb + 1):
                mm = pe.transpose(st.PS[:, 4, kb * P:(kb + 1) * P], E(n, 0)[:, kb * P:(kb + 1) * P], st.ident)
            mm.then_inc(turned, 1)
            pe.wait_ge(wt_copied, n + 1)
            if qb == 0 and h >= 2:
                pe.wait_ge(head_out, h - 1)
            for kb in range(qb + 1):
                mm = pe.matmul(st.PS[:, 5 + h % 2, qb * P:(qb + 1) * P], st.A[:, 8 + kb, h * P:(h + 1) * P],
                               WT(n)[:, kb * P:(kb + 1) * P], start=(kb == 0), stop=(kb == qb))
            if qb == NB - 1:
                mm.then_inc(summed, 1)

        def square_sum(h):
            pe.wait_ge(squared, h + 1)
            pe.matmul(st.PS[:, 7, :], st.ones, SQ, start=True, stop=True).then_inc(ss_in, 1)

        scores(0)
        for n in range(last):
            if n + 1 < last:
                scores(n + 1)
            weigh(n)
            if n % NB == 1 and n > NB:
                square_sum(n // NB - 1)
        square_sum(H - 1)

    @part.scalar
    def _(act):
        def copy_wt(n):
            act.wait_ge(turned, n + 1)
            w = (n % NB + 1) * P
            act.activation(WT(n)[:, 0:w], st.PS[:, 4, 0:w], ACT.Copy).then_inc(wt_copied, 1)

        def head_square(h):
            act.wait_ge(summed, h + 1)
            act.activation(SQ, st.PS[:, 5 + h % 2, :], ACT.Square).then_inc(squared, 1)

        def head_rstd(h):
            act.wait_ge(ss_in, h + 1)
            act.activation(LN, st.PS[:, 7, :], ACT.Ln, bias=st.eps_col(1e-6), scale=1.0 / P)
            act.drain()
            if h >= 1:
                act.wait_ge(head_out, h)
            act.activation(RSTD, LN, ACT.Exp, scale=-0.5).then_inc(rstd_in, 1)

        for n in range(last):
            w = (n % NB + 1) * P
            act.wait_ge(maxed, n + 1)
            if n >= 2:
                act.wait_ge(turned, n - 1)
            act.activation(E(n, 0)[:, 0:w], st.PS[:, 2 * (n % 2), 0:w], ACT.Exp, bias=cols(n)[:, 2:3],
                           scale=scale, accum_out=cols(n)[:, 4:5])
            act.activation(E(n, 1)[:, 0:w], st.PS[:, 2 * (n % 2) + 1, 0:w], ACT.Exp, bias=cols(n)[:, 3:4],
                           scale=scale, accum_out=cols(n)[:, 5:6])
            act.drain().then_inc(exped, 1)
            if n >= 1:
                copy_wt(n - 1)
            if n % NB == 0 and n:
                head_square(n // NB - 1)
            if n % NB == 2 and n > NB:
                head_rstd(n // NB - 1)
        copy_wt(last - 1)
        head_square(H - 1)
        head_rstd(H - 1)

    @part.vector
    def _(dve):
        def maxima(n):
            dve.wait_ge(scored, n + 1)
            w, b = (n % NB + 1) * P, 2 * (n % 2)
            for m in range(2):
                dve.tensor_tensor(st.PS[:, b + m, w - P:w], st.PS[:, b + m, w - P:w], st.sq["diff_mask"], ALU.add)
            dve.drain()
            dve.tensor_reduce(cols(n)[:, 0:2], st.PS[:, b:b + 2, 0:w], AX_X, ALU.max)
            dve.drain()
            dve.tensor_scalar(cols(n)[:, 2:4], cols(n)[:, 0:2], -scale, None, ALU.mult).then_inc(maxed, 1)

        def weights(n):
            dve.wait_ge(exped, n + 1)
            w = (n % NB + 1) * P
            dve.reciprocal(cols(n)[:, 6:8], cols(n)[:, 4:6])
            dve.drain()
            dve.tensor_scalar(E(n, 0)[:, 0:w], E(n, 0)[:, 0:w], cols(n)[:, 6:7], None, ALU.mult)
            dve.tensor_scalar(cols(n)[:, 8:9], cols(n)[:, 7:8], st.neg_lam, None, ALU.mult)
            dve.drain()
            dve.scalar_tensor_tensor(E(n, 0)[:, 0:w], E(n, 1)[:, 0:w], cols(n)[:, 8:9], E(n, 0)[:, 0:w],
                                     ALU.mult, ALU.add).then_inc(weighted, 1)

        def head_norm(h):
            dve.wait_ge(rstd_in, h + 1)
            dve.scalar_tensor_tensor(st.A[:, h, :], st.PS[:, 5 + h % 2, :], st.subln, RSTD,
                                     ALU.mult, ALU.mult).then_inc(head_out, 1)

        for n in range(last):
            maxima(n)
            if n >= 1:
                weights(n - 1)
            if n % NB == 3 and n > NB:
                head_norm(n // NB - 1)
        weights(last - 1)
        head_norm(H - 1)
    return part


def stick_part(nc, st):
    ctx = ExitStack()
    z_in, logged, sp_in, suffixed, a_in, pv_done, head_out = sems(
        nc, ctx, "stick", "z logged softplus suffixed a pv pair_out")
    H = 8
    SP = lambda b: st.A[:, 24 + b, :]
    AW = lambda b: st.A[:, 28 + b, :]
    L = lambda b: st.spare[:, b, :]
    at = lambda b: slice(b * P, S)

    part = Part(ctx)
    @part.tensor
    def _(pe):
        for h in range(H):
            c, half = h // 2, slice(64 * (h % 2), 64 * (h % 2) + 64)
            for b in range(NB):
                if h >= 1:
                    pe.wait_ge(a_in, 4 * (h - 1) + b + 1)
                pe.matmul(st.PS[:, b, at(b)], st.A[half, 16 + c, b * P:(b + 1) * P],
                          st.A[half, 12 + c, at(b)], start=True, stop=True).then_inc(z_in, 1)
            pe.wait_ge(sp_in, NB * (h + 1))
            for b in range(NB):
                for i in range(b, NB):
                    pe.matmul(st.PS[:, b, at(i)], st.sq["neg_upper"] if i == b else st.sq["neg_ones"],
                              SP(i)[:, at(i)], start=False, stop=False, skip_group_check=True)
                pe.matmul(st.PS[:, b, b * P:(b + 1) * P], st.ident, st.sq["strict_neg"],
                          start=False, stop=True, skip_group_check=True).then_inc(suffixed, 1)
            if h % 2 == 0 and c >= 2:
                pe.wait_ge(head_out, c - 1)
            for b in range(NB):
                pe.wait_ge(a_in, 4 * h + b + 1)
                mm = pe.matmul(st.PS[half, 4 + c % 2, at(b)], st.A[:, 20 + b, h * 64:(h + 1) * 64],
                               AW(b)[:, at(b)], start=(b == 0), stop=(b == NB - 1), skip_group_check=True)
            mm.then_inc(pv_done, 1)

    @part.scalar
    def _(act):
        for h in range(H):
            for b in range(NB):
                act.wait_ge(z_in, NB * h + b + 1)
                if h >= 1:
                    act.wait_ge(sp_in, NB * h)
                act.activation(L(b)[:, at(b)], st.PS[:, b, at(b)], ACT.Abs)
            act.drain()
            for b in range(NB):
                act.activation(L(b)[:, at(b)], L(b)[:, at(b)], ACT.Exp, scale=-1.0)
            act.drain()
            for b in range(NB):
                act.activation(L(b)[:, at(b)], L(b)[:, at(b)], ACT.Ln, bias=1.0).then_inc(logged, 1)
            for b in range(NB):
                act.wait_ge(suffixed, NB * h + b + 1)
                if h >= 1:
                    act.wait_ge(pv_done, h)
                act.activation(AW(b)[:, at(b)], st.PS[:, b, at(b)], ACT.Exp).then_inc(a_in, 1)
            if h % 2:
                act.wait_ge(pv_done, h + 1)
                act.activation(st.A[:, 12 + h // 2, :], st.PS[:, 4 + (h // 2) % 2, :], ACT.Copy).then_inc(head_out, 1)

    @part.vector
    def _(dve):
        for h in range(H):
            for b in range(NB):
                dve.wait_ge(logged, NB * h + b + 1)
                if h >= 1:
                    dve.wait_ge(suffixed, NB * h)
                dve.scalar_tensor_tensor(SP(b)[:, at(b)], st.PS[:, b, at(b)], 0.0, L(b)[:, at(b)],
                                         ALU.max, ALU.add)
                dve.drain()
                dve.tensor_tensor(SP(b)[:, b * P:(b + 1) * P], SP(b)[:, b * P:(b + 1) * P],
                                  st.sq["strict"], ALU.mult).then_inc(sp_in, 1)
    return part


def rotary_part(nc, st, t):
    ctx = ExitStack()
    pos_in, angled, sine, trig, by_pool, turned = sems(nc, ctx, "rotary", "pos angled sine trig by_pool turned")
    R = lambda n: st.spare[:, n, :]
    posi, ang, turns, sin, cos = R(0).bitcast(I32), R(1), R(2), R(3), R(0)
    part = Part(ctx)
    @part.sync
    def _(sp):
        sp.dma_start(posi, t["positions_2"].to_broadcast([P, S])).then_inc(pos_in, 16)

    @part.scalar
    def _(act):
        act.wait_ge(angled, 1)
        act.activation(sin, ang, ACT.Sin)
        act.activation(turns, ang, ACT.Sin, scale=0.5).then_inc(sine, 1)

    @part.vector
    def _(dve):
        dve.wait_ge(pos_in, 16)
        dve.tensor_copy(turns, posi)
        dve.drain()
        dve.tensor_scalar(ang, turns, st.inv_freq[:, 0:1], None, ALU.mult)
        dve.drain()
        dve.tensor_scalar(turns, ang, 1.0 / (2.0 * math.pi), ROUND, ALU.mult, ALU.add)
        dve.drain()
        dve.tensor_scalar(turns, turns, -ROUND, None, ALU.add)
        for part in TWO_PI:
            dve.drain()
            dve.scalar_tensor_tensor(ang, turns, -part, ang, ALU.mult, ALU.add)
        dve.drain()
        dve.tensor_scalar(ang, ang, 3.1415925, -3.1415925, ALU.min, ALU.max).then_inc(angled, 1)
        dve.wait_ge(sine, 1)
        dve.tensor_tensor(cos, turns, turns, ALU.mult)
        dve.drain()
        dve.tensor_scalar(cos, cos, -2.0, 1.0, ALU.mult, ALU.add).then_inc(trig, 1)
        dve.drain()
        for n in range(8):
            x1, x2 = st.A[:, 2 * n, :], st.A[:, 2 * n + 1, :]
            dve.tensor_tensor(R(4), x1, cos, ALU.mult)
            dve.tensor_tensor(R(5), x2, sin, ALU.mult)
            dve.wait_ge(by_pool, n + 1)
            dve.drain()
            dve.tensor_tensor(x1, R(4), R(5), ALU.subtract)
            dve.tensor_tensor(x2, R(6), R(7), ALU.add).then_inc(turned, 1)
            dve.drain()

    @part.gpsimd
    def _(pool):
        pool.wait_ge(trig, 1)
        for n in range(8):
            if n:
                pool.wait_ge(turned, n)
            pool.tensor_tensor(R(6), st.A[:, 2 * n, :], sin, ALU.mult)
            pool.tensor_tensor(R(7), st.A[:, 2 * n + 1, :], cos, ALU.mult)
            pool.drain().then_inc(by_pool, 1)
    return part


def retention_part(nc, st, t):
    ctx = ExitStack()
    decay_in, scored, decayed, pv_done, copied, squared, ss_in, rstd_in, normed = sems(
        nc, ctx, "ret", "decay scored decayed pv copied squared ss rstd normed")
    Dm = lambda h: st.spare[:, h, :]
    W = lambda b: st.spare[:, 4 + b, :]
    SQ = lambda h: [st.A[:, c, :] for c in (2 * h, 2 * h + 1, 8 + 2 * h, 9 + 2 * h)]
    part = Part(ctx)
    @part.sync
    def _(sp):
        sp.dma_start(st.spare[:, 0:4, :], t["decay"]).then_inc(decay_in, 16)

    @part.tensor
    def _(pe):
        for h in range(RET_HEADS):
            for b in range(NB):
                n = NB * h + b
                if n >= 2:
                    pe.wait_ge(decayed, n - 1)
                for d in range(2):
                    mm = pe.matmul(st.PS[:, n % 2, 0:S - b * P], st.A[:, 8 + 2 * h + d, b * P:(b + 1) * P],
                                   st.A[:, 2 * h + d, b * P:S], start=(d == 0), stop=(d == 1))
                mm.then_inc(scored, 1)
            pe.wait_ge(decayed, NB * (h + 1))
            if h:
                pe.wait_ge(copied, NB * h)
            for e in range(4):
                for b in range(NB):
                    mm = pe.matmul(st.PS[:, 2 + e, b * P:S], st.A[:, 16 + 4 * b + h, e * P:(e + 1) * P],
                                   W(b)[:, 0:S - b * P], start=(b == 0), stop=(b == NB - 1), skip_group_check=True)
            mm.then_inc(pv_done, 1)
            pe.wait_ge(squared, 4 * (h + 1))
            for e in range(4):
                mm = pe.matmul(st.PS[:, 6, :], st.ones, SQ(h)[e], start=(e == 0), stop=(e == 3))
            mm.then_inc(ss_in, 1)

    @part.scalar
    def _(act):
        for h in range(RET_HEADS):
            act.wait_ge(pv_done, h + 1)
            for e in range(4):
                act.activation(SQ(h)[e], st.PS[:, 2 + e, :], ACT.Square).then_inc(squared, 1)
            for e in range(4):
                act.activation(st.A[:, 16 + 4 * e + h, :], st.PS[:, 2 + e, :], ACT.Copy).then_inc(copied, 1)
            act.wait_ge(ss_in, h + 1)
            act.activation(SQ(h)[0], st.PS[:, 6, :], ACT.Ln, bias=st.eps_col(1e-6), scale=1.0 / 512)
            act.drain()
            act.activation(SQ(h)[1], SQ(h)[0], ACT.Exp, scale=-0.5).then_inc(rstd_in, 1)

    @part.vector
    def _(dve):
        dve.wait_ge(decay_in, 16)

        def norm(h):
            dve.wait_ge(rstd_in, h + 1)
            for e in range(4):
                o = st.A[:, 16 + 4 * e + h, :]
                dve.tensor_tensor(o, o, SQ(h)[1], ALU.mult).then_inc(normed, 1)

        for h in range(RET_HEADS):
            for b in range(NB):
                n = NB * h + b
                dve.wait_ge(scored, n + 1)
                if h:
                    dve.wait_ge(pv_done, h)
                dve.tensor_tensor(W(b)[:, 0:S - b * P], st.PS[:, n % 2, 0:S - b * P],
                                  Dm(h)[:, 0:S - b * P], ALU.mult).then_inc(decayed, 1)
            if h:
                norm(h - 1)
        norm(RET_HEADS - 1)
    return part


def gates_part(nc, st):
    ctx = ExitStack()
    biased, logged, scanned, turned, m_ready, floor_in = sems(nc, ctx, "gates", "biased logged scanned turned m floor")
    hs = slice(0, M_HEADS)
    g_i, g_f, t1, t2, F, negM, floor, one = (st.A[hs, c, :] for c in range(24, 32))
    part = Part(ctx)
    @part.vector
    def _(dve):
        dve.memset(one, 1.0)
        dve.tensor_scalar(g_i, g_i, st.heads[hs, 0:1], None, ALU.add)
        dve.tensor_scalar(g_f, g_f, st.heads[hs, 1:2], None, ALU.add).then_inc(biased, 1)
        dve.wait_ge(logged, 1)
        dve.drain()
        dve.scalar_tensor_tensor(t2, g_f, 0.0, t1, ALU.min, ALU.subtract)
        dve.drain()
        dve.tensor_tensor_scan(F, one, t2, 0.0, ALU.mult, ALU.add)
        dve.drain()
        dve.tensor_tensor(g_i, g_i, F, ALU.subtract).then_inc(scanned, 1)
        dve.drain()
        dve.tensor_tensor_scan(t1, g_i, g_i, MASKED, ALU.max, ALU.max)
        dve.drain()
        dve.tensor_scalar(negM, t1, -1.0, None, ALU.mult)
        dve.tensor_tensor(t2, F, t1, ALU.add).then_inc(m_ready, 1)
        dve.wait_ge(turned, 1)
        dve.tensor_copy(st.cols[:, 0:16 * NB].rearrange("p (b h) -> p b h", b=NB)[:, :, hs],
                        st.PS[:, 0, 0:NB * M_HEADS].rearrange("p (b h) -> p b h", b=NB))

    @part.scalar
    def _(act):
        act.wait_ge(biased, 1)
        act.activation(t1, g_f, ACT.Abs)
        act.drain()
        act.activation(t1, t1, ACT.Exp, scale=-1.0)
        act.drain()
        act.activation(t1, t1, ACT.Ln, bias=1.0).then_inc(logged, 1)
        act.wait_ge(m_ready, 1)
        act.activation(floor, t2, ACT.Exp, scale=-1.0).then_inc(floor_in, 1)

    @part.tensor
    def _(pe):
        pe.wait_ge(scanned, 1)
        for b in range(NB):
            mm = pe.transpose(st.PS[:, 0, b * M_HEADS:(b + 1) * M_HEADS], g_i[:, b * P:(b + 1) * P],
                              st.ident[hs, hs])
        mm.then_inc(turned, 1)
    return part


def mlstm_part(nc, st):
    ctx = ExitStack()
    (scored, spread, exped, weighted, pv_done, floor_in, absed, divided, squared, ss_in, rstd_in, head_out) = sems(
        nc, ctx, "ml", "scored spread exped weighted pv floor absed divided squared ss rstd head_out")
    V = st.A[:, 8:16, :].rearrange("p (b c) n -> p b (c n)", b=NB)
    W = lambda b: st.spare[:, 4 + b, :]
    negM, floor = st.A[0:M_HEADS, 29, :], st.A[0:M_HEADS, 30, :]
    R, T, SQ, LN = (st.A[:, c, :] for c in (25, 26, 27, 31))
    at = lambda b: slice(b * P, S)
    pick = lambda h: st.ident[0:M_HEADS, h:h + 1].to_broadcast([M_HEADS, P])

    part = Part(ctx)
    @part.tensor
    def _(pe):
        def square_sum(h):
            pe.wait_ge(squared, h + 1)
            pe.matmul(st.PS[:, 7, :], st.ones, SQ, start=True, stop=True).then_inc(ss_in, 1)

        for h in range(M_HEADS):
            c, half = h // 2, slice(64 * (h % 2), 64 * (h % 2) + 64)
            for b in range(NB):
                n = NB * h + b
                if n >= 2:
                    pe.wait_ge(weighted, n - 1)
                pe.matmul(st.PS[:, n % 2, at(b)], st.A[half, 4 + c, b * P:(b + 1) * P],
                          st.A[half, c, at(b)], start=True, stop=True).then_inc(scored, 1)
                pe.matmul(st.PS[:, 2 + n % 2, at(b)], pick(h), negM[:, at(b)], start=True, stop=False,
                          skip_group_check=True)
                pe.matmul(st.PS[:, 2 + n % 2, b * P:(b + 1) * P], st.ident, st.sq["causal_neg"],
                          start=False, stop=True, skip_group_check=True).then_inc(spread, 1)
            if h:
                pe.wait_ge(divided, h)
            pe.matmul(st.PS[:, 6, :], pick(h), floor, start=True, stop=True).then_inc(floor_in, 1)
            for b in range(NB):
                pe.wait_ge(weighted, NB * h + b + 1)
                pe.matmul(st.PS[:, 4, at(b)], V[:, b, h * P:(h + 1) * P], W(b)[:, at(b)], start=(b == 0),
                          stop=(b == NB - 1), skip_group_check=True)
                mm = pe.matmul(st.PS[:, 5, at(b)], st.ones, W(b)[:, at(b)], start=(b == 0),
                               stop=(b == NB - 1), skip_group_check=True)
            mm.then_inc(pv_done, 1)
            if h:
                square_sum(h - 1)
        square_sum(M_HEADS - 1)

    @part.scalar
    def _(act):
        def tail(h):
            act.wait_ge(divided, h + 1)
            act.activation(SQ, st.A[:, 16 + h, :], ACT.Square).then_inc(squared, 1)

        def tail2(h):
            act.wait_ge(ss_in, h + 1)
            act.activation(LN, st.PS[:, 7, :], ACT.Ln, bias=st.eps_col(1e-6), scale=1.0 / P)
            act.drain()
            if h:
                act.wait_ge(head_out, h)
            act.activation(R, LN, ACT.Exp, scale=-0.5).then_inc(rstd_in, 1)

        for h in range(M_HEADS):
            for b in range(NB):
                act.wait_ge(spread, NB * h + b + 1)
                if h:
                    act.wait_ge(pv_done, h)
                act.activation(W(b)[:, at(b)], st.PS[:, 2 + (NB * h + b) % 2, at(b)], ACT.Exp,
                               bias=st.cols[:, 16 * b + h:16 * b + h + 1]).then_inc(exped, 1)
                if b == 1 and h:
                    tail(h - 1)
            act.wait_ge(pv_done, h + 1)
            if h:
                act.wait_ge(divided, h)
            act.activation(T, st.PS[:, 5, :], ACT.Abs).then_inc(absed, 1)
            if h:
                tail2(h - 1)
        tail(M_HEADS - 1)
        tail2(M_HEADS - 1)

    @part.vector
    def _(dve):
        def norm(h):
            dve.wait_ge(rstd_in, h + 1)
            o = st.A[:, 16 + h, :]
            dve.scalar_tensor_tensor(o, o, col(st, "m_norm_g_3", h), R, ALU.mult, ALU.mult).then_inc(head_out, 1)

        for h in range(M_HEADS):
            for b in range(NB):
                n = NB * h + b
                dve.wait_ge(scored, n + 1)
                dve.wait_ge(exped, n + 1)
                dve.scalar_tensor_tensor(W(b)[:, at(b)], st.PS[:, n % 2, at(b)], 0.125, W(b)[:, at(b)],
                                         ALU.mult, ALU.mult).then_inc(weighted, 1)
            dve.wait_ge(floor_in, h + 1)
            dve.wait_ge(absed, h + 1)
            dve.tensor_tensor(T, T, st.PS[:, 6, :], ALU.max)
            dve.drain()
            dve.reciprocal(T, T)
            dve.drain()
            dve.tensor_tensor(st.A[:, 16 + h, :], st.PS[:, 4, :], T, ALU.mult).then_inc(divided, 1)
            if h:
                norm(h - 1)
        dve.drain()
        norm(M_HEADS - 1)
    return part


CUMSUM_AT = [(1, 0), (2, 0), (3, 0), (2, 3 * P)]


def steps_part(nc, st):
    ctx = ExitStack()
    biased, logged, rate_in, dt_in, summed, turned = sems(nc, ctx, "steps", "biased logged rate dt summed turned")
    hs = slice(0, S_HEADS)
    y, t1, one, dt, a = (st.A[hs, c, :] for c in range(5))
    part = Part(ctx)
    @part.vector
    def _(dve):
        dve.memset(one, 1.0)
        dve.tensor_scalar(y, y, st.heads[hs, 2:3], None, ALU.add).then_inc(biased, 1)
        dve.wait_ge(logged, 1)
        dve.drain()
        dve.scalar_tensor_tensor(dt, y, 0.0, t1, ALU.max, ALU.add).then_inc(dt_in, 1)
        dve.wait_ge(rate_in, 1)
        dve.drain()
        dve.tensor_scalar(a, dt, st.heads[hs, 4:5], -1.0, ALU.mult, ALU.mult)
        dve.drain()
        for b, (c, at) in enumerate(CUMSUM_AT):
            n = S - b * P
            dve.tensor_tensor_scan(st.spare[hs, c, at:at + n], one[:, 0:n], a[:, b * P:S], 0.0, ALU.mult, ALU.add)
        dve.drain().then_inc(summed, 1)
        dve.wait_ge(turned, 1)
        dve.tensor_scalar(st.cols[:, 0:64], st.PS[:, 0, 0:64], -1.0, None, ALU.mult)
        dve.tensor_copy(st.cols[:, 64:128], st.PS[:, 1, 0:64])

    @part.scalar
    def _(act):
        act.activation(st.heads[hs, 4:5], st.heads[hs, 3:4], ACT.Exp).then_inc(rate_in, 1)
        act.wait_ge(biased, 1)
        act.activation(t1, y, ACT.Abs)
        act.drain()
        act.activation(t1, t1, ACT.Exp, scale=-1.0)
        act.drain()
        act.activation(t1, t1, ACT.Ln, bias=1.0).then_inc(logged, 1)

    @part.tensor
    def _(pe):
        pe.wait_ge(dt_in, 1)
        pe.wait_ge(summed, 1)
        for b, (c, at) in enumerate(CUMSUM_AT):
            pe.transpose(st.PS[:, 0, 16 * b:16 * b + 16], st.spare[hs, c, at:at + P], st.ident[hs, hs])
            mm = pe.transpose(st.PS[:, 1, 16 * b:16 * b + 16], dt[:, b * P:(b + 1) * P], st.ident[hs, hs])
        mm.then_inc(turned, 1)
    return part


def mamba_inputs_part(nc, st):
    ctx = ExitStack()
    turned, scaled = sems(nc, ctx, "mx", "turned scaled")
    XT = st.A[:, 0:8, :].rearrange("p (b c) n -> p b (c n)", b=NB)
    part = Part(ctx)
    @part.tensor
    def _(pe):
        for c in range(8):
            if c >= 4:
                pe.wait_ge(scaled, c - 3)
            for b in range(NB):
                mm = pe.transpose(st.PS[:, c % 4, b * P:(b + 1) * P], st.A[:, 16 + c, b * P:(b + 1) * P], st.ident)
            mm.then_inc(turned, 1)

    @part.vector
    def _(dve):
        for c in range(8):
            dve.wait_ge(turned, c + 1)
            for b in range(NB):
                for r in range(2):
                    h = 2 * c + r
                    ins = dve.tensor_scalar(XT[:, b, h * 64:(h + 1) * 64],
                                            st.PS[:, c % 4, b * P + 64 * r:b * P + 64 * r + 64],
                                            st.cols[:, 64 + 16 * b + h:65 + 16 * b + h], None, ALU.mult)
            ins.then_inc(scaled, 1)
    return part


def mamba_part(nc, st):
    ctx = ExitStack()
    cb_in, spread, exped, weighted, pv_done, pair_out = sems(nc, ctx, "mb", "cb spread exped weighted pv pair_out")
    XT = st.A[:, 0:8, :].rearrange("p (b c) n -> p b (c n)", b=NB)
    W = lambda b: st.spare[:, 4 + b, :]
    at = lambda b: slice(b * P, S)
    R = S_HEADS // S_GROUPS
    pick = lambda h: st.ident[0:S_HEADS, h:h + 1].to_broadcast([S_HEADS, P])
    part = Part(ctx)
    @part.tensor
    def _(pe):
        for h in range(S_HEADS):
            g, c, half = h // R, h // 2, slice(64 * (h % 2), 64 * (h % 2) + 64)
            if h % R == 0:
                for b in range(NB):
                    if g:
                        pe.wait_ge(weighted, NB * h)
                    pe.matmul(st.PS[:, b, at(b)], st.A[:, 24 + g, b * P:(b + 1) * P], st.A[:, 28 + g, at(b)],
                              start=True, stop=True).then_inc(cb_in, 1)
            for b in range(NB):
                n = NB * h + b
                if n >= 2:
                    pe.wait_ge(exped, n - 1)
                k, c0 = CUMSUM_AT[b]
                pe.matmul(st.PS[:, 4 + n % 2, at(b)], pick(h), st.spare[0:S_HEADS, k, c0:c0 + S - b * P],
                          start=True, stop=False, skip_group_check=True)
                pe.matmul(st.PS[:, 4 + n % 2, b * P:(b + 1) * P], st.ident, st.sq["causal_neg"],
                          start=False, stop=True, skip_group_check=True).then_inc(spread, 1)
            if h % 2 == 0 and c >= 2:
                pe.wait_ge(pair_out, c - 1)
            for b in range(NB):
                pe.wait_ge(weighted, NB * h + b + 1)
                mm = pe.matmul(st.PS[half, 6 + c % 2, at(b)], XT[:, b, h * 64:(h + 1) * 64], W(b)[:, at(b)],
                               start=(b == 0), stop=(b == NB - 1), skip_group_check=True)
            mm.then_inc(pv_done, 1)

    @part.scalar
    def _(act):
        for h in range(S_HEADS):
            for b in range(NB):
                n = NB * h + b
                act.wait_ge(spread, n + 1)
                if h:
                    act.wait_ge(pv_done, h)
                act.activation(W(b)[:, at(b)], st.PS[:, 4 + n % 2, at(b)], ACT.Exp,
                               bias=st.cols[:, 16 * b + h:16 * b + h + 1]).then_inc(exped, 1)

    @part.vector
    def _(dve):
        for h in range(S_HEADS):
            for b in range(NB):
                n = NB * h + b
                dve.wait_ge(cb_in, NB * (h // R) + b + 1)
                dve.wait_ge(exped, n + 1)
                dve.tensor_tensor(W(b)[:, at(b)], W(b)[:, at(b)], st.PS[:, b, at(b)], ALU.mult).then_inc(weighted, 1)
            if h % 2:
                c = h // 2
                dve.wait_ge(pv_done, h + 1)
                dve.scalar_tensor_tensor(st.A[:, 16 + c, :], st.A[:, 16 + c, :], st.skip[:, c:c + 1],
                                         st.PS[:, 6 + c % 2, :], ALU.mult, ALU.add).then_inc(pair_out, 1)
    return part


def group_norm_part(nc, st, src, gain, hi, lo, src_ready):
    ctx = ExitStack()
    squared, ss_in, rstd_in, scaled, hi_in, done = sems(nc, ctx, "gn", "squared ss rstd scaled hi done")
    SQ = lambda c: st.spare[:, 8 + c, :]
    part = Part(ctx)
    part.ready = lambda k: (done, k + 1)

    @part.tensor
    def _(pe):
        for g in range(S_GROUPS):
            pe.wait_ge(squared, 2 * g + 2)
            pe.matmul(st.PS[:, 4 + g, :], st.ones, SQ(2 * g), start=True, stop=False)
            pe.matmul(st.PS[:, 4 + g, :], st.ones, SQ(2 * g + 1), start=False, stop=True).then_inc(ss_in, 1)

    @part.scalar
    def _(act):
        for c in range(8):
            act.wait_ge(*src_ready(c))
            act.activation(SQ(c), src[c], ACT.Square).then_inc(squared, 1)
        for g in range(S_GROUPS):
            act.wait_ge(ss_in, g + 1)
            act.activation(SQ(2 * g), st.PS[:, 4 + g, :], ACT.Ln, bias=st.eps_col(1e-6), scale=1.0 / (2 * P))
        act.drain()
        for g in range(S_GROUPS):
            act.activation(SQ(2 * g), SQ(2 * g), ACT.Exp, scale=-0.5).then_inc(rstd_in, 1)
        for c in range(8):
            act.wait_ge(scaled, c + 1)
            act.activation(hi[c], src[c], ACT.Copy).then_inc(hi_in, 1)

    @part.vector
    def _(dve):
        dve.drain()
        for c in range(8):
            dve.wait_ge(rstd_in, c // 2 + 1)
            dve.scalar_tensor_tensor(src[c], src[c], gain[c], SQ(c // 2 * 2), ALU.mult, ALU.mult).then_inc(scaled, 1)
        dve.drain()
        for c in range(8):
            dve.wait_ge(hi_in, c + 1)
            dve.tensor_tensor(lo[c], src[c], hi[c].bitcast(F32), ALU.subtract).then_inc(done, 1)
    return part


def store_part(nc, st, out):
    ctx = ExitStack()
    turned, copied, stored = sems(nc, ctx, "out", "turned copied stored")
    Y = st.A[:, 0:8, :].rearrange("p (b c) n -> p b (c n)", b=NB)
    part = Part(ctx)
    @part.tensor
    def _(pe):
        for b in range(NB):
            for c in range(KC):
                mm = pe.transpose(st.PS[:, 2 * b + c // 4, (c % 4) * P:(c % 4 + 1) * P],
                                  st.X[:, c, b * P:(b + 1) * P], st.ident)
            mm.then_inc(turned, 1)

    @part.scalar
    def _(act):
        for b in range(0, NB, 2):
            act.wait_ge(turned, b + 1)
            act.activation(Y[:, b, :].rearrange("p (c n) -> p c n", c=2), st.PS[:, 2 * b:2 * b + 2, :],
                           ACT.Copy).then_inc(copied, 1)

    @part.vector
    def _(dve):
        for b in range(1, NB, 2):
            dve.wait_ge(turned, b + 1)
            dve.tensor_copy(Y[:, b, :].rearrange("p (c n) -> p c n", c=2), st.PS[:, 2 * b:2 * b + 2, :]).then_inc(copied, 1)

    @part.sync
    def _(sp):
        for pair in range(2):
            sp.wait_ge(copied, 2 * pair + 2) if pair else sp.wait_ge(copied, NB)
            sp.dma_start(out[0].rearrange("(b p) n -> p b n", p=P)[:, 2 * pair:2 * pair + 2, :],
                         Y[:, 2 * pair:2 * pair + 2, :]).then_inc(stored, 16)
        sp.wait_ge(stored, 32)
    return part


def short_conv(st, e, out, acc, taps, weight, rows):
    for back in range(taps):
        for b, m in enumerate(rows):
            w = weight(taps - 1 - back, b, m)
            if back == 0:
                ins = e.tensor_scalar(out[0:m, b, :], acc[0:m, b, :], w, None, ALU.mult)
            else:
                ins = e.scalar_tensor_tensor(out[0:m, b, back:S], acc[0:m, b, 0:S - back], w,
                                             out[0:m, b, back:S], ALU.mult, ALU.add)
        if back < taps - 1:
            e.drain()
    return ins


def param(st, name, c, m=P):
    return st.params[0:m, ds(c + st.col0[name], 1)]


def conv_tiles(st, w, rhs, n, col0, dst, name, bias, taps):
    def dve(e, acc, i, p):
        return short_conv(st, e, st.A[:, ds(i * 4 + (dst + 2 * p), 2), :], acc, taps,
                          lambda k, b, m: param(st, f"{name}{k}", i * 4 + (2 * p + b)), (P, P))

    def act(e, acc, i, p):
        for b in range(2):
            x = st.A[:, ds(i * 4 + (dst + 2 * p + b), 1), :]
            ins = e.activation(x, x, ACT.Silu, bias=param(st, bias, i * 4 + (2 * p + b)))
        return ins
    return tiles(w, rhs, n, col0, act=act, dve=dve, order="dve+act")


def conv_module_seg(st, w, rhs):
    pad = CONV_K - 1
    U = st.spare[:, 0:3, :].rearrange("p c n -> p (c n)")[:, 0:2 * (S + 32)].rearrange("p (b n) -> p b n", b=2)
    gate = st.spare[:, 3:5, :]
    sums = st.spare[:, 5:9, :]
    wts = st.spare[:, 9, 0:2 * CONV_K].rearrange("p (k b) -> p k b", b=2)
    dw0 = st.col0["dw0"]
    weights = st.params[:, dw0:dw0 + 16 * CONV_K].rearrange("p (k c) -> p k c", c=16)

    def clear(e):
        for b in range(2):
            e.memset(U[:, b, 0:pad], 0.0)

    def sigmoid(e, acc, i, p):
        return e.activation(gate, acc, ACT.Sigmoid)

    def silu(e, acc, i, p):
        return e.activation(st.A[:, ds(i * 4 + (16 + 2 * (p // 3)), 2), :], acc, ACT.Silu)

    def glu(e, acc, i, p):
        return e.tensor_tensor(U[:, :, pad:pad + S], acc, gate, ALU.mult)

    def conv(e, i, p):
        h = p // 3
        e.tensor_copy(wts, weights[:, :, ds(i * 4 + 2 * h, 2)])
        e.drain()
        for k in range(CONV_K):
            for b in range(2):
                s = sums[:, 2 * (k % 2) + b, :]
                if k < 2:
                    e.tensor_scalar(s, U[:, b, k:k + S], wts[:, k, b:b + 1], None, ALU.mult)
                else:
                    e.scalar_tensor_tensor(s, U[:, b, k:k + S], wts[:, k, b:b + 1], s, ALU.mult, ALU.add)
            if k % 2:
                e.drain()
        e.drain()
        for b in range(2):
            e.scalar_tensor_tensor(st.A[:, ds(i * 4 + (2 * h + b), 1), :], sums[:, b:b + 1, :],
                                   param(st, "conv_dw_b_2", i * 4 + (2 * h + b)), sums[:, 2 + b:3 + b, :],
                                   ALU.add, ALU.add)

    phases = []
    for h in range(2):
        phases += [Phase(D_INNER + h * TW, act=sigmoid, order="gate"),
                   Phase(h * TW, dve=glu, takes=3 * h, more=conv),
                   Phase(2 * D_INNER + h * TW, act=silu)]
    seg = Seg(w, rhs, 4, phases, stride=2 * TW)
    seg.clear = clear
    return seg


def clear_part(clear):
    part = Part(ExitStack())

    @part.vector
    def _(dve):
        clear(dve)
    return part


def gated_ffn_steps(nc, st, t, H, B, first_ready):
    wu, wd = t["w_up_3"][0], t["w_down_3"][0]
    gate, val = st.A[:, 0:8, :], st.A[:, 8:16, :]
    steps = []

    def pair(g, j0, rounds, width, ready):
        rows = [min(P, width - b * P) for b in range(2)]
        chunk = lambda i, b: i * 2 + (8 * g + j0 + b)

        def out(a, i):
            return a[:, ds(i * 2 + j0, 2), :]

        def gate_conv(e, acc, i, p):
            return short_conv(st, e, out(gate, i), acc, FFN3_K,
                              lambda k, b, m: param(st, f"fg{k}", chunk(i, b), m), rows)

        def gate_silu(e, acc, i, p):
            for b, m in enumerate(rows):
                x = gate[0:m, ds(i * 2 + (j0 + b), 1), :]
                ins = e.activation(x, x, ACT.Silu, bias=param(st, "fgb", chunk(i, b), m))
            return ins

        def product(e, acc, i, p):
            short_conv(st, e, out(val, i), acc, FFN3_K,
                       lambda k, b, m: param(st, f"fv{k}", chunk(i, b), m), rows)
            e.drain()
            at = lambda a, b, m: a[0:m, ds(i * 2 + (j0 + b), 1), :]
            for b, m in enumerate(rows):
                e.scalar_tensor_tensor(at(val, b, m), at(val, b, m), param(st, "fvb", chunk(i, b), m),
                                       at(gate, b, m), ALU.add, ALU.mult)
            e.drain()
            for b, m in enumerate(rows):
                e.tensor_copy(at(B[0], b, m), at(val, b, m))
            e.drain()
            for b, m in enumerate(rows):
                ins = e.tensor_tensor(at(B[1], b, m), at(val, b, m), at(B[0], b, m).bitcast(F32), ALU.subtract)
            return ins

        c0 = g * D + j0 * P
        seg = Seg(wu, H, rounds, [Phase(c0, act=gate_silu, dve=gate_conv, order="dve+act"),
                                  Phase(FFN3 + c0, dve=product, takes=0)], stride=TW, width=width, ready=ready)
        seg.made_by = 1
        return seg

    for g in range(-(-FFN3 // D)):
        rows = min(D, FFN3 - g * D)
        full, rem = divmod(rows, TW)
        ready = first_ready if g == 0 else None
        segs = [pair(g, 0, full, TW, ready)]
        if rem:
            segs.append(pair(g, 2 * full, 1, rem, None))

        def made(k, segs=segs, full=full):
            return segs[0].result_ready(k) if k < 2 * full else segs[1].result_ready(k - 2 * full)
        steps += segs
        steps.append(tiles(wd, B, 4, 0, row0=g * D, rows=rows, ready=made,
                           dve=add_to_x(st, x_scale=ALPHA if g == 0 else 1.0)))
    return steps


def program(nc, t, out, stop=None):
    ctx = ExitStack()
    st = Store()
    FINISHED.clear()
    CURRENT.clear()

    def sb(name, shape, dt=F32):
        return ctx.enter_context(nc.sbuf_tensor(name, shape, dt))

    with ctx:
        base = -(-nc.sbuf_base // 32) * 32
        st.Bh, st.Bl = sb("Bh", [P, KC, S], F32R), sb("Bl", [P, KC, S], F32R)
        st.spare = nc.alloc_sbuf_tensor_at("spare", [P, 2 * KC, S], F32, offset=base)
        assert nc.sbuf_base >= base + 2 * KC * S * 4
        st.X = sb("X", [P, KC, S])
        st.A = sb("A", [P, 32, S])
        st.raw = sb("raw", [P, 8, S])
        st.Wh, st.Wl = sb("Wh", [P, SLOTS, KC, TW], F32R), sb("Wl", [P, SLOTS, KC, TW], F32R)
        st.Hh, st.Hl = sb("Hh", [P, KC, S], F32R), sb("Hl", [P, KC, S], F32R)
        st.params = sb("params", [P, 8 * P])
        st.squares = sb("squares", [P, len(CONST_SQ), P])
        st.small = sb("small", [P, 16])
        st.cols = sb("cols", [P, 128])
        mod = sb("mod", [P, 64])
        st.heads = sb("heads", [16, 8])
        st.skip = sb("skip", [P, 8])
        st.inv_freq = sb("inv_freq", [P, 1])
        misc = sb("misc", [P, 8])
        st.PS = ctx.enter_context(nc.psum_tensor("PS", [P, 8, S], F32))
        st.mod, st.gain = mod[:, 0:48], mod[:, 48:64]
        st.neg_lam, st.subln = misc[:, 0:1], misc[:, 1:2]
        st.eps = {1e-6: misc[:, 2:3], 1e-5: misc[:, 3:4]}
        st.eps_col = lambda e: st.eps[e]
        st.sq = {n: st.squares[:, k, :] for k, n in enumerate(CONST_SQ)}
        st.ident, st.ones = st.sq["ident"], st.sq["ones"]
        st.raw_slot = lambda s: st.raw[:, 4 * s:4 * s + 4, :].rearrange("p c (h n) -> p (c h) n", h=2)
        st.stage = st.A[:, 28:32, :].rearrange("p (s b) n -> p s b n", s=2)

        A = lambda a, n: chunks(st.A, a, n)
        X = chunks(st.X, 0, KC)
        H, B = (st.Hh, st.Hl), (st.Bh, st.Bl)
        halves = lambda pair: (chunks(pair[0], 0, KC), chunks(pair[1], 0, KC))
        both = (chunks(st.Hh, 0, 8) + chunks(st.Bh, 0, 8), chunks(st.Hl, 0, 8) + chunks(st.Bl, 0, 8))
        pcols = lambda name, n, first=0: [col(st, name, first + c) for c in range(n)]
        mcols = lambda k: [st.mod[:, 8 * k + c:8 * k + c + 1] for c in range(KC)]
        gcols = lambda k: [st.gain[:, 8 * k + c:8 * k + c + 1] for c in range(KC)]
        tokens = lambda a, n: st.A[:, a:a + n, :].rearrange("p (b c) n -> p b (c n)", b=NB)

        def front():
            load = load_part(nc, st, t)
            mod_part = modulation_part(nc, st, t, load.params_out)
            norm1 = norm_part(nc, st, "n1", X, D, 1e-6, gcols(0), mcols(0), split=halves(H), tmp=A(0, 8),
                              scratch=st.A[:, 16:22, :])
            w_in = t["w_in"][0]
            stage(nc, load, mod_part, weights_part(nc, st, "wi", [
                norm1,
                tiles(w_in, H, 4, 0, act=to_chunks(st, 0), ready=norm1.ready),
                tiles(w_in, H, 2, 1024, mode="tokens", act=to_tokens(tokens(8, 4))),
                tiles(w_in, H, 2, 1536, act=to_chunks(st, 12, scale=0.125)),
                tiles(w_in, H, 2, 2048, act=to_chunks(st, 16)),
                tiles(w_in, H, 2, 2560, mode="tokens", act=to_tokens(tokens(20, 4)))]))

        def squared_relu(e, s, acc, i, p):
            return e.scalar_tensor_tensor(s, acc, 0.0, s, ALU.max, ALU.mult)

        def middle():
            mixed = split_part(nc, st, "mx1", A(0, 4) + A(12, 4), *halves(H))
            w_out = tiles(t["w_out"][0], H, 4, 0, dve=add_to_x(st, st.mod[:, 16:24]), ready=mixed.ready)
            norm2 = norm_part(nc, st, "n2", X, D, 1e-6, gcols(1), mcols(3), split=halves(H), tmp=A(0, 8),
                              src_ready=w_out.result_ready)
            ffn = []
            for q in range(FF1 // D):
                up = tiles(t["w_ff1"][0], H, 4, q * D, act=staged_copy(st, ACT.Relu),
                           dve=split_chunks(st, B, squared_relu), ready=None if q else norm2.ready)
                ffn += [up, tiles(t["w_ff2"][0], B, 4, 0, row0=q * D, dve=add_to_x(st, st.mod[:, 40:48]),
                                  ready=up.result_ready)]
            norm3 = norm_part(nc, st, "n3", X, D, 1e-6, pcols("final_norm_g", 8), out=X,
                              src_ready=ffn[-1].all_ready)
            norm4 = norm_part(nc, st, "n4", X, D, 1e-6, pcols("conv_norm_2", 8), split=halves(H), tmp=A(0, 8),
                              src_ready=norm3.out_ready)
            conv_in = conv_module_seg(st, t["conv_w_in_2"][0], H)
            conv_in.ready = norm4.ready
            norm5 = norm_part(nc, st, "n5", A(0, 16), D_INNER, 1e-6, pcols("conv_ln_g_2", 16),
                              pcols("conv_ln_b_2", 16), centre=True, silu=True, times=A(16, 16),
                              split=both, scratch=st.spare[:, 10:16, :])
            conv_out = [tiles(t["conv_w_out_2"][0], rhs, 4, 0, row0=n * D, dve=add_to_x(st),
                              ready=lambda k, n=n: norm5.ready(8 * n + k)) for n, rhs in enumerate((H, B))]
            norm6 = norm_part(nc, st, "n6", X, D, 1e-6, pcols("ret_norm_2", 8), split=halves(H), tmp=A(0, 8),
                              src_ready=conv_out[-1].all_ready)
            rw = t["ret_w_in_2"][0]
            stage(nc, weights_part(nc, st, "mid", [
                mixed, w_out, norm2, *ffn, norm3, norm4, clear_part(conv_in.clear), conv_in, norm5, *conv_out, norm6,
                tiles(rw, H, 4, 0, act=to_chunks(st, 0), ready=norm6.ready),
                tiles(rw, H, 4, 1024, act=to_chunks(st, 8, scale=256 ** -0.5)),
                tiles(rw, H, 8, 2048, mode="tokens", act=to_tokens(tokens(16, 16)))]))

        w3 = t["w_in_3"][0]
        M_QK, M_V = 512, 1024
        at_v, at_o, at_i = 2 * M_QK, 2 * M_QK + M_V, 2 * M_QK + 2 * M_V
        at_z = at_i + 2 * M_HEADS
        at_xbc = at_z + D
        at_dt = at_xbc + 2 * D
        at_ga = at_dt + S_HEADS
        at_gb = at_ga + D

        def rows_to(c, n):
            def act(e, acc, i, p):
                return e.activation(st.A[0:n, c, :], acc[0:n, 0, :], ACT.Copy)
            return act

        def after_retention():
            o = st.A[:, 16:32, :].rearrange("p (b i) n -> p b i n", i=4)

            def gate(e, acc, i, p):
                return e.activation(st.A[:, 2 * p:2 * p + 2, :], acc, ACT.Silu)

            def gated_o(first):
                return lambda i, p: o[:, 2 * p:2 * p + 2, ds(i + first, 1), :].rearrange("p b i n -> p (b i) n")

            def to_parts(e, acc, i, p):
                g = st.A[:, 2 * p:2 * p + 2, :]
                e.tensor_tensor(g, g, gated_o(0)(i, p), ALU.mult)
                e.drain()
                hi = st.Bh[:, ds(i * 4 + 2 * p, 2), :]
                e.tensor_copy(hi, g)
                e.drain()
                return e.tensor_tensor(st.Bl[:, ds(i * 4 + 2 * p, 2), :], g, hi.bitcast(F32), ALU.subtract)

            def to_a(e, acc, i, p):
                return e.tensor_tensor(st.A[:, ds(i * 4 + (8 + 2 * p), 2), :], st.A[:, 2 * p:2 * p + 2, :],
                                       gated_o(2)(i, p), ALU.mult)
            rw, ro = t["ret_w_in_2"][0], t["ret_w_out_2"][0]
            gate0 = tiles(rw, H, 4, 4096, act=gate, dve=to_parts)
            gate1 = tiles(rw, H, 4, 4096 + D, act=gate, dve=to_a)
            second = split_part(nc, st, "rs", A(8, 8), *halves(H))
            out0 = tiles(ro, B, 4, 0, dve=add_to_x(st), ready=gate0.result_ready)
            out1 = tiles(ro, H, 4, 0, row0=D, dve=add_to_x(st), ready=second.ready)
            norm7 = norm_part(nc, st, "n7", X, D, 1e-6, pcols("final_norm_2", 8), out=X, src_ready=out1.all_ready)
            norm8 = norm_part(nc, st, "n8", X, D, 1e-5, pcols("in_ln_g_3", 8), pcols("in_ln_b_3", 8),
                              out=X, split=halves(H), centre=True)
            stage(nc, weights_part(nc, st, "ret_out", [
                gate0, gate1, second, out0, out1, norm7, norm8,
                tiles(w3, H, 1, at_i, width=M_HEADS, act=rows_to(24, M_HEADS), ready=norm8.ready),
                tiles(w3, H, 1, at_i + M_HEADS, width=M_HEADS, act=rows_to(25, M_HEADS)),
                conv_tiles(st, w3, H, 4, 0, 0, "mc", "m_conv_b_3", M_CONV),
                tiles(w3, H, 4, at_v, mode="tokens", act=to_tokens(tokens(8, 8)))]))

        def after_mlstm():
            def times_h(e, s, acc, i, p):
                return e.tensor_tensor(s, s, st.A[:, ds(i * 4 + (16 + 2 * p), 2), :], ALU.mult)

            def gated(e, acc, i, p):
                return e.tensor_tensor(st.A[:, ds(i * 4 + (8 + 2 * p), 2), :], acc,
                                       st.A[:, ds(i * 4 + 2 * p, 2), :], ALU.mult)
            o = tiles(w3, H, 4, at_o, act=staged_copy(st, ACT.Sigmoid), dve=split_chunks(st, B, times_h))
            stage(nc, weights_part(nc, st, "m_out", [
                o,
                tiles(w3, H, 4, at_ga, act=to_chunks(st, 0, ACT.Sigmoid)),
                tiles(t["p_a_3"][0], B, 4, 0, dve=gated, ready=o.result_ready),
                conv_tiles(st, w3, H, 8, at_xbc, 16, "sc", "s_conv_b_3", S_CONV),
                tiles(w3, H, 1, at_dt, width=S_HEADS, act=rows_to(0, S_HEADS))]))

        def after_mamba():
            def times_y(e, acc, i, p):
                y = st.A[:, ds(i * 4 + (16 + 2 * p), 2), :]
                return e.tensor_tensor(y, y, st.stage[:, p, :, :], ALU.mult)

            def merge(e, s, acc, i, p):
                e.tensor_tensor(s, acc, st.A[:, ds(i * 4 + 2 * p, 2), :], ALU.mult)
                e.drain()
                return e.tensor_tensor(s, s, st.A[:, ds(i * 4 + (8 + 2 * p), 2), :], ALU.add)
            z = tiles(w3, H, 4, at_z, act=staged_copy(st, ACT.Silu), dve=times_y)
            y_norm = group_norm_part(nc, st, A(16, 8), pcols("s_norm_g_3", 8), *halves(B), src_ready=z.result_ready)
            p_b = tiles(t["p_b_3"][0], B, 4, 0, dve=split_chunks(st, H, merge), ready=y_norm.ready)
            w_out = tiles(t["w_out_3"][0], H, 4, 0, dve=add_to_x(st, x_scale=ALPHA), ready=p_b.result_ready)
            ln1 = norm_part(nc, st, "l1", X, D, 1e-5, pcols("ln1_g_3", 8), pcols("ln1_b_3", 8),
                            out=X, split=halves(H), centre=True)
            ln2 = norm_part(nc, st, "l2", X, D, 1e-5, pcols("ln2_g_3", 8), pcols("ln2_b_3", 8),
                            out=X, centre=True)
            stage(nc, weights_part(nc, st, "end", [
                z, tiles(w3, H, 4, at_gb, act=to_chunks(st, 0, ACT.Sigmoid)), y_norm,
                p_b, w_out, ln1, *gated_ffn_steps(nc, st, t, H, B, ln1.ready), ln2]))

        for name, build in (
                ("front", front),
                ("rope", lambda: stage(nc, rope_part(nc, st, t))),
                ("diff", lambda: stage(nc, diff_part(nc, st))),
                ("stick", lambda: stage(nc, stick_part(nc, st))),
                ("middle", middle),
                ("rotary", lambda: stage(nc, rotary_part(nc, st, t))),
                ("retention", lambda: stage(nc, retention_part(nc, st, t))),
                ("after_retention", after_retention),
                ("gates", lambda: stage(nc, gates_part(nc, st))),
                ("mlstm", lambda: stage(nc, mlstm_part(nc, st))),
                ("after_mlstm", after_mlstm),
                ("steps", lambda: stage(nc, steps_part(nc, st))),
                ("mamba_x", lambda: stage(nc, mamba_inputs_part(nc, st))),
                ("mamba", lambda: stage(nc, mamba_part(nc, st))),
                ("after_mamba", after_mamba),
                ("store", lambda: stage(nc, store_part(nc, st, out)))):
            build()
            if name == stop:
                break


def kernel(**inputs):
    import concourse.bacc as bacc
    from concourse.bass_utils import run_bass_kernel_spmd

    nc = bacc.Bacc("TRN2", target_bir_lowering=False, num_devices=1)
    arrays, t = {}, {}
    for name, a in {**inputs, **constants()}.items():
        a = np.ascontiguousarray(a)
        arrays[f"in_{name}"] = a
        t[name] = nc.dram_tensor(f"in_{name}", a.shape, mybir.dt.from_np(a.dtype), kind="ExternalInput").ap()
    out = nc.dram_tensor("out", (1, S, D), F32, kind="ExternalOutput").ap()
    program(nc, t, out)
    r = run_bass_kernel_spmd(nc, [arrays], core_ids=[0])
    return r.results[0]["out"]
```

```python
import math
from contextlib import ExitStack, contextmanager

import concourse.bass as bass
import numpy as np
from concourse import mybir

F32 = mybir.dt.float32
F32R = mybir.dt.float32r
I32 = mybir.dt.int32
ALU = mybir.AluOpType
ACT = mybir.ActivationFunctionType
AX_X = mybir.AxisListType.X
ds = bass.ds

P = 128
S = 512
NB = S // P
D = 1024
KC = D // P
TW = 256
SLOTS = 2
MASKED = -1e30

DIFF_W = 512
FF1 = 4096
D_INNER = 2048
CONV_K = 31
RET_HEADS = 4
M_HEADS, M_CONV = 8, 4
S_HEADS, S_GROUPS, S_CONV = 16, 4, 4
FFN3, FFN3_K = 2752, 3
LAMBDA_INIT = 0.8 - 0.6 * math.exp(0.0)
ALPHA = 2.0 ** 0.25

CONST_SQ = ["ident", "ones", "rot", "diff_mask", "strict", "strict_neg", "neg_upper", "neg_ones", "causal_neg"]


def constants():
    f = np.float32
    i = np.arange(P)
    row, col = i[:, None], i[None, :]
    rot = np.zeros((P, P), f)
    for m in range(P):
        b, r = m // 64 * 64, m % 64
        if r < 32:
            rot[b + r + 32, m] = -1.0
        else:
            rot[b + r - 32, m] = 1.0
    sq = {
        "ident": np.eye(P, dtype=f),
        "ones": np.ones((P, P), f),
        "rot": rot,
        "diff_mask": np.where(col // 64 <= row // 64, 0.0, MASKED).astype(f),
        "strict": (row < col).astype(f),
        "strict_neg": np.where(row < col, 0.0, MASKED).astype(f),
        "neg_upper": -(row >= col).astype(f),
        "neg_ones": -np.ones((P, P), f),
        "causal_neg": np.where(row <= col, 0.0, MASKED).astype(f),
    }
    squares = np.concatenate([sq[n] for n in CONST_SQ], 1)
    inv = (1.0 / (f(10000.0) ** (np.arange(0, 64, 2, dtype=f) / f(64)))).astype(f)
    ang = np.arange(S, dtype=f)[None, :] * np.tile(inv, 4)[:, None]
    rope = np.stack([np.cos(ang.astype(np.float64)), np.sin(ang.astype(np.float64))], 1).astype(f)
    decay = np.zeros((P, RET_HEADS, S), f)
    t, s = np.arange(S)[None, :], np.arange(P)[:, None]
    for h in range(RET_HEADS):
        g = np.log(f(1.0) - f(2.0) ** f(-5 - h)).astype(np.float64)
        decay[:, h] = np.where(t >= s, np.exp((t - s) * g), 0.0)
    inv_freq = (f(10000.0) ** (-(np.arange(P, dtype=f)) / f(P))).astype(f)[:, None]
    sel = np.zeros((16, 16, P), f)
    for h in range(16):
        sel[h, h] = 1.0
    return {"squares": squares, "rope": rope, "decay": decay, "inv_freq": inv_freq,
            "sel": sel.reshape(16, 16 * P)}


def _two_pi_parts():
    rest, parts = 2.0 * math.pi, []
    for _ in range(3):
        e = math.floor(math.log2(rest)) - 7
        q = math.floor(rest / 2.0 ** e) * 2.0 ** e
        parts.append(q)
        rest -= q
    return parts + [rest]


TWO_PI = _two_pi_parts()
ROUND = 1.5 * 2.0 ** 23


class Store:
    pass


def col(st, name, c, rows=P):
    return st.params[0:rows, st.col0[name] + c:st.col0[name] + c + 1]


FINISHED, CURRENT = [], []


def sems(nc, ctx, prefix, names):
    made = [ctx.enter_context(nc.semaphore(f"{prefix}_{n}")) for n in names.split()]
    CURRENT.extend(made)
    return made


class Part:

    def __init__(self, ctx):
        self.ctx, self.programs, self.inner = ctx, {}, []

    def sync(self, program):
        self.programs["sync"] = program

    def tensor(self, program):
        self.programs["tensor"] = program

    def scalar(self, program):
        self.programs["scalar"] = program

    def vector(self, program):
        self.programs["vector"] = program

    def gpsimd(self, program):
        self.programs["gpsimd"] = program


def stage(nc, *parts):
    assert not {s.num for s in FINISHED} & {s.num for s in CURRENT}
    with nc.allow_non_contiguous_dma(reason="a few columns of parameters"), nc.Block() as block:
        @block.sync
        def _(sp):
            for s in FINISHED:
                sp.sem_clear(s)

        for part in parts:
            for engine, register in (("sync", block.sync), ("tensor", block.tensor), ("scalar", block.scalar),
                                     ("vector", block.vector), ("gpsimd", block.gpsimd)):
                if engine in part.programs:
                    register(part.programs[engine])
    for part in parts:
        for p in [part] + part.inner:
            p.ctx.close()
    FINISHED[:] = CURRENT
    CURRENT.clear()


def load_parts(nc, st, t):
    ctx = ExitStack()
    (cleared, const_in, rows_in, x_in, turned, params_out, xt_turned, x_out,
     lam_done, c_in, c_act, squares_in) = sems(
        nc, ctx, "ld", "cleared const_in rows_in x_in turned params_out xt_turned x_out lam_done c_in c_act "
                 "squares_in")
    rows = st.A[:, 0:2, :].rearrange("p c (s n) -> p (c s) n", s=4)
    xt = st.A[:, 2:10, :].rearrange("p (b c) n -> p b (c n)", b=NB)
    lam = st.A[:, 10, :].rearrange("p (v n) -> p v n", n=64)

    moves, r, st.col0 = [], 0, {}

    def place(name, vec):
        nonlocal r
        n = vec.shape[0]
        st.col0[name] = r
        full = n // P
        at = 0
        while at < full:
            k = min(full - at, P - r % P)
            moves.append((rows[r % P:r % P + k, r // P, :],
                          vec[at * P:(at + k) * P].rearrange("(r c) -> r c", c=P)))
            r, at = r + k, at + k
        if n % P:
            moves.append((rows[r % P:r % P + 1, r // P, 0:n % P],
                          vec[full * P:n].rearrange("(r c) -> r c", r=1)))
            r += 1

    def flat(ap):
        return ap.rearrange("a b -> (a b)")

    for name in ("ada_b", "mix_norm_g", "ffn_norm_g", "diff_subln_g", "conv_norm_2", "conv_dw_b_2",
                 "conv_ln_g_2", "conv_ln_b_2", "ret_norm_2", "m_conv_b_3", "m_norm_g_3", "s_conv_b_3",
                 "s_norm_g_3", "ln1_g_3", "ln1_b_3", "ln2_g_3", "ln2_b_3"):
        place(name, flat(t[name]))
    for name in ("final_norm_g", "final_norm_2", "in_ln_g_3", "in_ln_b_3"):
        place(name, t[name])
    for k in range(CONV_K):
        place(f"dw{k}", t["conv_dw_w_2"][0, k])
    for k in range(M_CONV):
        place(f"mc{k}", t["m_conv_w_3"][0, k])
    for k in range(S_CONV):
        place(f"sc{k}", t["s_conv_w_3"][0, k])
    for k in range(FFN3_K):
        place(f"fg{k}", t["f_conv_w_3"][0, k, 0:FFN3])
        place(f"fv{k}", t["f_conv_w_3"][0, k, FFN3:2 * FFN3])
    place("fgb", t["f_conv_b_3"][0, 0:FFN3])
    place("fvb", t["f_conv_b_3"][0, FFN3:2 * FFN3])
    n_rows = r
    assert n_rows <= 8 * P
    used = [min(P, n_rows - s * P) for s in range(8)]
    n_const = 11

    part, columns = Part(ctx), Part(ExitStack())
    part.c_act = c_act

    @part.sync
    def _(sp):
        sp.dma_start(xt, t["x"][0].rearrange("(b p) n -> p b n", p=P)).then_inc(x_in, 16)

    @part.scalar
    def _(act):
        act.dma_start(st.small[:, 8:8 + KC], t["c"][0].rearrange("(k p) -> p k", p=P)).then_inc(c_in, 16)
        act.dma_start(st.squares[:, :, :].rearrange("p s n -> p (s n)"), t["squares"]).then_inc(squares_in, 16)
        silu_c = st.small[:, 8:8 + KC]
        act.wait_ge(c_in, 16)
        act.activation(silu_c, silu_c, ACT.Silu).then_inc(c_act, 1)
        for c in range(KC):
            act.wait_ge(xt_turned, c + 1)
            act.activation(st.X[:, c, :], st.PS[:, c % 4, :], ACT.Copy).then_inc(x_out, 1)

    @columns.scalar
    def _(act):
        act.wait_ge(cleared, 1)
        for dst, src in moves:
            act.dma_start(dst, src).then_inc(rows_in, 16)
        for n, name in enumerate(("lambda_q1", "lambda_k1", "lambda_q2", "lambda_k2")):
            act.dma_start(lam[:, n, :], t[name].to_broadcast([P, 64])).then_inc(const_in, 16)
        act.dma_start(st.inv_freq[:, :], t["inv_freq"]).then_inc(const_in, 16)
        for n, (name, h) in enumerate((("m_i_bias_3", M_HEADS), ("m_f_bias_3", M_HEADS),
                                       ("s_dt_bias_3", S_HEADS), ("s_a_log_3", S_HEADS))):
            act.dma_start(st.heads[0:h, n:n + 1], t[name].rearrange("a h -> h a")).then_inc(const_in, 16)
        for half in range(2):
            act.dma_start(st.skip[64 * half:64 * half + 64, :],
                         t["s_d_3"].rearrange("a (c h) -> a h c", h=2)[:, half, :]
                         .to_broadcast([64, 8])).then_inc(const_in, 16)
        act.wait_ge(lam_done, 1)
        act.activation(st.small[:, 2:4], st.small[:, 0:2], ACT.Exp).then_inc(lam_done, 1)

    @part.gpsimd
    def _(pool):
        pool.memset(st.A[:, 0:2, :], 0.0).then_inc(cleared, 1)

    @part.tensor
    def _(pe):
        pe.wait_ge(squares_in, 16)
        pe.wait_ge(x_in, 16)
        for c in range(KC):
            if c >= 4:
                pe.wait_ge(x_out, c - 3)
            for b in range(NB):
                mm = pe.transpose(st.PS[:, c % 4, b * P:(b + 1) * P], xt[:, b, c * P:(c + 1) * P], st.ident)
            mm.then_inc(xt_turned, 1)

    @columns.tensor
    def _(pe):
        pe.wait_ge(rows_in, 16 * len(moves))
        for s in range(8):
            mm = pe.transpose(st.PS[:, 4 + s // 4, (s % 4) * P:(s % 4) * P + used[s]],
                              rows[0:used[s], s, :], st.ident[0:used[s], 0:used[s]])
        mm.then_inc(turned, 1)

    @columns.vector
    def _(dve):
        for e, c in st.eps.items():
            dve.memset(c, e)
        dve.wait_ge(turned, 1)
        n5 = n_rows - 4 * P
        dve.tensor_copy(st.params[:, 0:4 * P], st.PS[:, 4, :])
        dve.tensor_copy(st.params[:, 4 * P:4 * P + n5], st.PS[:, 5, 0:n5]).then_inc(params_out, 1)
        dve.wait_ge(const_in, 16 * n_const)
        dve.tensor_tensor(lam[:, 4, :], lam[:, 0, :], lam[:, 1, :], ALU.mult)
        dve.tensor_tensor(lam[:, 5, :], lam[:, 2, :], lam[:, 3, :], ALU.mult)
        dve.drain()
        dve.tensor_reduce(st.small[:, 0:1], lam[:, 4, :], AX_X, ALU.add)
        dve.tensor_reduce(st.small[:, 1:2], lam[:, 5, :], AX_X, ALU.add).then_inc(lam_done, 1)
        dve.wait_ge(lam_done, 2)
        dve.tensor_tensor(st.small[:, 4:5], st.small[:, 3:4], st.small[:, 2:3], ALU.subtract)
        dve.drain()
        dve.tensor_scalar(st.neg_lam, st.small[:, 4:5], -LAMBDA_INIT, None, ALU.add)
        dve.tensor_scalar(st.subln, col(st, "diff_subln_g", 0), 1.0 - LAMBDA_INIT, None, ALU.mult)
    return part, columns


def modulation_parts(nc, st, t, c_act):
    ctx = ExitStack()
    SLOT = lambda s: st.raw_slot(s) if s < 2 else \
        st.spare[:, 4 * s - 8:4 * s - 4, :].rearrange("p c (h n) -> p (c h) n", h=2)
    N, BY_PE = 6, (3,)
    landed = sems(nc, ctx, "ada", " ".join(f"landed{s}" for s in range(N)))
    free = sems(nc, ctx, "ada", " ".join(f"free{s}" for s in range(N)))
    asked, added, summed = sems(nc, ctx, "ada", "asked added summed")
    n_tiles = 6 * D // TW
    rounds, by_dve = n_tiles // N, N - len(BY_PE)
    silu_c = st.small[:, 8:8 + KC]
    sums = st.A[:, 11:11 + by_dve, :].rearrange("p c (h n) -> p (c h) n", h=2)
    w = t["ada_w"][0].rearrange("(k p) n -> p k n", p=P)
    part, final = Part(ctx), Part(ExitStack())

    @part.sync
    def _(sp):
        with sp.Fori(0, rounds) as i:
            for s in range(N):
                sp.wait_ge(free[s], i + 1)
                sp.sem_inc(asked, 1)
                sp.dma_start(SLOT(s), w[:, :, ds(i * (N * TW) + s * TW, TW)]).then_inc(landed[s], 16)
        for s in range(SLOTS):
            sp.wait_ge(free[s], rounds + 1)

    @part.gpsimd
    def _(pool):
        for s in range(N):
            pool.nop().then_inc(free[s], 1)
        pool.nop().then_inc(summed, by_dve)

    @part.tensor
    def _(pe):
        pe.wait_ge(c_act, 1)
        with pe.Fori(0, rounds) as i:
            for s in range(N):
                column = lambda b: st.PS[:, 6, ds(i * (2 * N) + 2 * s + b, 1)]
                if s in BY_PE:
                    pe.wait_ge(landed[s], i * 16 + 16)
                    for b in range(2):
                        for k in range(KC):
                            mm = pe.matmul(column(b), SLOT(s)[:, k, b * P:(b + 1) * P], silu_c[:, k:k + 1],
                                           start=(k == 0), stop=(k == KC - 1))
                    mm.then_inc(free[s], 1)
                else:
                    n = s - sum(q < s for q in BY_PE)
                    pe.wait_ge(added, i * by_dve + (n + 1))
                    for b in range(2):
                        for odd in range(2):
                            mm = pe.matmul(column(b), sums[:, 2 * n + odd, b * P:(b + 1) * P],
                                           st.ones[:, 0:1], start=(odd == 0), stop=(odd == 1))
                    mm.then_inc(summed, 1)

    @part.vector
    def _(dve):
        dve.wait_ge(c_act, 1)
        with dve.Fori(0, rounds) as i:
            for s in range(N):
                if s in BY_PE:
                    continue
                n = s - sum(q < s for q in BY_PE)
                dve.wait_ge(landed[s], i * 16 + 16)
                dve.wait_ge(summed, i * by_dve + (n + 1))
                for k in range(KC):
                    a = sums[:, 2 * n + k % 2, :]
                    if k < 2:
                        dve.tensor_scalar(a, SLOT(s)[:, k, :], silu_c[:, k:k + 1], None, ALU.mult)
                    else:
                        ins = dve.scalar_tensor_tensor(a, SLOT(s)[:, k, :], silu_c[:, k:k + 1], a,
                                                       ALU.mult, ALU.add)
                    if k % 2 and k < KC - 1:
                        dve.drain()
                dve.drain().then_inc(added, 1)
                dve.sem_inc(free[s], 1)

    @final.vector
    def _(dve):
        for s in BY_PE:
            dve.wait_ge(free[s], rounds + 1)
        dve.wait_ge(summed, by_dve + rounds * by_dve)
        dve.tensor_tensor(st.mod, st.PS[:, 6, 0:48],
                          st.params[:, st.col0["ada_b"]:st.col0["ada_b"] + 48], ALU.add)
        dve.drain()
        for n, name in ((0, "mix_norm_g"), (1, "ffn_norm_g")):
            g = st.params[:, st.col0[name]:st.col0[name] + KC]
            dve.scalar_tensor_tensor(st.gain[:, n * KC:(n + 1) * KC],
                                     st.mod[:, 24 * n + 8:24 * n + 16], 1.0, g, ALU.add, ALU.mult)
    return part, final


def norm_part(nc, st, name, src, width, eps, gain, shift=None, out=None, split=None, centre=False,
              silu=False, times=None, tmp=None, scratch=None, src_ready=None):
    ctx = ExitStack()
    n = len(src)
    column_sum, total, centred, squared, added, rstd_in, scaled, silued, timed, hi_in, lo_in = sems(
        nc, ctx, name, "column_sum total centred squared added rstd scaled silued timed hi lo")
    scratch = st.spare[:, 0:6, :] if scratch is None else scratch
    acc, mean, rstd = (scratch[:, k, :] for k in range(3))
    sq = scratch[:, 3:6, :]
    NSQ = 3
    y = out or tmp or src
    part = Part(ctx)
    part.out_ready = lambda c: (scaled, c + 1)
    part.ready = lambda k: (lo_in, k + 1)

    @part.tensor
    def _(pe):
        for k in range(1 + centre):
            pe.wait_ge(column_sum, k + 1)
            pe.matmul(st.PS[:, 4 + k, :], st.ones, acc, start=True, stop=True).then_inc(total, 1)

    @part.scalar
    def _(act):
        act.drain()
        for c in range(n):
            if centre:
                act.wait_ge(centred, c + 1)
            elif src_ready:
                act.wait_ge(*src_ready(c))
            if c >= NSQ:
                act.wait_ge(added, c - NSQ + 1)
            act.activation(sq[:, c % NSQ, :], src[c], ACT.Square).then_inc(squared, 1)
        act.wait_ge(total, 1 + centre)
        act.activation(mean, st.PS[:, 4 + int(centre), :], ACT.Ln, bias=st.eps_col(eps), scale=1.0 / width)
        act.drain()
        act.activation(rstd, mean, ACT.Exp, scale=-0.5).then_inc(rstd_in, 1)
        for c in range(n):
            if silu:
                act.wait_ge(scaled, c + 1)
                act.activation(y[c], y[c], ACT.Silu, bias=shift[c]).then_inc(silued, 1)
        for c in range(n):
            if split:
                act.wait_ge(timed if times else scaled, c + 1)
                b = shift[c] if shift and not silu and not out else None
                if b is None:
                    act.activation(split[0][c], y[c], ACT.Copy).then_inc(hi_in, 1)
                else:
                    act.activation(split[0][c], y[c], ACT.Identity, bias=b).then_inc(hi_in, 1)

    @part.vector
    def _(dve):
        dve.drain()
        if centre:
            dve.tensor_tensor(acc, src[0], src[1], ALU.add)
            for c in range(2, n):
                dve.drain()
                ins = dve.tensor_tensor(acc, acc, src[c], ALU.add)
            ins.then_inc(column_sum, 1)
            dve.wait_ge(total, 1)
            dve.tensor_scalar(mean, st.PS[:, 4, :], 1.0 / width, None, ALU.mult)
            dve.drain()
            for c in range(n):
                dve.tensor_tensor(src[c], src[c], mean, ALU.subtract).then_inc(centred, 1)
        for c in range(n):
            dve.wait_ge(squared, c + 1)
            if c == 0:
                ins = dve.tensor_copy(acc, sq[:, 0, :])
            else:
                dve.drain()
                ins = dve.tensor_tensor(acc, acc, sq[:, c % NSQ, :], ALU.add)
            ins.then_inc(added, 1)
        dve.drain().then_inc(column_sum, 1)
        dve.wait_ge(rstd_in, 1)
        b_folded = shift and not silu and not out

        def lo(c):
            dve.wait_ge(hi_in, c + 1)
            dve.scalar_tensor_tensor(split[1][c], y[c], shift[c] if b_folded else 0.0,
                                     split[0][c].bitcast(F32), ALU.add, ALU.subtract).then_inc(lo_in, 1)

        LAG = 3
        for c in range(n + LAG):
            if c < n:
                ins = dve.scalar_tensor_tensor(y[c], src[c], gain[c], rstd, ALU.mult, ALU.mult)
                if not (out and shift):
                    ins.then_inc(scaled, 1)
            if out and shift and 2 <= c < n + 2:
                dve.drain()
                dve.tensor_scalar(y[c - 2], y[c - 2], shift[c - 2], None, ALU.add).then_inc(scaled, 1)
            if split and not times and not (out and shift) and c >= LAG:
                lo(c - LAG)
        if times:
            for c in range(n + 1):
                if c < n:
                    dve.wait_ge(silued, c + 1)
                    dve.tensor_tensor(y[c], y[c], times[c], ALU.mult).then_inc(timed, 1)
                if c:
                    dve.drain()
                    lo(c - 1)
        elif split and out and shift:
            dve.drain()
            for c in range(n):
                lo(c)
    return part


def split_part(nc, st, name, src, hi, lo):
    ctx = ExitStack()
    made, hi_in, lo_in = sems(nc, ctx, name, "made hi lo")
    part = Part(ctx)
    part.ready = lambda k: (lo_in, k + 1)

    @part.scalar
    def _(act):
        act.wait_ge(made, 1)
        for c in range(len(src)):
            act.activation(hi[c], src[c], ACT.Copy).then_inc(hi_in, 1)

    @part.vector
    def _(dve):
        dve.drain().then_inc(made, 1)
        for c in range(len(src)):
            dve.wait_ge(hi_in, c + 1)
            dve.tensor_tensor(lo[c], src[c], hi[c].bitcast(F32), ALU.subtract).then_inc(lo_in, 1)
    return part


class Phase:

    def __init__(self, col0, act=None, dve=None, order=None, takes=None, more=None, act_more=None):
        self.col0, self.act, self.dve, self.more, self.act_more = col0, act, dve, more, act_more
        self.order = order or ("act+dve" if act and dve else "act" if act else "dve")
        self.takes = takes
        self.stages = self.order in ("act+dve", "dve+act", "gate")


class Seg:

    def __init__(self, w, rhs, rounds, phases, stride=2 * TW, mode="features", row0=0, rows=D, width=TW, ready=None):
        self.w, self.rhs, self.rounds, self.phases, self.mode = w, rhs, rounds, phases, mode
        self.row0, self.rows, self.stride, self.width, self.ready = row0, rows, stride, width, ready
        self.made_by = self.beside = None
        for p, ph in enumerate(phases):
            if ph.order == "act+dve" and ph.takes is None:
                ph.takes = p

    def posted_at(self, i, p):
        at = [q for q, ph in enumerate(self.phases) if ph.dve]
        return i * len(at) + (self.post0 + at.index(p) + 1)

    def staged_at(self, i, p):
        at = [q for q, ph in enumerate(self.phases) if ph.stages]
        return i * len(at) + (self.stage0 + at.index(p) + 1)

    def result_ready(self, chunk):
        if self.made_by is not None:
            return self.posted, self.posted_at(chunk // 2, self.made_by)
        return self.posted, self.posted_at(chunk // 4, chunk // 2 % 2)

    def act_ready(self, chunk):
        return self.staged, self.staged_at(chunk // 4, chunk // 2 % 2)

    def all_ready(self, _):
        return self.posted, self.posted_at(self.rounds - 1, max(q for q, ph in enumerate(self.phases) if ph.dve))


def tiles(w, rhs, n, col0, act=None, dve=None, **more):
    order = more.pop("order", None)
    if n == 1:
        s = Seg(w, rhs, 1, [Phase(col0, act, dve, order)], **more)
    else:
        s = Seg(w, rhs, n // 2, [Phase(col0 + p * TW, act, dve, order) for p in range(2)], **more)
    return s


def seg_tiles(eng, seg, peel=False):
    q = len(seg.phases)
    if seg.rounds > 1:
        assert q % 2 == 0
        for p in range(q * peel):
            yield seg.base + p, (seg.base + p) // 2, (seg.base + p) % 2, 0, p
        with eng.Fori(int(peel), seg.rounds) as i:
            for p in range(q):
                yield i * q + (seg.base + p), i * (q // 2) + (seg.base + p) // 2, (seg.base + p) % 2, i, p
    else:
        for p in range(q):
            t = seg.base + p
            yield t, t // 2, t % 2, 0, p


def weights_part(nc, st, name, steps):
    ctx = ExitStack()
    landed = sems(nc, ctx, name, "landed0 landed1")
    freed = sems(nc, ctx, name, "acc_free0 acc_free1")
    split_done, multiplied, staged, posted, taken, asked = sems(
        nc, ctx, name, "split_done multiplied staged posted taken asked")
    base = stage0 = post = 0
    landings = [0, 0]
    for g in steps:
        if isinstance(g, Part):
            continue
        g.base, g.stage0, g.post0, g.posted, g.staged = base, stage0, post, posted, staged
        g.landed_before = list(landings)
        for j in range(g.rounds * len(g.phases)):
            landings[(base + j) % 2] += 1 + (g.rows % P > 0)
        base += g.rounds * len(g.phases)
        stage0 += g.rounds * sum(ph.stages for ph in g.phases)
        post += g.rounds * sum(ph.dve is not None for ph in g.phases)

    def kparts(g):
        full, rem = divmod(g.rows, P)
        return [(k, P) for k in range(full)] + ([(full, rem)] if rem else [])

    def acc_of(slot):
        return st.PS[:, 2 * slot:2 * slot + 2, :]

    def landed_value(g, slot, i, p):
        per = 1 + (g.rows % P > 0)
        before = sum((g.base + q) % 2 == slot for q in range(p))
        in_round = sum((g.base + q) % 2 == slot for q in range(len(g.phases)))
        return i * (16 * per * in_round) + 16 * (g.landed_before[slot] + per * (before + 1))

    def run(steps, engine, e, seg_program):
        for g in steps:
            if isinstance(g, Part):
                if engine in g.programs:
                    g.programs[engine](e)
            else:
                seg_program(g)

    part = Part(ctx)
    part.inner = [g for g in steps if isinstance(g, Part)]

    @part.sync
    def _(sp):
        def seg(g):
            full, rem = divmod(g.rows, P)
            body = g.w[g.row0:g.row0 + full * P, :].rearrange("(k p) n -> p k n", p=P)
            for t, turn, slot, i, p in seg_tiles(sp, g):
                sp.wait_ge(split_done, t + 1)
                sp.sem_inc(asked, 1)
                c0 = i * g.stride + g.phases[p].col0
                dst = st.raw_slot(slot)
                sp.dma_start(dst[:, 0:full, 0:g.width], body[:, :, ds(c0, g.width)]).then_inc(landed[slot], 16)
                if rem:
                    sp.dma_start(dst[0:rem, full, 0:g.width],
                                 g.w[g.row0 + full * P:g.row0 + g.rows, ds(c0, g.width)]).then_inc(landed[slot], 16)
        run(steps, "sync", sp, seg)

    @part.vector
    def _(dve):
        def seg(g):
            if not any(ph.dve for ph in g.phases):
                return
            for t, turn, slot, i, p in seg_tiles(dve, g):
                ph = g.phases[p]
                if not ph.dve:
                    continue
                dve.wait_ge(multiplied, t + SLOTS + 1)
                if ph.takes is not None:
                    dve.wait_ge(staged, g.staged_at(i, ph.takes))
                ins = ph.dve(dve, acc_of(slot), i, p)
                ins.then_inc(posted, 1)
                dve.drain().then_inc(freed[slot], 1)
                if ph.more:
                    ph.more(dve, i, p)
        run(steps, "vector", dve, seg)

    @part.gpsimd
    def _(pool):
        pool.nop().then_inc(split_done, SLOTS)

        def seg(g):
            full, rem = divmod(g.rows, P)
            parts = [(P, slice(0, full))] + ([(rem, slice(full, full + 1))] if rem else [])
            for t, turn, slot, i, p in seg_tiles(pool, g, peel=g.beside is not None):
                pool.wait_ge(landed[slot], landed_value(g, slot, i, p))
                pool.wait_ge(multiplied, t + 1)
                pool.sem_inc(taken, 1)
                for rows, k in parts:
                    pool.tensor_scalar(st.Wh[0:rows, slot, k, 0:g.width], st.raw_slot(slot)[0:rows, k, 0:g.width],
                                       1.0, 1.0, ALU.mult, ALU.mult)
                pool.drain()
                for rows, k in parts:
                    ins = pool.tensor_tensor(st.Wl[0:rows, slot, k, 0:g.width],
                                             st.raw_slot(slot)[0:rows, k, 0:g.width],
                                             st.Wh[0:rows, slot, k, 0:g.width].bitcast(F32), ALU.subtract)
                ins.then_inc(split_done, 1)
                if g.beside:
                    g.beside(pool, i, p)
            if g.beside:
                g.beside(pool, g.rounds, 0)
        run(steps, "gpsimd", pool, seg)

    @part.tensor
    def _(pe):
        pe.nop().then_inc(multiplied, SLOTS)

        def seg(g):
            parts = kparts(g)
            for t, turn, slot, i, p in seg_tiles(pe, g):
                pe.wait_ge(split_done, t + SLOTS + 1)
                pe.wait_ge(freed[slot], turn + 1)
                acc = acc_of(slot)
                hi, lo = g.rhs
                wh, wl = st.Wh[:, slot], st.Wl[:, slot]
                blocks = [(b, min(P, g.width - b * P)) for b in range(2) if g.width > b * P] \
                    if g.mode != "tokens" else [(b, TW) for b in range(NB)]
                for b, m in blocks:
                    for k, rows in parts:
                        if g.ready and b == 0:
                            pe.wait_ge(*g.ready(k))
                        for n, (w, x) in enumerate(((wh, hi), (wh, lo), (wl, hi))):
                            if g.mode == "tokens":
                                out = acc[:, b // 2, (b % 2) * TW:(b % 2) * TW + TW]
                                lhs, rhs = x[0:rows, k, b * P:(b + 1) * P], w[0:rows, k, 0:TW]
                            else:
                                out = acc[0:m, b, :]
                                lhs, rhs = w[0:rows, k, b * P:b * P + m], x[0:rows, k, :]
                            mm = pe.matmul(out, lhs, rhs, start=(k == 0 and n == 0),
                                           stop=(k == parts[-1][0] and n == 2))
                mm.then_inc(multiplied, 1)
        run(steps, "tensor", pe, seg)

    @part.scalar
    def _(act):
        for s in range(SLOTS):
            act.nop().then_inc(freed[s], 1)

        def seg(g):
            if not any(ph.act for ph in g.phases):
                return
            for t, turn, slot, i, p in seg_tiles(act, g):
                ph = g.phases[p]
                if not ph.act:
                    if ph.act_more:
                        ph.act_more(act, i, p)
                    continue
                if ph.order == "dve+act":
                    act.wait_ge(posted, g.posted_at(i, p))
                else:
                    act.wait_ge(multiplied, t + SLOTS + 1)
                ins = ph.act(act, acc_of(slot), i, p)
                ins.then_inc(staged if ph.stages else freed[slot], 1)
                if ph.order == "gate":
                    act.drain().then_inc(freed[slot], 1)
                if ph.act_more:
                    ph.act_more(act, i, p)
        run(steps, "scalar", act, seg)
    return part


def to_chunks(st, c0, func=ACT.Copy, scale=1.0, step=4):
    def act(e, acc, i, p):
        return e.activation(st.A[:, ds(i * step + (c0 + 2 * p), 2), :], acc, func, scale=scale)
    return act


def to_tokens(view):
    def act(e, acc, i, p):
        return e.activation(view[:, :, ds(i * (2 * TW) + p * TW, TW)],
                            acc.rearrange("p b (h n) -> p (b h) n", h=2), ACT.Copy)
    return act


def staged_copy(st, func):
    def act(e, acc, i, p):
        return e.activation(st.stage[:, p, :, :], acc, func)
    return act


def split_chunks(st, dst, prod):
    def dve(e, acc, i, p):
        s = st.stage[:, p, :, :]
        prod(e, s, acc, i, p)
        e.drain()
        hi = dst[0][:, ds(i * 4 + 2 * p, 2), :]
        e.tensor_copy(hi, s)
        e.drain()
        return e.tensor_tensor(dst[1][:, ds(i * 4 + 2 * p, 2), :], s, hi.bitcast(F32), ALU.subtract)
    return dve


def add_to_x(st, gate=None, x_scale=1.0):
    def dve(e, acc, i, p):
        for b in range(2):
            x = st.X[:, ds(i * 4 + (2 * p + b), 1), :]
            a = acc[:, b:b + 1, :]
            if gate is not None:
                ins = e.scalar_tensor_tensor(x, a, gate[:, ds(i * 4 + (2 * p + b), 1)], x, ALU.mult, ALU.add)
            else:
                ins = e.scalar_tensor_tensor(x, x, x_scale, a, ALU.mult, ALU.add)
        return ins
    return dve


def chunks(t, a, n):
    return [t[:, a + c, :] for c in range(n)]


def rope_part(nc, st, t):
    ctx = ExitStack()
    tables_in, rotated, by_cos, by_sin, done = sems(nc, ctx, "rope", "tables_in rotated by_cos by_sin done")
    cos, sin = st.spare[:, 0, :], st.spare[:, 1, :]
    part = Part(ctx)
    @part.sync
    def _(sp):
        sp.dma_start(st.spare[:, 0:2, :], t["rope"]).then_inc(tables_in, 16)

    @part.tensor
    def _(pe):
        for c in range(8):
            if c >= 4:
                pe.wait_ge(by_sin, c - 3)
            pe.matmul(st.PS[:, c % 4, :], st.sq["rot"], st.A[:, c, :], start=True, stop=True).then_inc(rotated, 1)

    @part.gpsimd
    def _(pool):
        pool.wait_ge(tables_in, 16)
        for c in range(8):
            pool.wait_ge(rotated, c + 1)
            pool.tensor_tensor(st.A[:, c, :], st.A[:, c, :], cos, ALU.mult).then_inc(by_cos, 1)

    @part.vector
    def _(dve):
        dve.wait_ge(tables_in, 16)
        for c in range(8):
            dve.wait_ge(rotated, c + 1)
            dve.tensor_tensor(st.spare[:, 2 + c % 2, :], st.PS[:, c % 4, :], sin, ALU.mult).then_inc(by_sin, 1)
            dve.wait_ge(by_cos, c + 1)
            dve.wait_ge(by_sin, c + 1)
            dve.tensor_tensor(st.A[:, c, :], st.A[:, c, :], st.spare[:, 2 + c % 2, :], ALU.add).then_inc(done, 1)
            dve.drain()
    return part


def attention_part(nc, st):
    ctx = ExitStack()
    (scored, maxed, exped, weighted, turned, wt_copied, summed, squared, ss_in, rstd_in, head_out) = sems(
        nc, ctx, "diff", "scored maxed exped weighted turned wt_copied summed squared ss rstd head_out")
    z_in, logged, sp_in, suffixed, a_in, pv_done, pair_out = sems(
        nc, ctx, "stick", "z logged softplus suffixed a pv pair_out")
    DH, SH, scale = DIFF_W // P, 8, 64 ** -0.5
    last = DH * NB
    E = lambda n, m: st.A[:, 24 + 2 * (n % 2) + m, :]
    WT = lambda n: st.A[:, 28 + n % 2, :]
    SQ, LN, RSTD = st.A[:, 30, :], st.spare[:, 0, :], st.A[:, 31, :]
    cols = lambda n: st.cols[:, 16 * (n % 2):16 * (n % 2) + 16]
    TURNED, D_OUT, S_OUT = st.PS[:, 5, :], st.PS[:, 6, :], st.PS[:, 7, :]
    SCORES = lambda m: st.PS[:, 3 + m, :]
    AREA = 1280
    START = (0, 512, 1024, 896)
    flat = lambda a: a.rearrange("p c n -> p (c n)")[:, 0:AREA]
    Z, L, SP, AW = flat(st.PS[:, 0:3, :]), flat(st.spare[:, 1:4, :]), flat(st.spare[:, 4:7, :]), flat(st.spare[:, 7:10, :])

    def area(a, b, i=None):
        i = b if i is None else i
        return a[:, START[b] + (i - b) * P:START[b] + (NB - b) * P]

    part = Part(ctx)

    @part.tensor
    def _(pe):
        def scores(n):
            h, qb = divmod(n, NB)
            if n >= 1:
                pe.wait_ge(exped, n)
            for m in range(2):
                mm = pe.matmul(SCORES(m)[:, 0:(qb + 1) * P], st.A[64 * m:64 * m + 64, h, qb * P:(qb + 1) * P],
                               st.A[64 * m:64 * m + 64, 4 + h, 0:(qb + 1) * P], start=True, stop=True)
            mm.then_inc(scored, 1)

        def turn(n):
            h, qb = divmod(n, NB)
            pe.wait_ge(weighted, n + 1)
            if n >= 1:
                pe.wait_ge(wt_copied, n)
            if qb == 1 and h:
                pe.wait_ge(rstd_in, h)
            for kb in range(qb + 1):
                mm = pe.transpose(TURNED[:, kb * P:(kb + 1) * P], E(n, 0)[:, kb * P:(kb + 1) * P], st.ident)
            mm.then_inc(turned, 1)

        def weigh(n):
            h, qb = divmod(n, NB)
            pe.wait_ge(wt_copied, n + 1)
            if qb == 0 and h:
                pe.wait_ge(squared, h)
            for kb in range(qb + 1):
                mm = pe.matmul(D_OUT[:, qb * P:(qb + 1) * P], st.A[:, 8 + kb, h * P:(h + 1) * P],
                               WT(n)[:, kb * P:(kb + 1) * P], start=(kb == 0), stop=(kb == qb))
            if qb == NB - 1:
                mm.then_inc(summed, 1)

        def square_sum(h):
            pe.wait_ge(squared, h + 1)
            pe.wait_ge(wt_copied, min(NB * h + NB + 1, last))
            pe.matmul(TURNED, st.ones, SQ, start=True, stop=True).then_inc(ss_in, 1)

        def logits(h):
            c, half = h // 2, slice(64 * (h % 2), 64 * (h % 2) + 64)
            if h:
                pe.wait_ge(a_in, h)
            for b in range(NB):
                mm = pe.matmul(area(Z, b), st.A[half, 16 + c, b * P:(b + 1) * P], st.A[half, 12 + c, b * P:S],
                               start=(b != 3), stop=True, skip_group_check=True)
            mm.then_inc(z_in, 1)

        def suffix_sums(h):
            pe.wait_ge(sp_in, h + 1)
            for b in range(NB):
                for i in range(b, NB):
                    pe.matmul(area(Z, b, i), st.sq["neg_upper"] if i == b else st.sq["neg_ones"],
                              area(SP, i), start=False, stop=False, skip_group_check=True)
                mm = pe.matmul(area(Z, b)[:, 0:P], st.ident, st.sq["strict_neg"],
                               start=False, stop=True, skip_group_check=True)
            mm.then_inc(suffixed, 1)

        def values(h):
            c, half = h // 2, slice(64 * (h % 2), 64 * (h % 2) + 64)
            if h % 2 == 0 and c:
                pe.wait_ge(pair_out, c)
            pe.wait_ge(a_in, h + 1)
            for b in range(NB):
                mm = pe.matmul(S_OUT[half, b * P:S], st.A[:, 20 + b, h * 64:(h + 1) * 64], area(AW, b),
                               start=(b == 0), stop=(b == NB - 1), skip_group_check=True)
            mm.then_inc(pv_done, 1)

        for h in range(SH):
            logits(h)
            if h:
                values(h - 1)
                turn(2 * h - 1)
            scores(2 * h)
            if h:
                weigh(2 * h - 1)
            suffix_sums(h)
            turn(2 * h)
            scores(2 * h + 1)
            weigh(2 * h)
            if h and h % 2 == 0:
                square_sum(h // 2 - 1)
        values(SH - 1)
        turn(last - 1)
        weigh(last - 1)
        square_sum(DH - 1)

    @part.scalar
    def _(act):
        def softplus(h):
            act.wait_ge(z_in, h + 1)
            if h:
                act.wait_ge(sp_in, h)
            act.activation(L, Z, ACT.Abs)
            act.drain()
            act.activation(L, L, ACT.Exp, scale=-1.0)
            act.drain()
            act.activation(L, L, ACT.Ln, bias=1.0).then_inc(logged, 1)

        def attend(h):
            act.wait_ge(suffixed, h + 1)
            if h:
                act.wait_ge(pv_done, h)
            act.activation(AW, Z, ACT.Exp).then_inc(a_in, 1)

        def copy_pair(c):
            act.wait_ge(pv_done, 2 * c + 2)
            act.activation(st.A[:, 12 + c, :], S_OUT, ACT.Copy).then_inc(pair_out, 1)

        def exps(n):
            w = (n % NB + 1) * P
            act.wait_ge(maxed, n + 1)
            if n >= 2:
                act.wait_ge(turned, n - 1)
            for m in range(2):
                act.activation(E(n, m)[:, 0:w], SCORES(m)[:, 0:w], ACT.Exp, bias=cols(n)[:, 2 + m:3 + m],
                               scale=scale, accum_out=cols(n)[:, 4 + m:5 + m])
            act.drain().then_inc(exped, 1)

        def copy_wt(n):
            act.wait_ge(turned, n + 1)
            w = (n % NB + 1) * P
            act.activation(WT(n)[:, 0:w], TURNED[:, 0:w], ACT.Copy).then_inc(wt_copied, 1)

        def head_square(h):
            act.wait_ge(summed, h + 1)
            act.activation(SQ, D_OUT, ACT.Square)
            act.activation(st.A[:, h, :], D_OUT, ACT.Copy)
            act.drain().then_inc(squared, 1)

        def head_rstd(h):
            act.wait_ge(ss_in, h + 1)
            act.activation(LN, TURNED, ACT.Ln, bias=st.eps_col(1e-6), scale=1.0 / P)
            act.drain()
            if h >= 1:
                act.wait_ge(head_out, h)
            act.activation(RSTD, LN, ACT.Exp, scale=-0.5).then_inc(rstd_in, 1)

        for h in range(SH):
            softplus(h)
            if h:
                copy_wt(2 * h - 1)
                if h % 2 == 0:
                    head_square(h // 2 - 1)
            exps(2 * h)
            if h and h % 2 == 0:
                copy_pair(h // 2 - 1)
            attend(h)
            copy_wt(2 * h)
            exps(2 * h + 1)
            if h and h % 2 == 0:
                head_rstd(h // 2 - 1)
        copy_wt(last - 1)
        head_square(DH - 1)
        copy_pair(SH // 2 - 1)
        head_rstd(DH - 1)

    @part.vector
    def _(dve):
        def add_max(h):
            dve.wait_ge(logged, h + 1)
            if h:
                dve.wait_ge(suffixed, h)
            dve.scalar_tensor_tensor(SP, Z, 0.0, L, ALU.max, ALU.add)
            dve.drain()
            for b in range(NB):
                ins = dve.tensor_tensor(area(SP, b)[:, 0:P], area(SP, b)[:, 0:P], st.sq["strict"], ALU.mult)
            dve.drain().then_inc(sp_in, 1)

        def maxima(n):
            dve.wait_ge(scored, n + 1)
            w = (n % NB + 1) * P
            for m in range(2):
                dve.tensor_tensor(SCORES(m)[:, w - P:w], SCORES(m)[:, w - P:w], st.sq["diff_mask"], ALU.add)
            dve.drain()
            dve.tensor_reduce(cols(n)[:, 0:2], st.PS[:, 3:5, 0:w], AX_X, ALU.max)
            dve.drain()
            dve.tensor_scalar(cols(n)[:, 2:4], cols(n)[:, 0:2], -scale, None, ALU.mult).then_inc(maxed, 1)

        def weights(n):
            dve.wait_ge(exped, n + 1)
            w = (n % NB + 1) * P
            dve.reciprocal(cols(n)[:, 6:8], cols(n)[:, 4:6])
            dve.drain()
            dve.tensor_scalar(E(n, 0)[:, 0:w], E(n, 0)[:, 0:w], cols(n)[:, 6:7], None, ALU.mult)
            dve.tensor_scalar(cols(n)[:, 8:9], cols(n)[:, 7:8], st.neg_lam, None, ALU.mult)
            dve.drain()
            dve.scalar_tensor_tensor(E(n, 0)[:, 0:w], E(n, 1)[:, 0:w], cols(n)[:, 8:9], E(n, 0)[:, 0:w],
                                     ALU.mult, ALU.add).then_inc(weighted, 1)

        def head_norm(h):
            dve.wait_ge(rstd_in, h + 1)
            dve.scalar_tensor_tensor(st.A[:, h, :], st.A[:, h, :], st.subln, RSTD,
                                     ALU.mult, ALU.mult).then_inc(head_out, 1)

        for h in range(SH):
            maxima(2 * h)
            add_max(h)
            weights(2 * h)
            maxima(2 * h + 1)
            weights(2 * h + 1)
            if h and h % 2 == 0:
                head_norm(h // 2 - 1)
        head_norm(DH - 1)
    return part


def rotary_parts(nc, st, t, memory_free, chunk_ready):
    ctx = ExitStack()
    pos_in, angled, sine = sems(nc, ctx, "rotary", "pos angled sine")
    R = lambda n: st.spare[:, n, :]
    posi, ang, turns = st.A[:, 16, :].bitcast(I32), st.A[:, 17, :], st.A[:, 18, :]
    sin, half_sin, cos = R(6), R(7), R(8)
    tables, sines, turn = Part(ctx), Part(ExitStack()), Part(ExitStack())

    @tables.sync
    def _(sp):
        sp.wait_ge(*memory_free)
        sp.dma_start(posi, t["positions_2"].to_broadcast([P, S])).then_inc(pos_in, 16)

    @sines.scalar
    def _(act):
        act.wait_ge(angled, 1)
        act.activation(sin, ang, ACT.Sin)
        act.activation(half_sin, ang, ACT.Sin, scale=0.5).then_inc(sine, 1)

    @tables.vector
    def _(dve):
        dve.wait_ge(pos_in, 16)
        dve.tensor_copy(turns, posi)
        dve.drain()
        dve.tensor_scalar(ang, turns, st.inv_freq[:, 0:1], None, ALU.mult)
        dve.drain()
        dve.tensor_scalar(turns, ang, 1.0 / (2.0 * math.pi), ROUND, ALU.mult, ALU.add)
        dve.drain()
        dve.tensor_scalar(turns, turns, -ROUND, None, ALU.add)
        for part in TWO_PI:
            dve.drain()
            dve.scalar_tensor_tensor(ang, turns, -part, ang, ALU.mult, ALU.add)
        dve.drain()
        dve.tensor_scalar(ang, ang, 3.1415925, -3.1415925, ALU.min, ALU.max).then_inc(angled, 1)

    @turn.vector
    def _(dve):
        dve.wait_ge(sine, 1)
        dve.tensor_tensor(cos, half_sin, half_sin, ALU.mult)
        dve.drain()
        dve.tensor_scalar(cos, cos, -2.0, 1.0, ALU.mult, ALU.add)
        dve.drain()
        for n in range(8):
            x1, x2 = st.A[:, 2 * n, :], st.A[:, 2 * n + 1, :]
            dve.wait_ge(*chunk_ready(2 * n + 1))
            dve.tensor_tensor(R(0), x1, cos, ALU.mult)
            dve.tensor_tensor(R(1), x2, sin, ALU.mult)
            dve.tensor_tensor(R(2), x1, sin, ALU.mult)
            dve.tensor_tensor(R(3), x2, cos, ALU.mult)
            dve.drain()
            dve.tensor_tensor(x1, R(0), R(1), ALU.subtract)
            dve.tensor_tensor(x2, R(2), R(3), ALU.add)
            dve.drain()
    return tables, sines, turn


def retention_part(nc, st, t):
    ctx = ExitStack()
    decay_in, scored, decayed, pv_done, copied, squared, ss_in, rstd_in, normed = sems(
        nc, ctx, "ret", "decay scored decayed pv copied squared ss rstd normed")
    Dm = lambda h: st.spare[:, h, :]
    W = lambda b: st.spare[:, 4 + b, :]
    SQ = lambda h: [st.A[:, c, :] for c in (2 * h, 2 * h + 1, 8 + 2 * h, 9 + 2 * h)]
    part = Part(ctx)
    @part.sync
    def _(sp):
        sp.dma_start(st.spare[:, 0:4, :], t["decay"]).then_inc(decay_in, 16)

    @part.tensor
    def _(pe):
        for h in range(RET_HEADS):
            for b in range(NB):
                n = NB * h + b
                if n >= 2:
                    pe.wait_ge(decayed, n - 1)
                for d in range(2):
                    mm = pe.matmul(st.PS[:, n % 2, 0:S - b * P], st.A[:, 8 + 2 * h + d, b * P:(b + 1) * P],
                                   st.A[:, 2 * h + d, b * P:S], start=(d == 0), stop=(d == 1))
                mm.then_inc(scored, 1)
            pe.wait_ge(decayed, NB * (h + 1))
            if h:
                pe.wait_ge(copied, NB * h)
            for e in range(4):
                for b in range(NB):
                    mm = pe.matmul(st.PS[:, 2 + e, b * P:S], st.A[:, 16 + 4 * b + h, e * P:(e + 1) * P],
                                   W(b)[:, 0:S - b * P], start=(b == 0), stop=(b == NB - 1), skip_group_check=True)
            mm.then_inc(pv_done, 1)
            pe.wait_ge(squared, 4 * (h + 1))
            for e in range(4):
                mm = pe.matmul(st.PS[:, 6, :], st.ones, SQ(h)[e], start=(e == 0), stop=(e == 3))
            mm.then_inc(ss_in, 1)

    @part.scalar
    def _(act):
        for h in range(RET_HEADS):
            act.wait_ge(pv_done, h + 1)
            for e in range(4):
                act.activation(SQ(h)[e], st.PS[:, 2 + e, :], ACT.Square).then_inc(squared, 1)
            for e in range(4):
                act.activation(st.A[:, 16 + 4 * e + h, :], st.PS[:, 2 + e, :], ACT.Copy).then_inc(copied, 1)
            act.wait_ge(ss_in, h + 1)
            act.activation(SQ(h)[0], st.PS[:, 6, :], ACT.Ln, bias=st.eps_col(1e-6), scale=1.0 / 512)
            act.drain()
            act.activation(SQ(h)[1], SQ(h)[0], ACT.Exp, scale=-0.5).then_inc(rstd_in, 1)

    @part.vector
    def _(dve):
        dve.wait_ge(decay_in, 16)

        def norm(h):
            dve.wait_ge(rstd_in, h + 1)
            for e in range(4):
                o = st.A[:, 16 + 4 * e + h, :]
                dve.tensor_tensor(o, o, SQ(h)[1], ALU.mult).then_inc(normed, 1)

        for h in range(RET_HEADS):
            for b in range(NB):
                n = NB * h + b
                dve.wait_ge(scored, n + 1)
                if h:
                    dve.wait_ge(pv_done, h)
                dve.tensor_tensor(W(b)[:, 0:S - b * P], st.PS[:, n % 2, 0:S - b * P],
                                  Dm(h)[:, 0:S - b * P], ALU.mult).then_inc(decayed, 1)
            if h:
                norm(h - 1)
        norm(RET_HEADS - 1)
    return part


def gates_part(nc, st):
    ctx = ExitStack()
    biased, logged, scanned, turned, m_ready, floor_in = sems(nc, ctx, "gates", "biased logged scanned turned m floor")
    hs = slice(0, M_HEADS)
    g_i, g_f, t1, t2, F, negM, floor, one = (st.A[hs, c, :] for c in range(24, 32))
    part = Part(ctx)
    @part.vector
    def _(dve):
        dve.memset(one, 1.0)
        dve.tensor_scalar(g_i, g_i, st.heads[hs, 0:1], None, ALU.add)
        dve.tensor_scalar(g_f, g_f, st.heads[hs, 1:2], None, ALU.add).then_inc(biased, 1)
        dve.wait_ge(logged, 1)
        dve.drain()
        dve.scalar_tensor_tensor(t2, g_f, 0.0, t1, ALU.min, ALU.subtract)
        dve.drain()
        dve.tensor_tensor_scan(F, one, t2, 0.0, ALU.mult, ALU.add)
        dve.drain()
        dve.tensor_tensor(g_i, g_i, F, ALU.subtract).then_inc(scanned, 1)
        dve.drain()
        dve.tensor_tensor_scan(t1, g_i, g_i, MASKED, ALU.max, ALU.max)
        dve.drain()
        dve.tensor_scalar(negM, t1, -1.0, None, ALU.mult)
        dve.tensor_tensor(t2, F, t1, ALU.add).then_inc(m_ready, 1)
        dve.wait_ge(turned, 1)
        dve.tensor_copy(st.cols[:, 0:16 * NB].rearrange("p (b h) -> p b h", b=NB)[:, :, hs],
                        st.PS[:, 0, 0:NB * M_HEADS].rearrange("p (b h) -> p b h", b=NB))

    @part.scalar
    def _(act):
        act.wait_ge(biased, 1)
        act.activation(t1, g_f, ACT.Abs)
        act.drain()
        act.activation(t1, t1, ACT.Exp, scale=-1.0)
        act.drain()
        act.activation(t1, t1, ACT.Ln, bias=1.0).then_inc(logged, 1)
        act.wait_ge(m_ready, 1)
        act.activation(floor, t2, ACT.Exp, scale=-1.0).then_inc(floor_in, 1)

    @part.tensor
    def _(pe):
        pe.wait_ge(scanned, 1)
        for b in range(NB):
            mm = pe.transpose(st.PS[:, 0, b * M_HEADS:(b + 1) * M_HEADS], g_i[:, b * P:(b + 1) * P],
                              st.ident[hs, hs])
        mm.then_inc(turned, 1)
    return part


def mlstm_part(nc, st):
    ctx = ExitStack()
    (scored, spread, exped, weighted, pv_done, floor_in, absed, divided, squared, ss_in, rstd_in, head_out) = sems(
        nc, ctx, "ml", "scored spread exped weighted pv floor absed divided squared ss rstd head_out")
    V = st.A[:, 8:16, :].rearrange("p (b c) n -> p b (c n)", b=NB)
    W = lambda b: st.spare[:, 4 + b, :]
    negM, floor = st.A[0:M_HEADS, 29, :], st.A[0:M_HEADS, 30, :]
    R, T, SQ, LN = (st.A[:, c, :] for c in (25, 26, 27, 31))
    at = lambda b: slice(b * P, S)
    pick = lambda h: st.ident[0:M_HEADS, h:h + 1].to_broadcast([M_HEADS, P])

    part = Part(ctx)
    @part.tensor
    def _(pe):
        def square_sum(h):
            pe.wait_ge(squared, h + 1)
            pe.matmul(st.PS[:, 7, :], st.ones, SQ, start=True, stop=True).then_inc(ss_in, 1)

        for h in range(M_HEADS):
            c, half = h // 2, slice(64 * (h % 2), 64 * (h % 2) + 64)
            for b in range(NB):
                n = NB * h + b
                if n >= 2:
                    pe.wait_ge(weighted, n - 1)
                pe.matmul(st.PS[:, n % 2, at(b)], st.A[half, 4 + c, b * P:(b + 1) * P],
                          st.A[half, c, at(b)], start=True, stop=True).then_inc(scored, 1)
                pe.matmul(st.PS[:, 2 + n % 2, at(b)], pick(h), negM[:, at(b)], start=True, stop=False,
                          skip_group_check=True)
                pe.matmul(st.PS[:, 2 + n % 2, b * P:(b + 1) * P], st.ident, st.sq["causal_neg"],
                          start=False, stop=True, skip_group_check=True).then_inc(spread, 1)
            if h:
                pe.wait_ge(divided, h)
            pe.matmul(st.PS[:, 6, :], pick(h), floor, start=True, stop=True).then_inc(floor_in, 1)
            for b in range(NB):
                pe.wait_ge(weighted, NB * h + b + 1)
                pe.matmul(st.PS[:, 4, at(b)], V[:, b, h * P:(h + 1) * P], W(b)[:, at(b)], start=(b == 0),
                          stop=(b == NB - 1), skip_group_check=True)
                mm = pe.matmul(st.PS[:, 5, at(b)], st.ones, W(b)[:, at(b)], start=(b == 0),
                               stop=(b == NB - 1), skip_group_check=True)
            mm.then_inc(pv_done, 1)
            if h:
                square_sum(h - 1)
        square_sum(M_HEADS - 1)

    @part.scalar
    def _(act):
        def tail(h):
            act.wait_ge(divided, h + 1)
            act.activation(SQ, st.A[:, 16 + h, :], ACT.Square).then_inc(squared, 1)

        def tail2(h):
            act.wait_ge(ss_in, h + 1)
            act.activation(LN, st.PS[:, 7, :], ACT.Ln, bias=st.eps_col(1e-6), scale=1.0 / P)
            act.drain()
            if h:
                act.wait_ge(head_out, h)
            act.activation(R, LN, ACT.Exp, scale=-0.5).then_inc(rstd_in, 1)

        for h in range(M_HEADS):
            for b in range(NB):
                act.wait_ge(spread, NB * h + b + 1)
                if h:
                    act.wait_ge(pv_done, h)
                act.activation(W(b)[:, at(b)], st.PS[:, 2 + (NB * h + b) % 2, at(b)], ACT.Exp,
                               bias=st.cols[:, 16 * b + h:16 * b + h + 1]).then_inc(exped, 1)
                if b == 1 and h:
                    tail(h - 1)
            act.wait_ge(pv_done, h + 1)
            if h:
                act.wait_ge(divided, h)
            act.activation(T, st.PS[:, 5, :], ACT.Abs).then_inc(absed, 1)
            if h:
                tail2(h - 1)
        tail(M_HEADS - 1)
        tail2(M_HEADS - 1)

    @part.vector
    def _(dve):
        def norm(h):
            dve.wait_ge(rstd_in, h + 1)
            o = st.A[:, 16 + h, :]
            dve.scalar_tensor_tensor(o, o, col(st, "m_norm_g_3", h), R, ALU.mult, ALU.mult).then_inc(head_out, 1)

        for h in range(M_HEADS):
            for b in range(NB):
                n = NB * h + b
                dve.wait_ge(scored, n + 1)
                dve.wait_ge(exped, n + 1)
                dve.scalar_tensor_tensor(W(b)[:, at(b)], st.PS[:, n % 2, at(b)], 0.125, W(b)[:, at(b)],
                                         ALU.mult, ALU.mult).then_inc(weighted, 1)
            dve.wait_ge(floor_in, h + 1)
            dve.wait_ge(absed, h + 1)
            dve.tensor_tensor(T, T, st.PS[:, 6, :], ALU.max)
            dve.drain()
            dve.reciprocal(T, T)
            dve.drain()
            dve.tensor_tensor(st.A[:, 16 + h, :], st.PS[:, 4, :], T, ALU.mult).then_inc(divided, 1)
            if h:
                norm(h - 1)
        dve.drain()
        norm(M_HEADS - 1)
    return part


CUMSUM_AT = [(1, 0), (2, 0), (3, 0), (2, 3 * P)]


def steps_part(nc, st):
    ctx = ExitStack()
    biased, logged, rate_in, dt_in, summed, turned = sems(nc, ctx, "steps", "biased logged rate dt summed turned")
    hs = slice(0, S_HEADS)
    y, t1, one, dt, a = (st.A[hs, c, :] for c in range(5))
    part = Part(ctx)
    @part.vector
    def _(dve):
        dve.memset(one, 1.0)
        dve.tensor_scalar(y, y, st.heads[hs, 2:3], None, ALU.add).then_inc(biased, 1)
        dve.wait_ge(logged, 1)
        dve.drain()
        dve.scalar_tensor_tensor(dt, y, 0.0, t1, ALU.max, ALU.add).then_inc(dt_in, 1)
        dve.wait_ge(rate_in, 1)
        dve.drain()
        dve.tensor_scalar(a, dt, st.heads[hs, 4:5], -1.0, ALU.mult, ALU.mult)
        dve.drain()
        for b, (c, at) in enumerate(CUMSUM_AT):
            n = S - b * P
            dve.tensor_tensor_scan(st.spare[hs, c, at:at + n], one[:, 0:n], a[:, b * P:S], 0.0, ALU.mult, ALU.add)
        dve.drain().then_inc(summed, 1)
        dve.wait_ge(turned, 1)
        dve.tensor_scalar(st.cols[:, 0:64], st.PS[:, 0, 0:64], -1.0, None, ALU.mult)
        dve.tensor_copy(st.cols[:, 64:128], st.PS[:, 1, 0:64])

    @part.scalar
    def _(act):
        act.activation(st.heads[hs, 4:5], st.heads[hs, 3:4], ACT.Exp).then_inc(rate_in, 1)
        act.wait_ge(biased, 1)
        act.activation(t1, y, ACT.Abs)
        act.drain()
        act.activation(t1, t1, ACT.Exp, scale=-1.0)
        act.drain()
        act.activation(t1, t1, ACT.Ln, bias=1.0).then_inc(logged, 1)

    @part.tensor
    def _(pe):
        pe.wait_ge(dt_in, 1)
        pe.wait_ge(summed, 1)
        for b, (c, at) in enumerate(CUMSUM_AT):
            pe.transpose(st.PS[:, 0, 16 * b:16 * b + 16], st.spare[hs, c, at:at + P], st.ident[hs, hs])
            mm = pe.transpose(st.PS[:, 1, 16 * b:16 * b + 16], dt[:, b * P:(b + 1) * P], st.ident[hs, hs])
        mm.then_inc(turned, 1)
    return part


def mamba_inputs_part(nc, st):
    ctx = ExitStack()
    turned, scaled = sems(nc, ctx, "mx", "turned scaled")
    XT = st.A[:, 0:8, :].rearrange("p (b c) n -> p b (c n)", b=NB)
    part = Part(ctx)
    @part.tensor
    def _(pe):
        for c in range(8):
            if c >= 4:
                pe.wait_ge(scaled, c - 3)
            for b in range(NB):
                mm = pe.transpose(st.PS[:, c % 4, b * P:(b + 1) * P], st.A[:, 16 + c, b * P:(b + 1) * P], st.ident)
            mm.then_inc(turned, 1)

    @part.vector
    def _(dve):
        for c in range(8):
            dve.wait_ge(turned, c + 1)
            for b in range(NB):
                for r in range(2):
                    h = 2 * c + r
                    ins = dve.tensor_scalar(XT[:, b, h * 64:(h + 1) * 64],
                                            st.PS[:, c % 4, b * P + 64 * r:b * P + 64 * r + 64],
                                            st.cols[:, 64 + 16 * b + h:65 + 16 * b + h], None, ALU.mult)
            ins.then_inc(scaled, 1)
    return part


def mamba_part(nc, st):
    ctx = ExitStack()
    cb_in, spread, exped, weighted, pv_done, pair_out = sems(nc, ctx, "mb", "cb spread exped weighted pv pair_out")
    XT = st.A[:, 0:8, :].rearrange("p (b c) n -> p b (c n)", b=NB)
    W = lambda b: st.spare[:, 4 + b, :]
    at = lambda b: slice(b * P, S)
    R = S_HEADS // S_GROUPS
    pick = lambda h: st.ident[0:S_HEADS, h:h + 1].to_broadcast([S_HEADS, P])
    part = Part(ctx)
    @part.tensor
    def _(pe):
        for h in range(S_HEADS):
            g, c, half = h // R, h // 2, slice(64 * (h % 2), 64 * (h % 2) + 64)
            if h % R == 0:
                for b in range(NB):
                    if g:
                        pe.wait_ge(weighted, NB * h)
                    pe.matmul(st.PS[:, b, at(b)], st.A[:, 24 + g, b * P:(b + 1) * P], st.A[:, 28 + g, at(b)],
                              start=True, stop=True).then_inc(cb_in, 1)
            for b in range(NB):
                n = NB * h + b
                if n >= 2:
                    pe.wait_ge(exped, n - 1)
                k, c0 = CUMSUM_AT[b]
                pe.matmul(st.PS[:, 4 + n % 2, at(b)], pick(h), st.spare[0:S_HEADS, k, c0:c0 + S - b * P],
                          start=True, stop=False, skip_group_check=True)
                pe.matmul(st.PS[:, 4 + n % 2, b * P:(b + 1) * P], st.ident, st.sq["causal_neg"],
                          start=False, stop=True, skip_group_check=True).then_inc(spread, 1)
            if h % 2 == 0 and c >= 2:
                pe.wait_ge(pair_out, c - 1)
            for b in range(NB):
                pe.wait_ge(weighted, NB * h + b + 1)
                mm = pe.matmul(st.PS[half, 6 + c % 2, at(b)], XT[:, b, h * 64:(h + 1) * 64], W(b)[:, at(b)],
                               start=(b == 0), stop=(b == NB - 1), skip_group_check=True)
            mm.then_inc(pv_done, 1)

    @part.scalar
    def _(act):
        for h in range(S_HEADS):
            for b in range(NB):
                n = NB * h + b
                act.wait_ge(spread, n + 1)
                if h:
                    act.wait_ge(pv_done, h)
                act.activation(W(b)[:, at(b)], st.PS[:, 4 + n % 2, at(b)], ACT.Exp,
                               bias=st.cols[:, 16 * b + h:16 * b + h + 1]).then_inc(exped, 1)

    @part.vector
    def _(dve):
        for h in range(S_HEADS):
            for b in range(NB):
                n = NB * h + b
                dve.wait_ge(cb_in, NB * (h // R) + b + 1)
                dve.wait_ge(exped, n + 1)
                dve.tensor_tensor(W(b)[:, at(b)], W(b)[:, at(b)], st.PS[:, b, at(b)], ALU.mult).then_inc(weighted, 1)
            if h % 2:
                c = h // 2
                dve.wait_ge(pv_done, h + 1)
                dve.scalar_tensor_tensor(st.A[:, 16 + c, :], st.A[:, 16 + c, :], st.skip[:, c:c + 1],
                                         st.PS[:, 6 + c % 2, :], ALU.mult, ALU.add).then_inc(pair_out, 1)
    return part


def group_norm_part(nc, st, src, gain, hi, lo, src_ready):
    ctx = ExitStack()
    squared, ss_in, rstd_in, scaled, hi_in, done = sems(nc, ctx, "gn", "squared ss rstd scaled hi done")
    SQ = lambda c: st.spare[:, 8 + c, :]
    part = Part(ctx)
    part.ready = lambda k: (done, k + 1)

    @part.tensor
    def _(pe):
        for g in range(S_GROUPS):
            pe.wait_ge(squared, 2 * g + 2)
            pe.matmul(st.PS[:, 4 + g, :], st.ones, SQ(2 * g), start=True, stop=False)
            pe.matmul(st.PS[:, 4 + g, :], st.ones, SQ(2 * g + 1), start=False, stop=True).then_inc(ss_in, 1)

    @part.scalar
    def _(act):
        for c in range(8):
            act.wait_ge(*src_ready(c))
            act.activation(SQ(c), src[c], ACT.Square).then_inc(squared, 1)
        for g in range(S_GROUPS):
            act.wait_ge(ss_in, g + 1)
            act.activation(SQ(2 * g), st.PS[:, 4 + g, :], ACT.Ln, bias=st.eps_col(1e-6), scale=1.0 / (2 * P))
        act.drain()
        for g in range(S_GROUPS):
            act.activation(SQ(2 * g), SQ(2 * g), ACT.Exp, scale=-0.5).then_inc(rstd_in, 1)
        for c in range(8):
            act.wait_ge(scaled, c + 1)
            act.activation(hi[c], src[c], ACT.Copy).then_inc(hi_in, 1)

    @part.vector
    def _(dve):
        dve.drain()
        for c in range(8):
            dve.wait_ge(rstd_in, c // 2 + 1)
            dve.scalar_tensor_tensor(src[c], src[c], gain[c], SQ(c // 2 * 2), ALU.mult, ALU.mult).then_inc(scaled, 1)
        dve.drain()
        for c in range(8):
            dve.wait_ge(hi_in, c + 1)
            dve.tensor_tensor(lo[c], src[c], hi[c].bitcast(F32), ALU.subtract).then_inc(done, 1)
    return part


def store_part(nc, st, out):
    ctx = ExitStack()
    turned, copied, stored = sems(nc, ctx, "out", "turned copied stored")
    Y = st.A[:, 0:8, :].rearrange("p (b c) n -> p b (c n)", b=NB)
    part = Part(ctx)
    @part.tensor
    def _(pe):
        for b in range(NB):
            for c in range(KC):
                mm = pe.transpose(st.PS[:, 2 * b + c // 4, (c % 4) * P:(c % 4 + 1) * P],
                                  st.X[:, c, b * P:(b + 1) * P], st.ident)
            mm.then_inc(turned, 1)

    @part.scalar
    def _(act):
        for b in range(0, NB, 2):
            act.wait_ge(turned, b + 1)
            act.activation(Y[:, b, :].rearrange("p (c n) -> p c n", c=2), st.PS[:, 2 * b:2 * b + 2, :],
                           ACT.Copy).then_inc(copied, 1)

    @part.vector
    def _(dve):
        for b in range(1, NB, 2):
            dve.wait_ge(turned, b + 1)
            dve.tensor_copy(Y[:, b, :].rearrange("p (c n) -> p c n", c=2), st.PS[:, 2 * b:2 * b + 2, :]).then_inc(copied, 1)

    @part.sync
    def _(sp):
        for pair in range(2):
            sp.wait_ge(copied, 2 * pair + 2) if pair else sp.wait_ge(copied, NB)
            sp.dma_start(out[0].rearrange("(b p) n -> p b n", p=P)[:, 2 * pair:2 * pair + 2, :],
                         Y[:, 2 * pair:2 * pair + 2, :]).then_inc(stored, 16)
        sp.wait_ge(stored, 32)
    return part


def short_conv(st, e, out, acc, taps, weight, rows):
    for back in range(taps):
        for b, m in enumerate(rows):
            w = weight(taps - 1 - back, b, m)
            if back == 0:
                ins = e.tensor_scalar(out[0:m, b, :], acc[0:m, b, :], w, None, ALU.mult)
            else:
                ins = e.scalar_tensor_tensor(out[0:m, b, back:S], acc[0:m, b, 0:S - back], w,
                                             out[0:m, b, back:S], ALU.mult, ALU.add)
        if back < taps - 1:
            e.drain()
    return ins


def param(st, name, c, m=P):
    return st.params[0:m, ds(c + st.col0[name], 1)]


def conv_tiles(st, w, rhs, n, col0, dst, name, bias, taps):
    def dve(e, acc, i, p):
        return short_conv(st, e, st.A[:, ds(i * 4 + (dst + 2 * p), 2), :], acc, taps,
                          lambda k, b, m: param(st, f"{name}{k}", i * 4 + (2 * p + b)), (P, P))

    def act(e, acc, i, p):
        for b in range(2):
            x = st.A[:, ds(i * 4 + (dst + 2 * p + b), 1), :]
            ins = e.activation(x, x, ACT.Silu, bias=param(st, bias, i * 4 + (2 * p + b)))
        return ins
    return tiles(w, rhs, n, col0, act=act, dve=dve, order="dve+act")


def conv_module_steps(nc, st, w, rhs):
    ctx = ExitStack()
    products, gate_free, pool_done, going = sems(nc, ctx, "dw", "products gate_free pool_done going")
    pad = CONV_K - 1
    U = st.spare[:, 0:3, :].rearrange("p c n -> p (c n)")[:, 0:2 * (S + 32)].rearrange("p (b n) -> p b n", b=2)
    gate = st.spare[:, 3:5, :]
    sums = st.spare[:, 5:9, :]
    wts = st.spare[:, 9, 0:2 * CONV_K].rearrange("p (k b) -> p k b", b=2)
    pool_sum = st.spare[:, 10:12, :]
    PROD = (pool_sum, gate, st.spare[:, 12:14, :], st.spare[:, 14:16, :], st.A[:, 14:16, :])
    BESIDE = len(PROD)
    dw0 = st.col0["dw0"]
    weights = st.params[:, dw0:dw0 + 16 * CONV_K].rearrange("p (k c) -> p k c", c=16)

    def clear(e):
        for b in range(2):
            e.memset(U[:, b, 0:pad], 0.0)

    def sigmoid(e, acc, i, p):
        e.wait_ge(gate_free, i * 2 + (p // 3 + 1))
        e.sem_inc(going, 1)
        return e.activation(gate, acc, ACT.Sigmoid)

    def silu(e, acc, i, p):
        return e.activation(st.A[:, ds(i * 4 + (16 + 2 * (p // 3)), 2), :], acc, ACT.Silu)

    def act_products(e, i, p):
        e.wait_ge(seg.posted, seg.posted_at(i, p))
        e.sem_inc(going, 1)
        for k in range(BESIDE):
            for b in range(2):
                ins = e.activation(PROD[k][:, b, :], U[:, b, k:k + S], ACT.Copy, scale=wts[:, k, b:b + 1])
        ins.then_inc(products, 1)

    def glu(e, acc, i, p):
        e.tensor_copy(wts, weights[:, :, ds(i * 4 + 2 * (p // 3), 2)])
        e.tensor_tensor(U[:, :, pad:pad + S], acc, gate, ALU.mult)
        return e.drain()

    def add_products(e, i, p):
        first = isinstance(i, int) and i == 0 and p < 3
        if first or p % 3 == 2:
            return
        pair = i * 2 + (p // 3 - 1)
        for half in (p % 3,) if not isinstance(i, int) or i < 4 else (0, 1):
            if half == 0:
                e.wait_ge(products, pair + 1)
                e.sem_inc(going, 1)
            for k in (1, 2) if half == 0 else range(3, BESIDE):
                ins = e.tensor_tensor(pool_sum, pool_sum, PROD[k], ALU.add)
                if k == 1:
                    ins.then_inc(gate_free, 1)
                e.drain()
        if half == 1:
            e.drain().then_inc(pool_done, 1)

    def conv(e, i, p):
        h = p // 3
        for k in range(BESIDE, CONV_K):
            for b in range(2):
                s = sums[:, 2 * (k % 2) + b, :]
                if k < BESIDE + 2:
                    e.tensor_scalar(s, U[:, b, k:k + S], wts[:, k, b:b + 1], None, ALU.mult)
                else:
                    e.scalar_tensor_tensor(s, U[:, b, k:k + S], wts[:, k, b:b + 1], s, ALU.mult, ALU.add)
            if k % 2:
                e.drain()
        e.drain()
        e.wait_ge(pool_done, i * 2 + (h + 1))
        e.tensor_tensor(sums[:, 0:2, :], sums[:, 0:2, :], pool_sum, ALU.add)
        e.drain()
        for b in range(2):
            e.scalar_tensor_tensor(st.A[:, ds(i * 4 + (2 * h + b), 1), :], sums[:, b:b + 1, :],
                                   param(st, "conv_dw_b_2", i * 4 + (2 * h + b)), sums[:, 2 + b:3 + b, :],
                                   ALU.add, ALU.add)

    phases = []
    for h in range(2):
        phases += [Phase(D_INNER + h * TW, act=sigmoid, order="gate"),
                   Phase(h * TW, dve=glu, takes=3 * h, more=conv, act_more=act_products),
                   Phase(2 * D_INNER + h * TW, act=silu)]
    seg = Seg(w, rhs, 4, phases, stride=2 * TW)
    seg.beside = add_products
    clearing = Part(ctx)
    clearing.vector(clear)
    clearing.gpsimd(lambda e: e.nop().then_inc(gate_free, 1))
    return clearing, seg


def gated_ffn_steps(nc, st, t, H, B, first_ready):
    wu, wd = t["w_up_3"][0], t["w_down_3"][0]
    gate, val = st.A[:, 0:8, :], st.A[:, 8:16, :]
    steps = []

    def pair(g, j0, rounds, width, ready):
        rows = [min(P, width - b * P) for b in range(2)]
        chunk = lambda i, b: i * 2 + (8 * g + j0 + b)

        def out(a, i):
            return a[:, ds(i * 2 + j0, 2), :]

        def gate_conv(e, acc, i, p):
            return short_conv(st, e, out(gate, i), acc, FFN3_K,
                              lambda k, b, m: param(st, f"fg{k}", chunk(i, b), m), rows)

        def gate_silu(e, acc, i, p):
            for b, m in enumerate(rows):
                x = gate[0:m, ds(i * 2 + (j0 + b), 1), :]
                ins = e.activation(x, x, ACT.Silu, bias=param(st, "fgb", chunk(i, b), m))
            return ins

        def product(e, acc, i, p):
            short_conv(st, e, out(val, i), acc, FFN3_K,
                       lambda k, b, m: param(st, f"fv{k}", chunk(i, b), m), rows)
            e.drain()
            at = lambda a, b, m: a[0:m, ds(i * 2 + (j0 + b), 1), :]
            for b, m in enumerate(rows):
                e.scalar_tensor_tensor(at(val, b, m), at(val, b, m), param(st, "fvb", chunk(i, b), m),
                                       at(gate, b, m), ALU.add, ALU.mult)
            e.drain()
            for b, m in enumerate(rows):
                e.tensor_copy(at(B[0], b, m), at(val, b, m))
            e.drain()
            for b, m in enumerate(rows):
                ins = e.tensor_tensor(at(B[1], b, m), at(val, b, m), at(B[0], b, m).bitcast(F32), ALU.subtract)
            return ins

        c0 = g * D + j0 * P
        seg = Seg(wu, H, rounds, [Phase(c0, act=gate_silu, dve=gate_conv, order="dve+act"),
                                  Phase(FFN3 + c0, dve=product, takes=0)], stride=TW, width=width, ready=ready)
        seg.made_by = 1
        return seg

    for g in range(-(-FFN3 // D)):
        rows = min(D, FFN3 - g * D)
        full, rem = divmod(rows, TW)
        ready = first_ready if g == 0 else None
        segs = [pair(g, 0, full, TW, ready)]
        if rem:
            segs.append(pair(g, 2 * full, 1, rem, None))

        def made(k, segs=segs, full=full):
            return segs[0].result_ready(k) if k < 2 * full else segs[1].result_ready(k - 2 * full)
        steps += segs
        steps.append(tiles(wd, B, 4, 0, row0=g * D, rows=rows, ready=made,
                           dve=add_to_x(st, x_scale=ALPHA if g == 0 else 1.0)))
    return steps


def program(nc, t, out, stop=None):
    ctx = ExitStack()
    st = Store()
    FINISHED.clear()
    CURRENT.clear()

    def sb(name, shape, dt=F32):
        return ctx.enter_context(nc.sbuf_tensor(name, shape, dt))

    with ctx:
        base = -(-nc.sbuf_base // 32) * 32
        st.Bh, st.Bl = sb("Bh", [P, KC, S], F32R), sb("Bl", [P, KC, S], F32R)
        st.spare = nc.alloc_sbuf_tensor_at("spare", [P, 2 * KC, S], F32, offset=base)
        assert nc.sbuf_base >= base + 2 * KC * S * 4
        st.X = sb("X", [P, KC, S])
        st.A = sb("A", [P, 32, S])
        st.raw = sb("raw", [P, 8, S])
        st.Wh, st.Wl = sb("Wh", [P, SLOTS, KC, TW], F32R), sb("Wl", [P, SLOTS, KC, TW], F32R)
        st.Hh, st.Hl = sb("Hh", [P, KC, S], F32R), sb("Hl", [P, KC, S], F32R)
        st.params = sb("params", [P, 8 * P])
        st.squares = sb("squares", [P, len(CONST_SQ), P])
        st.small = sb("small", [P, 16])
        st.cols = sb("cols", [P, 128])
        mod = sb("mod", [P, 64])
        st.heads = sb("heads", [16, 8])
        st.skip = sb("skip", [P, 8])
        st.inv_freq = sb("inv_freq", [P, 1])
        misc = sb("misc", [P, 8])
        st.PS = ctx.enter_context(nc.psum_tensor("PS", [P, 8, S], F32))
        st.mod, st.gain = mod[:, 0:48], mod[:, 48:64]
        st.neg_lam, st.subln = misc[:, 0:1], misc[:, 1:2]
        st.eps = {1e-6: misc[:, 2:3], 1e-5: misc[:, 3:4]}
        st.eps_col = lambda e: st.eps[e]
        st.sq = {n: st.squares[:, k, :] for k, n in enumerate(CONST_SQ)}
        st.ident, st.ones = st.sq["ident"], st.sq["ones"]
        st.raw_slot = lambda s: st.raw[:, 4 * s:4 * s + 4, :].rearrange("p c (h n) -> p (c h) n", h=2)
        st.stage = st.A[:, 28:32, :].rearrange("p (s b) n -> p s b n", s=2)

        A = lambda a, n: chunks(st.A, a, n)
        X = chunks(st.X, 0, KC)
        H, B = (st.Hh, st.Hl), (st.Bh, st.Bl)
        halves = lambda pair: (chunks(pair[0], 0, KC), chunks(pair[1], 0, KC))
        both = (chunks(st.Hh, 0, 8) + chunks(st.Bh, 0, 8), chunks(st.Hl, 0, 8) + chunks(st.Bl, 0, 8))
        pcols = lambda name, n, first=0: [col(st, name, first + c) for c in range(n)]
        mcols = lambda k: [st.mod[:, 8 * k + c:8 * k + c + 1] for c in range(KC)]
        gcols = lambda k: [st.gain[:, 8 * k + c:8 * k + c + 1] for c in range(KC)]
        tokens = lambda a, n: st.A[:, a:a + n, :].rearrange("p (b c) n -> p b (c n)", b=NB)

        def front():
            load, columns = load_parts(nc, st, t)
            mod_products, mod_rest = modulation_parts(nc, st, t, load.c_act)
            norm1 = norm_part(nc, st, "n1", X, D, 1e-6, gcols(0), mcols(0), split=halves(H), tmp=A(0, 8),
                              scratch=st.A[:, 16:22, :])
            w_in = t["w_in"][0]
            stage(nc, load, mod_products, columns, mod_rest, weights_part(nc, st, "wi", [
                norm1,
                tiles(w_in, H, 4, 0, act=to_chunks(st, 0), ready=norm1.ready),
                tiles(w_in, H, 2, 1024, mode="tokens", act=to_tokens(tokens(8, 4))),
                tiles(w_in, H, 2, 1536, act=to_chunks(st, 12, scale=0.125)),
                tiles(w_in, H, 2, 2048, act=to_chunks(st, 16)),
                tiles(w_in, H, 2, 2560, mode="tokens", act=to_tokens(tokens(20, 4)))]))

        def squared_relu(e, s, acc, i, p):
            return e.scalar_tensor_tensor(s, acc, 0.0, s, ALU.max, ALU.mult)

        def middle():
            mixed = split_part(nc, st, "mx1", A(0, 4) + A(12, 4), *halves(H))
            w_out = tiles(t["w_out"][0], H, 4, 0, dve=add_to_x(st, st.mod[:, 16:24]), ready=mixed.ready)
            norm2 = norm_part(nc, st, "n2", X, D, 1e-6, gcols(1), mcols(3), split=halves(H), tmp=A(0, 8),
                              src_ready=w_out.result_ready)
            ffn = []
            for q in range(FF1 // D):
                up = tiles(t["w_ff1"][0], H, 4, q * D, act=staged_copy(st, ACT.Relu),
                           dve=split_chunks(st, B, squared_relu), ready=None if q else norm2.ready)
                ffn += [up, tiles(t["w_ff2"][0], B, 4, 0, row0=q * D, dve=add_to_x(st, st.mod[:, 40:48]),
                                  ready=up.result_ready)]
            norm3 = norm_part(nc, st, "n3", X, D, 1e-6, pcols("final_norm_g", 8), out=X,
                              src_ready=ffn[-1].all_ready)
            norm4 = norm_part(nc, st, "n4", X, D, 1e-6, pcols("conv_norm_2", 8), split=halves(H), tmp=A(0, 8),
                              src_ready=norm3.out_ready)
            clearing, conv_in = conv_module_steps(nc, st, t["conv_w_in_2"][0], H)
            conv_in.ready = norm4.ready
            norm5 = norm_part(nc, st, "n5", A(0, 16), D_INNER, 1e-6, pcols("conv_ln_g_2", 16),
                              pcols("conv_ln_b_2", 16), centre=True, silu=True, times=A(16, 16),
                              split=both, scratch=st.spare[:, 10:16, :])
            conv_out = [tiles(t["conv_w_out_2"][0], rhs, 4, 0, row0=n * D, dve=add_to_x(st),
                              ready=lambda k, n=n: norm5.ready(8 * n + k)) for n, rhs in enumerate((H, B))]
            norm6 = norm_part(nc, st, "n6", X, D, 1e-6, pcols("ret_norm_2", 8), split=halves(H), tmp=A(0, 8),
                              src_ready=conv_out[-1].all_ready)
            rw = t["ret_w_in_2"][0]
            queries = tiles(rw, H, 4, 0, act=to_chunks(st, 0), order="gate", ready=norm6.ready)
            keys = tiles(rw, H, 4, 1024, act=to_chunks(st, 8, scale=256 ** -0.5), order="gate")
            tables, sines, turn = rotary_parts(
                nc, st, t, norm5.ready(15), lambda c: queries.act_ready(c) if c < 8 else keys.act_ready(c - 8))
            stage(nc, weights_part(nc, st, "mid", [
                mixed, w_out, norm2, *ffn, norm3, norm4, clearing, conv_in, norm5,
                conv_out[0], tables, conv_out[1], norm6, sines, queries, keys, turn,
                tiles(rw, H, 8, 2048, mode="tokens", act=to_tokens(tokens(16, 16)))]))

        w3 = t["w_in_3"][0]
        M_QK, M_V = 512, 1024
        at_v, at_o, at_i = 2 * M_QK, 2 * M_QK + M_V, 2 * M_QK + 2 * M_V
        at_z = at_i + 2 * M_HEADS
        at_xbc = at_z + D
        at_dt = at_xbc + 2 * D
        at_ga = at_dt + S_HEADS
        at_gb = at_ga + D

        def rows_to(c, n):
            def act(e, acc, i, p):
                return e.activation(st.A[0:n, c, :], acc[0:n, 0, :], ACT.Copy)
            return act

        def after_retention():
            o = st.A[:, 16:32, :].rearrange("p (b i) n -> p b i n", i=4)

            def gate(e, acc, i, p):
                return e.activation(st.A[:, 2 * p:2 * p + 2, :], acc, ACT.Silu)

            def gated_o(first):
                return lambda i, p: o[:, 2 * p:2 * p + 2, ds(i + first, 1), :].rearrange("p b i n -> p (b i) n")

            def to_parts(e, acc, i, p):
                g = st.A[:, 2 * p:2 * p + 2, :]
                e.tensor_tensor(g, g, gated_o(0)(i, p), ALU.mult)
                e.drain()
                hi = st.Bh[:, ds(i * 4 + 2 * p, 2), :]
                e.tensor_copy(hi, g)
                e.drain()
                return e.tensor_tensor(st.Bl[:, ds(i * 4 + 2 * p, 2), :], g, hi.bitcast(F32), ALU.subtract)

            def to_a(e, acc, i, p):
                return e.tensor_tensor(st.A[:, ds(i * 4 + (8 + 2 * p), 2), :], st.A[:, 2 * p:2 * p + 2, :],
                                       gated_o(2)(i, p), ALU.mult)
            rw, ro = t["ret_w_in_2"][0], t["ret_w_out_2"][0]
            gate0 = tiles(rw, H, 4, 4096, act=gate, dve=to_parts)
            gate1 = tiles(rw, H, 4, 4096 + D, act=gate, dve=to_a)
            second = split_part(nc, st, "rs", A(8, 8), *halves(H))
            out0 = tiles(ro, B, 4, 0, dve=add_to_x(st), ready=gate0.result_ready)
            out1 = tiles(ro, H, 4, 0, row0=D, dve=add_to_x(st), ready=second.ready)
            norm7 = norm_part(nc, st, "n7", X, D, 1e-6, pcols("final_norm_2", 8), out=X, src_ready=out1.all_ready)
            norm8 = norm_part(nc, st, "n8", X, D, 1e-5, pcols("in_ln_g_3", 8), pcols("in_ln_b_3", 8),
                              out=X, split=halves(H), centre=True)
            stage(nc, weights_part(nc, st, "ret_out", [
                gate0, gate1, second, out0, out1, norm7, norm8,
                tiles(w3, H, 1, at_i, width=M_HEADS, act=rows_to(24, M_HEADS), ready=norm8.ready),
                tiles(w3, H, 1, at_i + M_HEADS, width=M_HEADS, act=rows_to(25, M_HEADS)),
                conv_tiles(st, w3, H, 4, 0, 0, "mc", "m_conv_b_3", M_CONV),
                tiles(w3, H, 4, at_v, mode="tokens", act=to_tokens(tokens(8, 8)))]))

        def after_mlstm():
            def times_h(e, s, acc, i, p):
                return e.tensor_tensor(s, s, st.A[:, ds(i * 4 + (16 + 2 * p), 2), :], ALU.mult)

            def gated(e, acc, i, p):
                return e.tensor_tensor(st.A[:, ds(i * 4 + (8 + 2 * p), 2), :], acc,
                                       st.A[:, ds(i * 4 + 2 * p, 2), :], ALU.mult)
            o = tiles(w3, H, 4, at_o, act=staged_copy(st, ACT.Sigmoid), dve=split_chunks(st, B, times_h))
            stage(nc, weights_part(nc, st, "m_out", [
                o,
                tiles(w3, H, 4, at_ga, act=to_chunks(st, 0, ACT.Sigmoid)),
                tiles(t["p_a_3"][0], B, 4, 0, dve=gated, ready=o.result_ready),
                conv_tiles(st, w3, H, 8, at_xbc, 16, "sc", "s_conv_b_3", S_CONV),
                tiles(w3, H, 1, at_dt, width=S_HEADS, act=rows_to(0, S_HEADS))]))

        def after_mamba():
            def times_y(e, acc, i, p):
                y = st.A[:, ds(i * 4 + (16 + 2 * p), 2), :]
                return e.tensor_tensor(y, y, st.stage[:, p, :, :], ALU.mult)

            def merge(e, s, acc, i, p):
                e.tensor_tensor(s, acc, st.A[:, ds(i * 4 + 2 * p, 2), :], ALU.mult)
                e.drain()
                return e.tensor_tensor(s, s, st.A[:, ds(i * 4 + (8 + 2 * p), 2), :], ALU.add)
            z = tiles(w3, H, 4, at_z, act=staged_copy(st, ACT.Silu), dve=times_y)
            y_norm = group_norm_part(nc, st, A(16, 8), pcols("s_norm_g_3", 8), *halves(B), src_ready=z.result_ready)
            p_b = tiles(t["p_b_3"][0], B, 4, 0, dve=split_chunks(st, H, merge), ready=y_norm.ready)
            w_out = tiles(t["w_out_3"][0], H, 4, 0, dve=add_to_x(st, x_scale=ALPHA), ready=p_b.result_ready)
            ln1 = norm_part(nc, st, "l1", X, D, 1e-5, pcols("ln1_g_3", 8), pcols("ln1_b_3", 8),
                            out=X, split=halves(H), centre=True)
            ln2 = norm_part(nc, st, "l2", X, D, 1e-5, pcols("ln2_g_3", 8), pcols("ln2_b_3", 8),
                            out=X, centre=True)
            stage(nc, weights_part(nc, st, "end", [
                z, tiles(w3, H, 4, at_gb, act=to_chunks(st, 0, ACT.Sigmoid)), y_norm,
                p_b, w_out, ln1, *gated_ffn_steps(nc, st, t, H, B, ln1.ready), ln2]))

        for name, build in (
                ("front", front),
                ("rope", lambda: stage(nc, rope_part(nc, st, t))),
                ("attention", lambda: stage(nc, attention_part(nc, st))),
                ("middle", middle),
                ("retention", lambda: stage(nc, retention_part(nc, st, t))),
                ("after_retention", after_retention),
                ("gates", lambda: stage(nc, gates_part(nc, st))),
                ("mlstm", lambda: stage(nc, mlstm_part(nc, st))),
                ("after_mlstm", after_mlstm),
                ("steps", lambda: stage(nc, steps_part(nc, st))),
                ("mamba_x", lambda: stage(nc, mamba_inputs_part(nc, st))),
                ("mamba", lambda: stage(nc, mamba_part(nc, st))),
                ("after_mamba", after_mamba),
                ("store", lambda: stage(nc, store_part(nc, st, out)))):
            build()
            if name == stop:
                break


def kernel(**inputs):
    import concourse.bacc as bacc
    from concourse.bass_utils import run_bass_kernel_spmd

    nc = bacc.Bacc("TRN2", target_bir_lowering=False, num_devices=1)
    arrays, t = {}, {}
    for name, a in {**inputs, **constants()}.items():
        a = np.ascontiguousarray(a)
        arrays[f"in_{name}"] = a
        t[name] = nc.dram_tensor(f"in_{name}", a.shape, mybir.dt.from_np(a.dtype), kind="ExternalInput").ap()
    out = nc.dram_tensor("out", (1, S, D), F32, kind="ExternalOutput").ap()
    program(nc, t, out)
    r = run_bass_kernel_spmd(nc, [arrays], core_ids=[0])
    return r.results[0]["out"]
```
